# Optimizing a Trainium2 kernel written in Bass

```python
import math
import numpy as np
import jax
import jax.numpy as jnp
from jax import lax

D_MODEL = 1024
BATCH = 1
SEQ = 512
DEPTH = 2
DEC_BATCH = 8
DEC_SEQ = 8
PAST_LEN = 4096
PAGE_SIZE = 128

D_MIX = D_MODEL
D_CONV = D_MIX // 4
CONV_WIDTH = 31
N_GDN_HEADS = 4
GDN_HEAD_DIM = D_MIX // (2 * N_GDN_HEADS)
D_GDN = N_GDN_HEADS * GDN_HEAD_DIM
GDN_CONV = 4
GDN_CHUNK = 64
D_LRU = D_MIX - D_CONV - D_GDN
N_LRU_BLOCKS = 4
LRU_BLOCK = D_LRU // N_LRU_BLOCKS
LRU_CONV = 4
LRU_C = 8.0
D_FF = 2816
N_EXPERTS = 8
TOP_K = 2
D_FF_EXPERT = 1408
MOE_BLOCK = 128
N_DENSE_LAYERS = (DEPTH + 1) // 2
N_MOE_LAYERS = DEPTH // 2
EPS = 1e-6
IN_SIZES = (D_CONV, D_CONV, 3 * D_GDN, D_GDN, N_GDN_HEADS, N_GDN_HEADS, D_LRU, D_LRU)
D_IN = sum(IN_SIZES)

kernel_name = 'hybrid_conv_gdn_rglru_adaln_step'

def rmsnorm(x, g):
    xf = x.astype(jnp.float32)
    y = xf * lax.rsqrt(jnp.mean(xf * xf, axis=-1, keepdims=True) + EPS)
    return (y * g.astype(jnp.float32)).astype(x.dtype)

def layernorm(x, g, b):
    xf = x.astype(jnp.float32)
    mu = jnp.mean(xf, axis=-1, keepdims=True)
    var = jnp.mean(jnp.square(xf - mu), axis=-1, keepdims=True)
    y = (xf - mu) * lax.rsqrt(var + EPS) * g.astype(jnp.float32) + b.astype(jnp.float32)
    return y.astype(x.dtype)

def l2norm(x):
    xf = x.astype(jnp.float32)
    return xf * lax.rsqrt(jnp.sum(xf * xf, axis=-1, keepdims=True) + EPS)

def causal_dwconv(x, buf, w):
    width, ch = w.shape
    xp = jnp.concatenate([buf.astype(x.dtype), x], axis=1)
    y = lax.conv_general_dilated(xp, w[:, None, :].astype(x.dtype), window_strides=(1,), padding='VALID',
                                 dimension_numbers=('NWC', 'WIO', 'NWC'), feature_group_count=ch)
    return y, xp[:, xp.shape[1] - (width - 1):]

def swiglu(x, wg, wu, wd):
    return (jax.nn.silu(x @ wg) * (x @ wu)) @ wd

def gated_delta_chunked(q, k, v, g, beta, s0):
    bsz, t, nh, dk = q.shape
    cs = min(GDN_CHUNK, t)
    nc = -(-t // cs)
    pad = nc * cs - t

    def blocks(a):
        a = a.astype(jnp.float32)
        a = jnp.pad(a, [(0, 0), (0, pad)] + [(0, 0)] * (a.ndim - 2))
        a = jnp.moveaxis(a, 2, 1)
        return a.reshape((bsz, nh, nc, cs) + a.shape[3:])

    q, k, v, g, beta = (blocks(a) for a in (q, k, v, g, beta))
    g = jnp.cumsum(g, axis=-1)
    pos = jnp.arange(cs)
    incl = pos[:, None] >= pos[None, :]
    strict = pos[:, None] > pos[None, :]
    decay = jnp.exp(jnp.where(incl, g[..., :, None] - g[..., None, :], -jnp.inf))
    kb = k * beta[..., None]
    lower = jnp.where(strict, jnp.einsum('bhncd,bhnsd->bhncs', kb, k) * decay, 0.0)
    eye = jnp.eye(cs, dtype=jnp.float32)
    tinv = lax.linalg.triangular_solve(lower + eye, jnp.broadcast_to(eye, lower.shape),
                                       left_side=True, lower=True, unit_diagonal=True)
    u = jnp.einsum('bhncs,bhnse->bhnce', tinv, v * beta[..., None])
    w = jnp.einsum('bhncs,bhnsd->bhncd', tinv, kb * jnp.exp(g)[..., None])
    qk = jnp.einsum('bhncd,bhnsd->bhncs', q, k) * decay
    g_last = g[..., -1]

    def chunk_step(s, xs):
        q_c, k_c, u_c, w_c, g_c, gl_c, qk_c = xs
        v_new = u_c - jnp.einsum('bhcd,bhde->bhce', w_c, s)
        o_c = (jnp.einsum('bhcd,bhde->bhce', q_c * jnp.exp(g_c)[..., None], s)
               + jnp.einsum('bhcs,bhse->bhce', qk_c, v_new))
        k_dec = k_c * jnp.exp(gl_c[..., None] - g_c)[..., None]
        s = s * jnp.exp(gl_c)[..., None, None] + jnp.einsum('bhcd,bhce->bhde', k_dec, v_new)
        return s, o_c

    xs = tuple(jnp.moveaxis(a, 2, 0) for a in (q, k, u, w, g, g_last, qk))
    s_fin, o = lax.scan(chunk_step, s0.astype(jnp.float32), xs)
    o = jnp.moveaxis(o, 0, 2).reshape(bsz, nh, nc * cs, -1)[:, :, :t]
    return jnp.moveaxis(o, 1, 2), s_fin

def rg_lru(x, h0, w_a, b_a, w_i, b_i, lam):
    bsz, t, _ = x.shape
    xb = x.reshape(bsz, t, N_LRU_BLOCKS, LRU_BLOCK)
    r = jax.nn.sigmoid((jnp.einsum('btni,nij->btnj', xb, w_a).reshape(bsz, t, D_LRU) + b_a).astype(jnp.float32))
    i = jax.nn.sigmoid((jnp.einsum('btni,nij->btnj', xb, w_i).reshape(bsz, t, D_LRU) + b_i).astype(jnp.float32))
    log_a = -LRU_C * r * jax.nn.softplus(-lam.astype(jnp.float32))
    a = jnp.exp(log_a)
    b = jnp.sqrt(-jnp.expm1(2.0 * log_a)) * (i * x.astype(jnp.float32))
    b = b.at[:, 0].add(a[:, 0] * h0.astype(jnp.float32))

    def combine(lhs, rhs):
        return lhs[0] * rhs[0], rhs[0] * lhs[1] + rhs[1]

    _, h = lax.associative_scan(combine, (a, b), axis=1)
    return h.astype(x.dtype), h[:, -1]

def moe_ffn(h, w_router, b_router, wg, wu, wd):
    bsz, t, d = h.shape
    x = h.reshape(-1, d)
    n_tok = x.shape[0]
    logits = (x @ w_router).astype(jnp.float32) + b_router.astype(jnp.float32)
    top_val, top_idx = lax.top_k(logits, TOP_K)
    gates = jax.nn.softmax(top_val, axis=-1)
    n_asg = n_tok * TOP_K
    e_flat = top_idx.reshape(-1)
    tok = jnp.arange(n_asg) // TOP_K
    order = jnp.argsort(e_flat)
    e_sorted = e_flat[order]
    counts = jnp.bincount(e_flat, length=N_EXPERTS)
    padded = (counts + MOE_BLOCK - 1) // MOE_BLOCK * MOE_BLOCK
    start = jnp.cumsum(counts) - counts
    pends = jnp.cumsum(padded)
    pstart = pends - padded
    dest = pstart[e_sorted] + jnp.arange(n_asg) - start[e_sorted]
    n_blocks = -(-n_asg // MOE_BLOCK) + N_EXPERTS
    rows = n_blocks * MOE_BLOCK
    xs = jnp.zeros((rows, d), x.dtype).at[dest].set(x[tok[order]])
    block_e = jnp.minimum(jnp.searchsorted(pends, jnp.arange(n_blocks) * MOE_BLOCK, side='right'), N_EXPERTS - 1)

    def expert_block(args):
        xblk, e = args
        return swiglu(xblk, wg[e], wu[e], wd[e])

    ys = lax.map(expert_block, (xs.reshape(n_blocks, MOE_BLOCK, d), block_e)).reshape(rows, d)
    y_asg = jnp.zeros((n_asg, d), ys.dtype).at[order].set(ys[dest])
    y = jnp.einsum('nk,nkd->nd', gates.astype(y_asg.dtype), y_asg.reshape(n_tok, TOP_K, d))
    return y.reshape(bsz, t, d)

def hybrid_layer(l, x, c_act, s_conv_a, s_qkv, s_delta, s_conv_lru, s_lru, p):
    bsz, t, _ = x.shape
    f32 = jnp.float32
    mod = (c_act @ p['w_ada'][l] + p['b_ada'][l])[:, None, :]
    sh1, sc1, g1, sh2, sc2, g2 = jnp.split(mod, 6, axis=-1)
    h = rmsnorm(x, p['norm1'][l]) * (1 + sc1) + sh1
    proj = h @ p['w_in'][l]
    a_val, a_gate, qkv, z, b_raw, a_raw, lru_x, lru_g = jnp.split(proj, np.cumsum(IN_SIZES)[:-1].tolist(), axis=-1)

    u = a_val * jax.nn.sigmoid(a_gate)
    u, new_conv_a = causal_dwconv(u, s_conv_a, p['conv_a_w'][l])
    y_a = jax.nn.silu(layernorm(u + p['conv_a_b'][l], p['ln_a_g'][l], p['ln_a_b'][l]))

    qkv_c, new_qkv = causal_dwconv(qkv, s_qkv, p['conv_qkv_w'][l])
    q, k, v = jnp.split(jax.nn.silu(qkv_c).reshape(bsz, t, 3 * N_GDN_HEADS, GDN_HEAD_DIM), 3, axis=2)
    q = l2norm(q) * GDN_HEAD_DIM ** -0.5
    k = l2norm(k)
    beta = jax.nn.sigmoid(b_raw.astype(f32))
    g = -jnp.exp(p['gdn_a_log'][l].astype(f32)) * jax.nn.softplus(a_raw.astype(f32) + p['gdn_dt_bias'][l].astype(f32))
    o, new_delta = gated_delta_chunked(q, k, v, g, beta, s_delta)
    o = rmsnorm(o, p['gdn_norm'][l]) * jax.nn.silu(z.reshape(bsz, t, N_GDN_HEADS, GDN_HEAD_DIM).astype(f32))
    y_b = o.reshape(bsz, t, D_GDN).astype(x.dtype)

    xc, new_conv_lru = causal_dwconv(lru_x, s_conv_lru, p['conv_lru_w'][l])
    hs, new_lru = rg_lru(xc + p['conv_lru_b'][l], s_lru, p['lru_w_a'][l], p['lru_b_a'][l],
                         p['lru_w_i'][l], p['lru_b_i'][l], p['lru_lambda'][l])
    y_c = rmsnorm(hs * jax.nn.gelu(lru_g), p['lru_norm'][l])

    mix = jnp.concatenate([y_a, y_b, y_c], axis=-1) @ p['w_out'][l]
    x = x + g1 * mix

    h = rmsnorm(x, p['norm2'][l]) * (1 + sc2) + sh2
    if l % 2 == 0:
        j = l // 2
        f = swiglu(h, p['ffn_wg'][j], p['ffn_wu'][j], p['ffn_wd'][j])
    else:
        j = l // 2
        f = moe_ffn(h, p['router_w'][j], p['router_b'][j], p['moe_wg'][j], p['moe_wu'][j], p['moe_wd'][j])
    x = x + g2 * f
    return x, (new_conv_a, new_qkv, new_delta.astype(s_delta.dtype), new_conv_lru, new_lru.astype(s_lru.dtype))

def run_trunk(x, c, s_conv_a, s_qkv, s_delta, s_conv_lru, s_lru, p):
    c_act = jax.nn.silu(c)
    new = []
    for l in range(DEPTH):
        x, st = hybrid_layer(l, x, c_act, s_conv_a[l], s_qkv[l], s_delta[l], s_conv_lru[l], s_lru[l], p)
        new.append(st)
    y = rmsnorm(x, p['final_norm'])
    stacked = [jnp.stack(parts, axis=0) for parts in zip(*new)]
    return y, stacked

def setup_inputs(seed: int = 0) -> dict:
    key = jax.random.key(seed)
    keys = iter(jax.random.split(key, 64))

    def nrm(shape, scale):
        return jax.random.normal(next(keys), shape, jnp.float32) * scale

    def gain(shape):
        return 1.0 + nrm(shape, 0.02)

    dsc = D_MODEL ** -0.5
    lru_a0 = jax.random.uniform(next(keys), (DEPTH, D_LRU), jnp.float32, 0.9, 0.999)
    lru_p = lru_a0 ** (1.0 / LRU_C)
    dt = jnp.exp(jax.random.uniform(next(keys), (DEPTH, N_GDN_HEADS), jnp.float32, math.log(1e-3), math.log(0.1)))
    a_init = jax.random.uniform(next(keys), (DEPTH, N_GDN_HEADS), jnp.float32, 1.0, 16.0)
    inp = {}
    inp['x_prompt'] = nrm((BATCH, SEQ, D_MODEL), 1.0)
    inp['x_sample'] = nrm((DEC_BATCH, DEC_SEQ, D_MODEL), 1.0)
    inp['c_prompt'] = nrm((BATCH, D_MODEL), 1.0)
    inp['c_sample'] = nrm((DEC_BATCH, D_MODEL), 1.0)
    inp['state_conv_a'] = nrm((DEPTH, DEC_BATCH, CONV_WIDTH - 1, D_CONV), 0.5)
    inp['state_conv_qkv'] = nrm((DEPTH, DEC_BATCH, GDN_CONV - 1, 3 * D_GDN), 1.0)
    inp['state_delta'] = nrm((DEPTH, DEC_BATCH, N_GDN_HEADS, GDN_HEAD_DIM, GDN_HEAD_DIM), 0.1)
    inp['state_conv_lru'] = nrm((DEPTH, DEC_BATCH, LRU_CONV - 1, D_LRU), 1.0)
    inp['state_lru'] = nrm((DEPTH, DEC_BATCH, D_LRU), 0.5)
    inp['w_ada'] = nrm((DEPTH, D_MODEL, 6 * D_MODEL), dsc)
    inp['b_ada'] = nrm((DEPTH, 6 * D_MODEL), 0.02)
    inp['norm1'] = gain((DEPTH, D_MODEL))
    inp['norm2'] = gain((DEPTH, D_MODEL))
    inp['w_in'] = nrm((DEPTH, D_MODEL, D_IN), dsc)
    inp['w_out'] = nrm((DEPTH, D_MIX, D_MODEL), D_MIX ** -0.5)
    inp['conv_a_w'] = nrm((DEPTH, CONV_WIDTH, D_CONV), CONV_WIDTH ** -0.5)
    inp['conv_a_b'] = nrm((DEPTH, D_CONV), 0.02)
    inp['ln_a_g'] = gain((DEPTH, D_CONV))
    inp['ln_a_b'] = nrm((DEPTH, D_CONV), 0.02)
    inp['conv_qkv_w'] = nrm((DEPTH, GDN_CONV, 3 * D_GDN), GDN_CONV ** -0.5)
    inp['gdn_a_log'] = jnp.log(a_init)
    inp['gdn_dt_bias'] = dt + jnp.log(-jnp.expm1(-dt))
    inp['gdn_norm'] = gain((DEPTH, GDN_HEAD_DIM))
    inp['conv_lru_w'] = nrm((DEPTH, LRU_CONV, D_LRU), LRU_CONV ** -0.5)
    inp['conv_lru_b'] = nrm((DEPTH, D_LRU), 0.02)
    inp['lru_w_a'] = nrm((DEPTH, N_LRU_BLOCKS, LRU_BLOCK, LRU_BLOCK), LRU_BLOCK ** -0.5)
    inp['lru_b_a'] = nrm((DEPTH, D_LRU), 0.02)
    inp['lru_w_i'] = nrm((DEPTH, N_LRU_BLOCKS, LRU_BLOCK, LRU_BLOCK), LRU_BLOCK ** -0.5)
    inp['lru_b_i'] = nrm((DEPTH, D_LRU), 0.02)
    inp['lru_lambda'] = jnp.log(lru_p) - jnp.log1p(-lru_p)
    inp['lru_norm'] = gain((DEPTH, D_LRU))
    inp['ffn_wg'] = nrm((N_DENSE_LAYERS, D_MODEL, D_FF), dsc)
    inp['ffn_wu'] = nrm((N_DENSE_LAYERS, D_MODEL, D_FF), dsc)
    inp['ffn_wd'] = nrm((N_DENSE_LAYERS, D_FF, D_MODEL), D_FF ** -0.5)
    inp['router_w'] = nrm((N_MOE_LAYERS, D_MODEL, N_EXPERTS), dsc)
    inp['router_b'] = nrm((N_MOE_LAYERS, N_EXPERTS), 0.01)
    inp['moe_wg'] = nrm((N_MOE_LAYERS, N_EXPERTS, D_MODEL, D_FF_EXPERT), dsc)
    inp['moe_wu'] = nrm((N_MOE_LAYERS, N_EXPERTS, D_MODEL, D_FF_EXPERT), dsc)
    inp['moe_wd'] = nrm((N_MOE_LAYERS, N_EXPERTS, D_FF_EXPERT, D_MODEL), D_FF_EXPERT ** -0.5)
    inp['final_norm'] = gain((D_MODEL,))
    return inp

def reference(x_prompt, x_sample, c_prompt, c_sample, state_conv_a, state_conv_qkv, state_delta,
              state_conv_lru, state_lru, w_ada, b_ada, norm1, norm2, w_in, w_out, conv_a_w, conv_a_b,
              ln_a_g, ln_a_b, conv_qkv_w, gdn_a_log, gdn_dt_bias, gdn_norm, conv_lru_w, conv_lru_b,
              lru_w_a, lru_b_a, lru_w_i, lru_b_i, lru_lambda, lru_norm, ffn_wg, ffn_wu, ffn_wd,
              router_w, router_b, moe_wg, moe_wu, moe_wd, final_norm):
    p = dict(w_ada=w_ada, b_ada=b_ada, norm1=norm1, norm2=norm2, w_in=w_in, w_out=w_out,
             conv_a_w=conv_a_w, conv_a_b=conv_a_b, ln_a_g=ln_a_g, ln_a_b=ln_a_b, conv_qkv_w=conv_qkv_w,
             gdn_a_log=gdn_a_log, gdn_dt_bias=gdn_dt_bias, gdn_norm=gdn_norm, conv_lru_w=conv_lru_w,
             conv_lru_b=conv_lru_b, lru_w_a=lru_w_a, lru_b_a=lru_b_a, lru_w_i=lru_w_i, lru_b_i=lru_b_i,
             lru_lambda=lru_lambda, lru_norm=lru_norm, ffn_wg=ffn_wg, ffn_wu=ffn_wu, ffn_wd=ffn_wd,
             router_w=router_w, router_b=router_b, moe_wg=moe_wg, moe_wu=moe_wu, moe_wd=moe_wd,
             final_norm=final_norm)
    bp = x_prompt.shape[0]

    def zeros_like_state(s):
        return jnp.zeros((DEPTH, bp) + s.shape[2:], x_prompt.dtype)

    y_prompt, (conv_a_p, conv_qkv_p, delta_p, conv_lru_p, lru_p) = run_trunk(
        x_prompt, c_prompt, zeros_like_state(state_conv_a), zeros_like_state(state_conv_qkv),
        zeros_like_state(state_delta), zeros_like_state(state_conv_lru), zeros_like_state(state_lru), p)
    y_sample, (conv_a_s, conv_qkv_s, delta_s, conv_lru_s, lru_s) = run_trunk(
        x_sample, c_sample, state_conv_a, state_conv_qkv, state_delta, state_conv_lru, state_lru, p)
    return (y_prompt, y_sample, conv_a_p, conv_qkv_p, delta_p, conv_lru_p, lru_p,
            conv_a_s, conv_qkv_s, delta_s, conv_lru_s, lru_s)


_drawn_inputs = setup_inputs


def setup_inputs(seed=0):
    import zlib

    import numpy as np

    out = dict(_drawn_inputs(seed))
    spreads = {}
    factors = {'conv_a_b': 3.869,
     'ln_a_g': 15.755,
     'ln_a_b': 9.182,
     'gdn_norm': 11.387,
     'lru_b_a': 8.0,
     'lru_b_i': 7.974,
     'router_b': 11.697,
     'final_norm': 19.497,
     'lru_norm': 6.291,
     'norm2': 3.641}
    for name, (base, spread) in spreads.items():
        noise = np.random.default_rng([zlib.crc32(name.encode()), seed]).standard_normal(out[name].shape)
        drawn = base * np.exp(spread * noise) if base else spread * noise
        out[name] = jnp.asarray(drawn.astype(out[name].dtype))
    for name, factor in factors.items():
        out[name] = (out[name] * factor).astype(out[name].dtype)
    return out
```

```python
from contextlib import ExitStack

import concourse.bass as bass
from concourse import mybir

F32 = mybir.dt.float32
U32 = mybir.dt.uint32
ALU = mybir.AluOpType
ACT = mybir.ActivationFunctionType
AX_X = mybir.AxisListType.X

P = 128
L = 2
TP = 512
NB = 8
NS = 8
TS = NB * NS
T = TP + TS
G9 = NB + 1
D = 1024
KD = D // P
M_ADA = 6 * KD
M_IN = 24
FF = 22
NE = 8
FE = 11
H = 4
WA = 31
WQ = 4
EPS = 1e-6
RING = 4
SLOT = FE * P
CW = WQ - 1 + TP + NB * (WQ - 1 + NS)
SO = WQ - 1 + TP
CA = WA - 1 + TP + NB * (WA - 1 + NS)
AO = WA - 1 + TP
A_VAL, A_GATE, LRU_X, LRU_G, QKV, ZT = 0, 2, 4, 6, 8, 20
LEVELS = 7
SLEVELS = 3
NCH = 5
C_ID, C_TRI, C_BTRI, C_BONE, C_BM, C_IOTA, C_LVL = 0, 128, 256, 320, 384, 392, 400
C_END = C_LVL + LEVELS * P
PC = {}
_n = 0
for _name, _w in (("b_ada", M_ADA), ("norm1", KD), ("norm2", KD), ("conv_a_w", 2 * WA), ("conv_qkv_w", 12 * WQ),
                  ("conv_lru_w", 2 * WQ), ("conv_a_b", 2), ("ln_a_g", 2), ("ln_a_b", 2), ("conv_lru_b", 2),
                  ("lru_b_a", 2), ("lru_b_i", 2), ("lru_lambda", 2), ("lru_norm", 2), ("gdn_norm", 1),
                  ("a_log", H), ("dt_bias", H)):
    PC[_name] = (_n, _w)
    _n += _w
PCOLS = _n

F_ADA, F_IN, F_OUT, F_GU, F_DN = M_ADA, M_IN, KD, 2 * FF, 2 * KD
FILL, TILE = {}, {}
_f = _t = 0
for _l in range(L):
    _stages = [("ada", F_ADA, 0), ("in", F_IN, M_IN), ("out", F_OUT, KD)]
    _stages += [("gu", F_GU, 2 * FF), ("dn", F_DN, KD)] if _l % 2 == 0 else [("moe", NE * (2 * FE + KD), NE * (2 * FE + KD))]
    for _s, _nf, _nt in _stages:
        FILL[_s, _l], TILE[_s, _l] = _f, _t
        _f += _nf
        _t += _nt
LOG1P = [1.0 / (2 * i + 1) for i in range(9, 0, -1)]


def build(nc, io):
    ctx = ExitStack()
    with ctx:
        sb = lambda name, shape, dt=F32: ctx.enter_context(nc.sbuf_tensor(name, shape, dt))
        sem = lambda name: ctx.enter_context(nc.semaphore(name))

        xT = sb("xT", [P, KD, T])
        hT = sb("hT", [P, KD, T])
        PJ = sb("PJ", [P, M_IN * CW])
        UA = sb("UA", [P, 2, CA])
        QC = sb("QC", [P, 12, T])
        XA = sb("XA", [P, 2, T])
        XL = sb("XL", [P, 2, T])
        ring = sb("ring", [P, RING, SLOT])
        SP_ = sb("SP_", [P, H, P])
        SS = sb("SS", [P, NB, H, P])
        RS = sb("RS", [P, T])
        EPSC = sb("EPSC", [P, 2])
        SQ = sb("SQ", [P, 2, T])
        CO = sb("CO", [P, C_END])
        ONES = sb("ONES", [P, P])
        PA = sb("PA", [P, L, PCOLS])
        CT = sb("CT", [P, KD, G9])
        MOD = sb("MOD", [P, M_ADA, G9])
        AM = sb("AM", [P, 2, KD, G9])
        TMP = sb("TMP", [P, 2, TS])
        WAB = sb("WAB", [P, L, KD, 2 * H])
        WL = sb("WL", [P, L, 2, 2, P])
        FN = sb("FN", [P, KD])
        RW = sb("RW", [P, KD, NE])
        RB = sb("RB", [1, NE])
        ST = sb("ST", [P, 2 * NB])
        SN = sb("SN", [P, 2 * G9])
        SC = sb("SC", [P, 2, NB, WA - 1])
        SCQ = sb("SCQ", [P, 14, NB, WQ - 1])
        NA = sb("NA", [P, 2, NB, WA - 1])
        NQ = sb("NQ", [P, 14, G9, WQ - 1])
        ABt = sb("ABt", [P, NCH, 2 * H])
        SM = sb("SM", [P, 16, NCH * H])
        LM = sb("LM", [P, L, 8, 2])
        LG = sb("LG", [P, NCH, NE])
        MX = sb("MX", [P, NCH, NE])
        IX = sb("IX", [P, NCH, NE], U32)
        IXF = sb("IXF", [P, NCH, 2])
        GG = sb("GG", [P, 2, NCH, NE])
        G12 = sb("G12", [P, 4, NCH])
        ELS = sb("ELS", [P, NB, H])
        GSEL = sb("GSEL", [TS, NB, H])

        PB = [ctx.enter_context(nc.psum_tensor(f"PB{i}", [P, 512], F32)) for i in range(8)]
        PM, PS = [PB[0], PB[2]], [PB[1], PB[3]]

        pj = PJ[:, :].rearrange("p (m c) -> p m c", c=CW)
        act_t = PJ[:, 0:FF * T].rearrange("p (m t) -> p m t", t=T)
        work0 = QKV * CW
        def wk(i, n=1):
            return PJ[:, work0 + i * 512:work0 + (i + n) * 512]
        w4 = lambda i: wk(i).rearrange("p (h c) -> p h c", h=H)
        lw = lambda i: PJ[:, work0 + i * 2 * T:work0 + (i + 1) * 2 * T].rearrange("p (c t) -> p c t", c=2)
        ident, tri = CO[:, C_ID:C_ID + P], CO[:, C_TRI:C_TRI + P]
        btri, bone = CO[0:TS, C_BTRI:C_BTRI + TS], CO[0:TS, C_BONE:C_BONE + TS]
        bm, iota = CO[0:TS, C_BM:C_BM + NB], CO[:, C_IOTA:C_IOTA + NE]
        lvl = lambda v, n: CO[0:n, C_LVL + v * P:C_LVL + v * P + n]
        par = lambda name, l, i=0, w=1: PA[:, l, PC[name][0] + i:PC[name][0] + i + w]
        pv_s = lambda ap: ap.rearrange("p (b s) -> p b s", s=NS)

        names = """ab_gates ab_pe act_own c_act consts conv_a conv_l conv_q dd_exp dd_min dd_ready dve_own
            eg_ready free_m0 free_m1 free_s0 free_s1 gate_exp gb_pe gb_ready gc_pe gelu_ready glu_ready
            gt_copied gt_pe h_main h_mul h_small in_small ks_copied ks_pe ks_tr l2_done l2_pe l2_sq l2_sqrt
            lam_abs lg_exp lg_pe lg_ready ln_done ln_mean ln_sq ln_sub ln_sum ln_used lru_g_pe lru_new
            lru_scan lru_sqrt lru_t lru_tz mat_pe mod_done new_states o_copied o_pe on_pe on_scaled on_sq
            on_sqrt ones_ready out_done out_states p_copied p_pe pads_ready pool_own q_silu qg_ready
            r_ready rhs_ready rs_sqrt sg_gated silu_z sm_mask sm_pe sm_upd small_exp small_exp2 small_ready
            small_tanh sp_exp sp_zero sq_ready sq_used st_done st_pe states_in t_done t_pe tr_evac tr_pe
            um_ready vn_copied vn_pe w_used x_ready y_ready ya_ready yb_ready yc_pe yc_ready yc_sq yc_sqrt""".split()
        S = {n: sem(n) for n in names}
        landed = [sem(f"landed{i}") for i in range(RING)]
        free_m, free_s = [S["free_m0"], S["free_m1"]], [S["free_s0"], S["free_s1"]]
        block = ctx.enter_context(nc.Block())

        def slot_of(f0, s):
            return (f0 + s) % RING

        def wait_landed(eng, f0, s, j):
            eng.wait_ge(landed[(f0 + s) % RING], (j + ((f0 + s) // RING + 1)) * 16)

        @block.sync
        def _(sp):
            first = (("consts", CO), ("params", PA), ("cT", CT), ("x", xT), ("wab", WAB), ("fnorm", FN), ("rw", RW), ("rb", RB))
            for name, dst in first:
                sp.dma_start(dst[:], io[name]).then_inc(S["consts"], 16)

            def stream(src, width, f0, nf, guard=True):
                def fill(j, s):
                    if guard:
                        sp.wait_ge(S["w_used"], j * RING + (f0 + s - RING + 1))
                    sp.dma_start(ring[:, slot_of(f0, s), 0:width], src[j * RING + s]).then_inc(landed[slot_of(f0, s)], 16)
                if nf == RING:
                    for s in range(RING):
                        fill(0, s)
                else:
                    with sp.Fori(0, nf // RING) as j:
                        for s in range(RING):
                            fill(j, s)
            for l in range(L):
                if l == 0:
                    stream(io["w_ada"][l, 0:RING], KD * P, 0, RING, guard=False)
                    stream(io["w_ada"][l, RING:M_ADA], KD * P, RING, F_ADA - RING)
                else:
                    stream(io["w_ada"][l], KD * P, FILL["ada", l], F_ADA)
                stream(io["w_in"][l], KD * P, FILL["in", l], F_IN)
                stream(io["w_out"][l], KD * P, FILL["out", l], F_OUT)
                if l % 2 == 0:
                    stream(io["ffn_gu"], KD * P, FILL["gu", l], F_GU)
                    stream(io["ffn_dn"], SLOT, FILL["dn", l], F_DN)
                else:
                    pair = 2 * (2 * FE + KD)
                    f0 = FILL["moe", l]
                    with sp.Fori(0, NE // 2) as e2:
                        for e in range(2):
                            fe = f0 + e * (pair // 2)
                            def fill(src, width, f):
                                sp.wait_ge(S["w_used"], e2 * pair + (f - RING + 1))
                                sp.dma_start(ring[:, f % RING, 0:width], src).then_inc(landed[f % RING], 16)
                            for g in range(2 * FE):
                                fill(io["moe_gu"][e2 * 2 + e, g], KD * P, fe + g)
                            for m in range(KD):
                                fill(io["moe_dn"][e2 * 2 + e, m], SLOT, fe + 2 * FE + m)
            sp.wait_ge(S["y_ready"], KD)
            sp.dma_start(io["y"], hT[:]).then_inc(S["out_done"], 16)
            sp.wait_ge(S["out_done"], 16)

        def chunk(n):
            return (slice(n * P, n * P + P), P, LEVELS) if n < 4 else (slice(TP, T), TS, SLEVELS)

        LVL_ALL = [(n, v) for n in range(NCH) for v in range(chunk(n)[2])]

        def mixer_pe(pe, l):
            mm = pe.matmul
            t1 = TILE["in", l] + M_IN
            for b in range(2):
                pe.wait_ge(free_m[b], t1 // 2)
                pe.wait_ge(free_s[b], t1 // 2)
            for r in range(2):
                for c in range(2):
                    if r == 0:
                        pe.wait_ge(S["conv_a"], 2 * l + c + 1)
                        src = XA[:, c, :]
                    else:
                        pe.wait_ge(S["ln_sq"], 2 * l + c + 1)
                        src = SQ[:, c, :]
                    mm(PB[2 * r][:, :], ONES[:], src[:, 0:TP], start=(c == 0), stop=(c == 1))
                    end = mm(PB[2 * r + 1][:, 0:TS], ONES[:], src[:, TP:T], start=(c == 0), stop=(c == 1))
                end.then_inc(S["ln_sum"], 1)
            pe.wait_ge(S["small_ready"], 4 * l + 2)
            g = SM[:, 3, :]
            mm(PB[7][:, 64:80], tri, g[:, 0:16], start=True, stop=True)
            mm(PB[7][0:TS, 80:84], btri, g[0:TS, 16:20], start=True, stop=True)
            mm(PB[7][:, 84:100], ONES[:], g[:, 0:16], start=True, stop=True)
            mm(PB[7][0:TS, 100:104], bone, g[0:TS, 16:20], start=True, stop=True)
            mm(PB[7][:, 104:136], ONES[0:TS, :], GSEL[:].rearrange("p b h -> p (b h)"), start=True, stop=True).then_inc(S["gc_pe"], 1)
            pe.wait_ge(S["conv_l"], 2 * (l + 1))
            pe.wait_ge(S["in_small"], 16 * 8 * L)
            for c in range(2):
                for a in range(2):
                    if 2 * c + a > 0:
                        pe.wait_ge(S["lru_t"], 4 * l + 2 * c + a)
                    mm(PB[5][:, :], WL[:, l, a, c, :], XL[:, c, 0:TP], start=True, stop=True)
                    mm(PB[6][:, 0:TS], WL[:, l, a, c, :], XL[:, c, TP:T], start=True, stop=True).then_inc(S["lru_g_pe"], 1)
            for c in range(2):
                pe.wait_ge(S["yc_sq"], 2 * l + c + 1)
                mm(PB[5][:, :], ONES[:], SQ[:, c, 0:TP], start=(c == 0), stop=(c == 1))
                end = mm(PB[6][:, 0:TS], ONES[:], SQ[:, c, TP:T], start=(c == 0), stop=(c == 1))
            end.then_inc(S["yc_pe"], 1)
            for i in range(2 * H):
                pe.wait_ge(S["l2_sq"], 8 * l + i + 1)
                mm(PM[i % 2][:, :], ONES[:], SQ[:, i % 2, 0:TP], start=True, stop=True)
                mm(PS[i % 2][:, 0:TS], ONES[:], SQ[:, i % 2, TP:T], start=True, stop=True).then_inc(S["l2_pe"], 1)
            pe.wait_ge(S["l2_done"], 8 * (l + 1))
            pe.wait_ge(S["yc_sqrt"], l + 1)
            for n in range(NCH):
                tok, m, levels = chunk(n)
                q = NCH * l + n
                b4 = lambda i, rows=P, w=P: PB[i][0:rows, 0:H * w].rearrange("p (h c) -> p h c", h=H)
                kT = lambda hh: QC[:, H + hh, tok]
                qT = lambda hh: QC[:, hh, tok]
                pe.wait_ge(S["q_silu"], 12 * (l + 1))
                if n > 0:
                    pe.wait_ge(S["st_done"], H * 4 * l + H * n)
                    pe.wait_ge(S["o_copied"], q)
                for hh in range(H):
                    pe.transpose(b4(0, m)[:, hh, :], kT(hh), ident)
                for hh in range(H):
                    end = pe.transpose(b4(1, m)[:, hh, :], QC[:, 2 * H + hh, tok], ident)
                end.then_inc(S["tr_pe"], 1)
                for hh in range(H):
                    mm(b4(2, m, m)[:, hh, :], kT(hh), kT(hh), start=True, stop=True)
                    mm(b4(3, m, m)[:, hh, :], kT(hh), qT(hh), start=True, stop=True)
                pe.wait_ge(S["rhs_ready"], q + 1)
                mm(PB[4][:, 0:H * m], ONES[0:m, :], w4(7)[0:m, :, 0:m], start=True, stop=True)
                mm(PB[5][0:m, 0:H * m], ONES[0:m, 0:m], w4(8)[0:m, :, 0:m], start=True, stop=True).then_inc(S["mat_pe"], 1)
                for v in range(levels):
                    z = sum(chunk(i)[2] for i in range(n)) + v + len(LVL_ALL) * l
                    pe.wait_ge(S["um_ready"], z + 1)
                    if v > 0:
                        pe.wait_ge(S["t_done"], z)
                    else:
                        pe.wait_ge(S["tr_evac"], 2 * (q + 1))
                    um = w4(7 + v % 2)
                    for hh in range(H):
                        end = mm(b4(6, m, m)[:, hh, :], um[0:m, hh, 0:m], ident[0:m, 0:m] if v == 0 else w4(9)[0:m, hh, 0:m], start=True, stop=True)
                    end.then_inc(S["p_pe"], 1)
                    if v == 0:
                        continue
                    pe.wait_ge(S["p_copied"], z - q)
                    if v < levels - 1:
                        for hh in range(H):
                            mm(b4(7, m, m)[:, hh, :], w4(10)[0:m, hh, 0:m], w4(11)[0:m, hh, 0:m], start=True, stop=True)
                    for hh in range(H):
                        end = mm(b4(0, m, m)[:, hh, :], w4(11)[0:m, hh, 0:m], w4(10)[0:m, hh, 0:m], start=True, stop=True)
                    end.then_inc(S["t_pe"], 1)
                z1 = sum(chunk(i)[2] for i in range(n + 1)) + len(LVL_ALL) * l
                pe.wait_ge(S["t_done"], z1)
                pe.wait_ge(S["dd_ready"], q + 1)
                if n < 4:
                    if n == 0:
                        pe.wait_ge(S["sp_zero"], l + 1)
                    for hh in range(H):
                        end = mm(b4(1, m)[:, hh, :], kT(hh), SP_[:, hh, :], start=True, stop=True)
                    end.then_inc(S["ks_pe"], 1)
                    kb = 1
                else:
                    pe.wait_ge(S["states_in"], 16 * 5 * (l + 1))
                    for hh in range(H):
                        for b in range(NB):
                            end = mm(b4(1, P, m)[:, hh, b * NS:(b + 1) * NS], SS[:, b, hh, :], QC[:, H + hh, TP + b * NS:TP + (b + 1) * NS],
                                     start=True, stop=True)
                    end.then_inc(S["ks_pe"], 1)
                    pe.wait_ge(S["ks_copied"], l + 1)
                    for hh in range(H):
                        end = pe.transpose(b4(5, m)[:, hh, :], w4(11)[:, hh, 0:m], ident)
                    end.then_inc(S["ks_tr"], 1)
                pe.wait_ge(S["r_ready"], q + 1)
                for hh in range(H):
                    end = mm(b4(2, m)[:, hh, :], w4(10)[0:m, hh, 0:m], w4(12)[0:m, hh, :], start=True, stop=True)
                end.then_inc(S["vn_pe"], 1)
                pe.wait_ge(S["vn_copied"], q + 1)
                pe.wait_ge(S["qg_ready"], q + 1)
                for hh in range(H):
                    o = b4(3, P, m)[:, hh, :]
                    end = mm(o, w4(13)[0:m, hh, :], w4(6)[0:m, hh, 0:m], start=True, stop=False, skip_group_check=True)
                    if n < 4:
                        end = mm(o, SP_[:, hh, :], w4(2)[:, hh, 0:m], start=False, stop=True, skip_group_check=True)
                    else:
                        for b in range(NB):
                            end = mm(o[:, b * NS:(b + 1) * NS], SS[:, b, hh, :], w4(2)[:, hh, b * NS:(b + 1) * NS],
                                     start=False, stop=True, skip_group_check=True)
                end.then_inc(S["o_pe"], 1)
                if n < 4:
                    for hh in range(H):
                        end = mm(b4(4)[:, hh, :], w4(0)[:, hh, :], w4(13)[:, hh, :], start=True, stop=True)
                    end.then_inc(S["st_pe"], 1)
                else:
                    for b in range(NB):
                        pe.wait_ge(S["sm_mask"], NB * l + b + 1)
                        if b >= 2:
                            pe.wait_ge(S["sm_upd"], H * (NB * l + b - 1))
                        for hh in range(H):
                            end = mm(b4(6 + b % 2)[:, hh, :], w4(7 + b % 2)[0:TS, hh, :], w4(13)[0:TS, hh, :], start=True, stop=True)
                        end.then_inc(S["sm_pe"], 1)
            for hh in range(H):
                pe.wait_ge(S["on_sq"], H * l + hh + 1)
                mm(PM[hh % 2][:, :], ONES[:], SQ[:, hh % 2, 0:TP], start=True, stop=True)
                mm(PS[hh % 2][:, 0:TS], ONES[:], SQ[:, hh % 2, TP:T], start=True, stop=True).then_inc(S["on_pe"], 1)
            pe.wait_ge(S["on_sqrt"], 2 * H * (l + 1))

        @block.tensor
        def _(pe):
            mm = pe.matmul

            def norm_sums(q):
                if q == 0:
                    pe.wait_ge(S["ones_ready"], 2)
                for k in range(KD):
                    pe.wait_ge(S["sq_ready"], KD * q + k + 1)
                    mm(PB[5][:, :], ONES[:], SQ[:, k % 2, 0:TP], start=(k == 0), stop=(k == KD - 1))
                    mm(PB[6][:, 0:TS], ONES[:], SQ[:, k % 2, TP:T], start=(k == 0), stop=(k == KD - 1)).then_inc(S["sq_used"], 1)

            def tile_mms(slot, b, nk, rhs, first=True, last=True, k0=0):
                for k in range(nk):
                    w = ring[:, slot, k * P:(k + 1) * P]
                    a, z = first and k == 0, last and k == nk - 1
                    mm(PM[b][:, :], w, rhs(k0 + k)[:, 0:TP], start=a, stop=z)
                    end = mm(PS[b][:, 0:TS], w, rhs(k0 + k)[:, TP:T], start=a, stop=z)
                end.then_inc(S["w_used"], 1)

            def wait_free(b, count):
                pe.wait_ge(free_m[b], count)
                pe.wait_ge(free_s[b], count)

            def gemm(l, stage, nf, rhs):
                f0, t0 = FILL[stage, l], TILE[stage, l]
                def rnd(j, peeled):
                    for s in range(RING):
                        wait_landed(pe, f0, s, j)
                        if not (peeled and t0 + s < 2):
                            wait_free(s % 2, j * 2 + (t0 + s) // 2)
                        tile_mms(slot_of(f0, s), s % 2, KD, rhs)
                if t0 == 0:
                    rnd(0, True)
                with pe.Fori(1 if t0 == 0 else 0, nf // RING) as j:
                    rnd(j, False)

            h = lambda k: hT[:, k, :]
            for l in range(L):
                if l == 0:
                    pe.wait_ge(S["c_act"], 1)
                else:
                    pe.wait_ge(S["mod_done"], l)
                f0 = FILL["ada", l]
                with pe.Fori(0, M_ADA // RING) as j:
                    for s in range(RING):
                        wait_landed(pe, f0, s, j)
                        for k in range(KD):
                            end = mm(PB[4][:, bass.ds((j * RING + s) * G9, G9)], ring[:, slot_of(f0, s), k * P:(k + 1) * P], CT[:, k, :],
                                     start=(k == 0), stop=(k == KD - 1))
                        end.then_inc(S["w_used"], 1)
                norm_sums(2 * l)
                pe.wait_ge(S["h_main"], KD * (2 * l + 1))
                pe.wait_ge(S["h_small"], 2 * l + 1)
                gemm(l, "in", F_IN, h)
                for n in range(NCH):
                    tok = slice(n * P, min((n + 1) * P, T))
                    m = tok.stop - tok.start
                    for k in range(KD):
                        end = mm(PB[7][0:m, n * 8:n * 8 + 8], hT[:, k, tok], WAB[:, l, k, :], start=(k == 0), stop=(k == KD - 1))
                end.then_inc(S["ab_pe"], 1)
                mixer_pe(pe, l)
                pe.wait_ge(S["ya_ready"], 2 * (l + 1))
                pe.wait_ge(S["yb_ready"], H * (l + 1))
                pe.wait_ge(S["yc_ready"], 2 * (l + 1))
                gemm(l, "out", F_OUT, h)
                norm_sums(2 * l + 1)
                pe.wait_ge(S["h_main"], KD * (2 * l + 2))
                pe.wait_ge(S["h_small"], 2 * l + 2)
                if l % 2 == 0:
                    gemm(l, "gu", F_GU, h)
                    f0, t0 = FILL["dn", l], TILE["dn", l]
                    for fr in (free_m[1], free_s[1]):
                        pe.wait_ge(fr, t0 // 2)
                    with pe.Fori(0, KD // 2) as j:
                        for s in range(2):
                            wait_free(s, j + (t0 + s) // 2)
                            for half in range(2):
                                wait_landed(pe, f0, 2 * s + half, j)
                                tile_mms(slot_of(f0, 2 * s + half), s, FE, lambda k: act_t[:, k, :], half == 0, half == 1, half * FE)
                else:
                    for n in range(NCH):
                        tok = slice(n * P, min((n + 1) * P, T))
                        m = tok.stop - tok.start
                        for k in range(KD):
                            mm(PB[4][0:m, n * NE:(n + 1) * NE], hT[:, k, tok], RW[:, k, :], start=(k == 0), stop=False)
                        end = mm(PB[4][0:m, n * NE:(n + 1) * NE], ONES[0:1, 0:m], RB[:], start=False, stop=True)
                    end.then_inc(S["lg_pe"], 1)
                    pe.wait_ge(S["lg_ready"], 1)
                    for n in range(NCH):
                        m = min((n + 1) * P, T) - n * P
                        out = PB[5][0:NE, n * P:n * P + m] if n < 4 else PB[6][0:NE, 0:m]
                        end = pe.transpose(out, GG[0:m, 1, n, :], ident[0:m, 0:m])
                    end.then_inc(S["gt_pe"], 1)
                    pe.wait_ge(S["gt_copied"], 1)
                    for e in range(NE):
                        if e > 0:
                            pe.wait_ge(S["gb_ready"], e)
                        sel = ident[0:NE, e:e + 1].broadcast_to([NE, P])
                        mm(PB[5][:, :], sel, RS[0:NE, 0:TP], start=True, stop=True)
                        mm(PB[6][:, 0:TS], sel, RS[0:NE, TP:T], start=True, stop=True).then_inc(S["gb_pe"], 1)
                    pair = 2 * FE + KD
                    f0, t0 = FILL["moe", l], TILE["moe", l]
                    with pe.Fori(0, NE // 2) as e2:
                        for e in range(2):
                            for i in range(pair):
                                f, t = f0 + e * pair + i, t0 + e * pair + i
                                pe.wait_ge(landed[f % RING], (e2 * (2 * pair // RING) + (f // RING + 1)) * 16)
                                wait_free(t % 2, e2 * pair + t // 2)
                                if i == 2 * FE:
                                    for fr in (free_m[1], free_s[1]):
                                        pe.wait_ge(fr, e2 * pair + t // 2)
                                if i < 2 * FE:
                                    tile_mms(f % RING, t % 2, KD, h)
                                else:
                                    tile_mms(f % RING, t % 2, FE, lambda k: act_t[:, e * FE + k, :])
            norm_sums(2 * L)

        def mixer_act(act, l):
            fn = act.activation
            t1 = TILE["in", l] + M_IN
            for fr in free_m + free_s:
                act.wait_ge(fr, t1 // 2)
            act.wait_ge(S["ab_gates"], l + 1)
            fn(SM[:, 1, :], SM[:, 0, :], ACT.Exp).then_inc(S["small_exp"], 1)
            fn(SM[:, 11, :].rearrange("p (n h) -> p n h", h=H), ABt[:, :, 0:H], ACT.Tanh, scale=0.5).then_inc(S["small_tanh"], 1)
            fn(SM[:, 12, 0:H], par("a_log", l, 0, H), ACT.Exp).then_inc(S["small_tanh"], 1)
            for c in range(2):
                act.wait_ge(S["ln_sub"], 2 * l + c + 1)
                fn(SQ[:, c, :], XA[:, c, :], ACT.Square).then_inc(S["ln_sq"], 1)
            act.wait_ge(S["ln_sum"], 2 * l + 2)
            fn(RS[:, 0:TP], PB[2][:, :], ACT.Sqrt, scale=1.0 / 256, bias=EPSC[:, 0:1]).then_inc(S["ln_mean"], 1)
            fn(RS[:, TP:T], PB[3][:, 0:TS], ACT.Sqrt, scale=1.0 / 256, bias=EPSC[:, 0:1]).then_inc(S["ln_mean"], 1)
            act.wait_ge(S["conv_q"], 12 * (l + 1))
            act.wait_ge(S["new_states"], l + 1)
            for c in range(2):
                for a in range(2):
                    act.wait_ge(S["lru_g_pe"], 4 * l + 2 * c + a + 1)
                    bias = LM[:, l, 6 + a, c:c + 1]
                    fn(lw(a)[:, c, 0:TP], PB[5][:, :], ACT.Tanh, scale=0.5, bias=bias).then_inc(S["act_own"], 1)
                    fn(lw(a)[:, c, TP:T], PB[6][:, 0:TS], ACT.Tanh, scale=0.5, bias=bias).then_inc(S["lru_t"], 1)
            act.wait_ge(S["lru_t"], 4 * (l + 1))
            for c in range(2):
                fn(lw(2)[:, c, :], lw(0)[:, c, :], ACT.Tanh, scale=LM[:, l, 5, c:c + 1], bias=LM[:, l, 5, c:c + 1]).then_inc(S["lru_tz"], 1)
            act.wait_ge(S["small_ready"], 4 * l + 3)
            fn(SM[:, 6, :], SM[:, 4, :], ACT.Exp).then_inc(S["small_exp2"], 1)
            fn(SM[:, 8, :], SM[:, 7, :], ACT.Exp).then_inc(S["small_exp2"], 1)
            fn(SM[:, 9, :], SM[:, 5, :], ACT.Exp).then_inc(S["small_exp2"], 1)
            fn(ELS[:], ELS[:], ACT.Exp).then_inc(S["small_exp2"], 1)
            for c in range(2):
                fn(pj[:, LRU_G + c, SO - TP:CW], pj[:, LRU_G + c, SO - TP:CW], ACT.Gelu_apprx_tanh).then_inc(S["gelu_ready"], 1)
            act.wait_ge(S["lru_tz"], 2 * (l + 1))
            fn(lw(4)[:], lw(2)[:], ACT.Sqrt).then_inc(S["lru_sqrt"], 1)
            for c in range(2):
                act.wait_ge(S["ln_done"], 2 * l + c + 1)
                fn(hT[:, c, :], XA[:, c, :], ACT.Silu, scale=par("ln_a_g", l, c), bias=par("ln_a_b", l, c)).then_inc(S["ya_ready"], 1)
            for i in range(12):
                act.wait_ge(S["conv_q"], 12 * l + i + 1)
                fn(QC[:, i, :], QC[:, i, :], ACT.Silu).then_inc(S["q_silu"], 1)
            fn(pj[:, ZT:ZT + H, SO - TP:CW], pj[:, ZT:ZT + H, SO - TP:CW], ACT.Silu).then_inc(S["silu_z"], 1)
            for c in range(2):
                act.wait_ge(S["lru_scan"], 2 * l + c + 1)
                fn(SQ[:, c, :], lw(3)[:, c, :], ACT.Square).then_inc(S["yc_sq"], 1)
            act.wait_ge(S["yc_pe"], l + 1)
            act.wait_ge(S["ln_used"], l + 1)
            fn(RS[:, 0:TP], PB[5][:, :], ACT.Sqrt, scale=1.0 / 256, bias=EPSC[:, 0:1]).then_inc(S["act_own"], 1)
            fn(RS[:, TP:T], PB[6][:, 0:TS], ACT.Sqrt, scale=1.0 / 256, bias=EPSC[:, 0:1]).then_inc(S["yc_sqrt"], 1)
            for i in range(2 * H):
                act.wait_ge(S["q_silu"], 12 * (l + 1))
                if i >= 2:
                    act.wait_ge(S["l2_pe"], 8 * l + i - 1)
                else:
                    act.wait_ge(S["yc_pe"], l + 1)
                fn(SQ[:, i % 2, :], QC[:, i, :], ACT.Square).then_inc(S["l2_sq"], 1)
                if i > 0:
                    l2_root(act, l, i - 1)
            l2_root(act, l, 2 * H - 1)
            for n in range(NCH):
                tok, m, levels = chunk(n)
                q = NCH * l + n
                act.wait_ge(S["tr_pe"], q + 1)
                b4 = lambda i, rows=P, w=P: PB[i][0:rows, 0:H * w].rearrange("p (h c) -> p h c", h=H)
                act.wait_ge(S["small_exp2"], 4 * (l + 1))
                for hh in range(H):
                    e = fn(w4(0)[0:m, hh, :], b4(0, m)[:, hh, :], ACT.Copy, scale=SM[0:m, 8, n * H + hh:n * H + hh + 1])
                e.then_inc(S["tr_evac"], 1)
                for hh in range(H):
                    e = fn(w4(1)[0:m, hh, :], b4(1, m)[:, hh, :], ACT.Copy, scale=SM[0:m, 2, n * H + hh:n * H + hh + 1])
                e.then_inc(S["tr_evac"], 1)
                act.wait_ge(S["mat_pe"], q + 1)
                fn(w4(3)[:, :, 0:m], b4(4, P, m), ACT.Exp).then_inc(S["eg_ready"], 1)
                act.wait_ge(S["dd_min"], q + 1)
                fn(w4(4)[0:m, :, 0:m], w4(4)[0:m, :, 0:m], ACT.Exp).then_inc(S["dd_exp"], 1)
                for v in range(1, levels):
                    z = sum(chunk(i)[2] for i in range(n)) + v + len(LVL_ALL) * l
                    act.wait_ge(S["p_pe"], z + 1)
                    fn(w4(11)[0:m, :, 0:m], b4(6, m, m), ACT.Copy).then_inc(S["p_copied"], 1)
                if n == 4:
                    act.wait_ge(S["ks_pe"], q + 1)
                    fn(w4(11)[:, :, 0:m], b4(1, P, m), ACT.Copy).then_inc(S["ks_copied"], 1)
                act.wait_ge(S["vn_pe"], q + 1)
                fn(w4(13)[0:m], b4(2, m), ACT.Copy).then_inc(S["vn_copied"], 1)
                act.wait_ge(S["o_pe"], q + 1)
                fn(hT[:, 2:2 + H, tok], b4(3, P, m), ACT.Copy).then_inc(S["o_copied"], 1)
            for hh in range(H):
                act.wait_ge(S["o_copied"], NCH * (l + 1))
                if hh >= 2:
                    act.wait_ge(S["on_pe"], H * l + hh - 1)
                fn(SQ[:, hh % 2, :], hT[:, 2 + hh, :], ACT.Square).then_inc(S["on_sq"], 1)
                if hh > 0:
                    on_root(act, l, hh - 1)
            on_root(act, l, H - 1)

        def l2_root(act, l, i):
            s = float(P) if i < H else 1.0
            act.wait_ge(S["l2_pe"], 8 * l + i + 1)
            if i > 0:
                act.wait_ge(S["l2_done"], 8 * l + i)
            else:
                act.wait_ge(S["yc_ready"], 2 * (l + 1))
            bias = EPSC[:, 1:2] if i < H else EPSC[:, 0:1]
            act.activation(RS[:, 0:TP], PM[i % 2][:, :], ACT.Sqrt, scale=s, bias=bias).then_inc(S["l2_sqrt"], 1)
            act.activation(RS[:, TP:T], PS[i % 2][:, 0:TS], ACT.Sqrt, scale=s, bias=bias).then_inc(S["l2_sqrt"], 1)

        def on_root(act, l, hh):
            act.wait_ge(S["on_pe"], H * l + hh + 1)
            if hh > 0:
                act.wait_ge(S["on_scaled"], H * l + hh)
            act.activation(RS[:, 0:TP], PM[hh % 2][:, :], ACT.Sqrt, scale=1.0 / P, bias=EPSC[:, 0:1]).then_inc(S["on_sqrt"], 1)
            act.activation(RS[:, TP:T], PS[hh % 2][:, 0:TS], ACT.Sqrt, scale=1.0 / P, bias=EPSC[:, 0:1]).then_inc(S["on_sqrt"], 1)


        X_DONE = {1: 16, 2: 32, 3: 48, 4: 48 + 16 * NE}

        @block.scalar
        def _(act):
            fn = act.activation

            def squares(q):
                if q == 0:
                    act.wait_ge(S["consts"], 8 * 16)
                else:
                    act.wait_ge(S["x_ready"], X_DONE[q])
                for k in range(KD):
                    if KD * q + k >= 2:
                        act.wait_ge(S["sq_used"], KD * q + k - 1)
                    fn(SQ[:, k % 2, :], xT[:, k, :], ACT.Square).then_inc(S["sq_ready"], 1)

            def root(q):
                act.wait_ge(S["sq_used"], KD * (q + 1))
                fn(RS[:, 0:TP], PB[5][:, :], ACT.Sqrt, scale=1.0 / D, bias=EPSC[:, 0:1]).then_inc(S["rs_sqrt"], 1)
                fn(RS[:, TP:T], PB[6][:, 0:TS], ACT.Sqrt, scale=1.0 / D, bias=EPSC[:, 0:1]).then_inc(S["rs_sqrt"], 1)

            def modulate(q):
                l, w = q // 2, q % 2
                act.wait_ge(S["mod_done"], l + 1)
                for k in range(KD):
                    act.wait_ge(S["h_mul"], KD * q + k + 1)
                    fn(hT[:, k, 0:TP], hT[:, k, 0:TP], ACT.Identity, scale=AM[:, w, k, 0:1], bias=MOD[:, 3 * KD * w + k, 0:1]).then_inc(S["h_main"], 1)

            act.wait_ge(S["consts"], 8 * 16)
            act.wait_ge(S["ones_ready"], 2)
            fn(CT[:], CT[:], ACT.Silu).then_inc(S["c_act"], 1)
            act.wait_ge(S["lam_abs"], 1)
            fn(LM[:, :, 1, :], LM[:, :, 0, :], ACT.Exp).then_inc(S["sp_exp"], 1)
            for l in range(L):
                squares(2 * l)
                root(2 * l)
                modulate(2 * l)
                f0 = FILL["in", l]
                act.wait_ge(S["pads_ready"], l + 1)
                for s in range(4):
                    act.wait_ge(S["w_used"], f0 + s + 1)
                    func = ACT.Copy if s < 2 else ACT.Tanh
                    smp = pj[:, s, SO:CW].rearrange("p (b c) -> p b c", c=WQ - 1 + NS)[:, :, WQ - 1:]
                    fn(pj[:, s, WQ - 1:SO], PM[s % 2][:, :], func, scale=0.5).then_inc(free_m[s % 2], 1)
                    fn(smp, pv_s(PS[s % 2][:, 0:TS]), func, scale=0.5).then_inc(free_s[s % 2], 1)
                with act.Fori(1, F_IN // RING) as j:
                    for s in range(RING):
                        act.wait_ge(S["w_used"], j * RING + (f0 + s + 1))
                        row = PJ[:, bass.ds((j * RING + s) * CW, CW)]
                        fn(row[:, WQ - 1:SO], PM[s % 2][:, :], ACT.Copy).then_inc(free_m[s % 2], 1)
                        smp = row[:, SO:CW].rearrange("p (b c) -> p b c", c=WQ - 1 + NS)[:, :, WQ - 1:]
                        fn(smp, pv_s(PS[s % 2][:, 0:TS]), ACT.Copy).then_inc(free_s[s % 2], 1)
                mixer_act(act, l)
                squares(2 * l + 1)
                root(2 * l + 1)
                modulate(2 * l + 1)
                def silu_tile(f, sq, used):
                    act.wait_ge(S["w_used"], f)
                    act.wait_ge(free_m[1], used)
                    act.wait_ge(free_s[1], used)
                    fn(SQ[:, sq, 0:TP], PM[0][:, :], ACT.Silu).then_inc(free_m[0], 1)
                    fn(SQ[:, sq, TP:T], PS[0][:, 0:TS], ACT.Silu).then_inc(free_s[0], 1)
                if l % 2 == 0:
                    f0 = FILL["gu", l]
                    t0 = TILE["gu", l]
                    with act.Fori(0, FF // 2) as j:
                        for pr in range(2):
                            silu_tile(j * 4 + (f0 + 2 * pr + 1), pr, j * 2 + (t0 // 2 + pr - 1))
                else:
                    act.wait_ge(S["lg_pe"], 1)
                    act.wait_ge(S["lg_exp"], 1)
                    fn(G12[:, 1, :], G12[:, 0, :], ACT.Exp).then_inc(S["gate_exp"], 1)
                    act.wait_ge(S["gt_pe"], 1)
                    act.wait_ge(S["h_mul"], KD * (2 * l + 2))
                    fn(RS[0:NE, 0:TP], PB[5][0:NE, :], ACT.Copy).then_inc(S["act_own"], 1)
                    fn(RS[0:NE, TP:T], PB[6][0:NE, 0:TS], ACT.Copy).then_inc(S["gt_copied"], 1)
                    for e in range(NE):
                        act.wait_ge(S["gb_pe"], e + 1)
                        fn(QC[:, e, 0:TP], PB[5][:, :], ACT.Copy).then_inc(S["act_own"], 1)
                        fn(QC[:, e, TP:T], PB[6][:, 0:TS], ACT.Copy).then_inc(S["gb_ready"], 1)
                    pair = 2 * FE + KD
                    f0, t0 = FILL["moe", l], TILE["moe", l]
                    with act.Fori(0, NE // 2) as e2:
                        for e in range(2):
                            for i in range(FE):
                                silu_tile(e2 * (2 * pair) + (f0 + e * pair + 2 * i + 1), i % 2, e2 * pair + ((t0 + e * pair) // 2 + i - 1))
            squares(2 * L)
            root(2 * L)

        def mixer_dve(dve, l, then, log1p_steps):
            t0 = TILE["in", l]
            for c in range(2):
                dve.wait_ge(free_s[c], t0 // 2 + 2)
                sv = lambda ap: ap.rearrange("p (b c) -> p b c", c=WQ - 1 + NS)[:, :, WQ - 1:]
                dve.scalar_tensor_tensor(UA[:, c, WA - 1:AO], pj[:, A_GATE + c, WQ - 1:SO], 1.0, pj[:, A_VAL + c, WQ - 1:SO], ALU.add, ALU.mult).then_inc(S["glu_ready"], 1)
                us = UA[:, c, AO:CA].rearrange("p (b c) -> p b c", c=WA - 1 + NS)[:, :, WA - 1:]
                dve.scalar_tensor_tensor(us, sv(pj[:, A_GATE + c, SO:CW]), 1.0, sv(pj[:, A_VAL + c, SO:CW]), ALU.add, ALU.mult).then_inc(S["glu_ready"], 1)
            dve.wait_ge(S["glu_ready"], 4 * (l + 1))
            dve.wait_ge(S["pads_ready"], l + 1)

            def conv(dst, src, so, width, w, bias, last_sem):
                step = width - 1 + NS
                for k in range(width):
                    smp = src[:, so:].rearrange("p (b c) -> p b c", c=step)[:, :, k:k + NS]
                    wk_ = w[:, k:k + 1]
                    if k == 0 and bias is not None:
                        a = dve.tensor_scalar(dst[:, 0:TP], src[:, 0:TP], wk_, bias, ALU.mult, ALU.add)
                        then(a)
                        a = dve.tensor_scalar(pv_s(dst[:, TP:T]), smp, wk_, bias, ALU.mult, ALU.add)
                    elif k == 0:
                        a = dve.tensor_scalar(dst[:, 0:TP], src[:, 0:TP], wk_, None, ALU.mult)
                        then(a)
                        a = dve.tensor_scalar(pv_s(dst[:, TP:T]), smp, wk_, None, ALU.mult)
                    else:
                        a = dve.scalar_tensor_tensor(dst[:, 0:TP], src[:, k:k + TP], wk_, dst[:, 0:TP], ALU.mult, ALU.add)
                        then(a)
                        a = dve.scalar_tensor_tensor(pv_s(dst[:, TP:T]), smp, wk_, pv_s(dst[:, TP:T]), ALU.mult, ALU.add)
                    if k < width - 1:
                        then(a)
                a.then_inc(last_sem, 1)

            for c in range(2):
                o = PC["conv_a_w"][0] + c * WA
                conv(XA[:, c, :], UA[:, c, :], AO, WA, PA[:, l, o:o + WA], par("conv_a_b", l, c), S["conv_a"])
            for c in range(2):
                dve.wait_ge(free_s[c], t0 // 2 + 3)
                o = PC["conv_lru_w"][0] + c * WQ
                conv(XL[:, c, :], pj[:, LRU_X + c, :], SO, WQ, PA[:, l, o:o + WQ], par("conv_lru_b", l, c), S["conv_l"])
            for i in range(12):
                dve.wait_ge(free_s[i % 2], (t0 + QKV + i) // 2 + 1)
                o = PC["conv_qkv_w"][0] + i * WQ
                conv(QC[:, i, :], pj[:, QKV + i, :], SO, WQ, PA[:, l, o:o + WQ], None, S["conv_q"])
            dve.wait_ge(S["conv_q"], 12 * (l + 1))
            dve.wait_ge(S["ab_pe"], l + 1)
            then(dve.tensor_copy(ABt[:, 0:4, :], PB[7][:, 0:32].rearrange("p (n c) -> p n c", c=8)))
            then(dve.tensor_copy(ABt[0:TS, 4, :], PB[7][0:TS, 32:40]))
            sm = lambda i: SM[:, i, :]
            v3 = lambda i: SM[:, i, :].rearrange("p (n h) -> p n h", h=H)
            b3 = lambda ap: ap.unsqueeze(1).broadcast_to([P, NCH, H])
            then(dve.tensor_tensor(v3(10), ABt[:, :, H:2 * H], b3(par("dt_bias", l, 0, H)), ALU.add))
            dve.scalar_tensor_tensor(sm(0), sm(10), -1.0, sm(10), ALU.mult, ALU.min).then_inc(S["ab_gates"], 1)
            then(dve.tensor_scalar(sm(10), sm(10), 0.0, None, ALU.max))
            dve.wait_ge(S["small_exp"], l + 1)
            dve.wait_ge(S["small_tanh"], 2 * (l + 1))
            log1p_steps(sm(3), sm(1), sm(13), sm(14), sm(10))
            then(dve.tensor_tensor(v3(3), v3(3), b3(SM[:, 12, 0:H]), ALU.mult))
            then(dve.tensor_scalar(sm(3), sm(3), -1.0, None, ALU.mult))
            dve.tensor_scalar(sm(2), sm(11), 0.5, 0.5, ALU.mult, ALU.add).then_inc(S["small_ready"], 1)
            dve.tensor_tensor(GSEL[:], SM[0:TS, 3, 16:20].unsqueeze(1).broadcast_to([TS, NB, H]),
                              bm.unsqueeze(2).broadcast_to([TS, NB, H]), ALU.mult).then_inc(S["small_ready"], 1)
            dve.wait_ge(S["ln_sum"], 2 * l + 1)
            for c in range(2):
                then(dve.scalar_tensor_tensor(XA[:, c, 0:TP], PB[0][:, :], -1.0 / 256, XA[:, c, 0:TP], ALU.mult, ALU.add))
                dve.scalar_tensor_tensor(XA[:, c, TP:T], PB[1][:, 0:TS], -1.0 / 256, XA[:, c, TP:T], ALU.mult, ALU.add).then_inc(S["ln_sub"], 1)
            dve.wait_ge(S["ln_mean"], 2 * (l + 1))
            then(dve.reciprocal(RS[:], RS[:]))
            for c in range(2):
                ins = dve.tensor_tensor(XA[:, c, :], XA[:, c, :], RS[:], ALU.mult)
                ins.then_inc(S["ln_done"], 1)
            dve.wait_ge(S["ln_done"], 2 * (l + 1))
            dve.sem_inc(S["ln_used"], 1)
            dve.wait_ge(S["gc_pe"], l + 1)
            then(dve.tensor_copy(SM[:, 4, 0:16], PB[7][:, 64:80]))
            then(dve.tensor_copy(SM[0:TS, 4, 16:20], PB[7][0:TS, 80:84]))
            then(dve.tensor_copy(SM[:, 5, 0:16], PB[7][:, 84:100]))
            then(dve.tensor_copy(SM[0:TS, 5, 16:20], PB[7][0:TS, 100:104]))
            then(dve.tensor_copy(ELS[:].rearrange("p b h -> p (b h)"), PB[7][:, 104:136]))
            dve.tensor_tensor(sm(7), sm(5), sm(4), ALU.subtract).then_inc(S["small_ready"], 1)
            dve.wait_ge(S["small_exp2"], 4 * (l + 1))
            dve.scalar_tensor_tensor(sm(15), sm(2), -1.0, sm(6), ALU.mult, ALU.mult).then_inc(S["small_ready"], 1)
            dve.wait_ge(S["lru_sqrt"], l + 1)
            tr, ti, tz, hs, sq = lw(0), lw(1), lw(2), lw(3), lw(4)
            then(dve.tensor_scalar(tr, tz, 1.0, None, ALU.add))
            then(dve.reciprocal(tr, tr))
            then(dve.tensor_scalar(tz, tz, -1.0, 1.0, ALU.mult, ALU.add))
            then(dve.tensor_tensor(tz, tz, tr, ALU.mult))
            then(dve.tensor_tensor(sq, sq, tr, ALU.mult))
            then(dve.scalar_tensor_tensor(ti, ti, 1.0, XL[:], ALU.add, ALU.mult))
            then(dve.tensor_tensor(sq, sq, ti, ALU.mult))
            a0 = tz[:, :, TP:T].rearrange("p c (b s) -> p c b s", s=NS)[:, :, :, 0]
            b0 = sq[:, :, TP:T].rearrange("p c (b s) -> p c b s", s=NS)[:, :, :, 0]
            t0_ = SN[:, 0:2 * NB].rearrange("p (c b) -> p c b", c=2)
            dve.wait_ge(S["states_in"], 16 * 5 * (l + 1))
            then(dve.tensor_tensor(t0_, a0, ST[:].rearrange("p (c b) -> p c b", c=2), ALU.mult))
            then(dve.tensor_tensor(b0, b0, t0_, ALU.add))
            then(dve.memset(a0, 0.0))
            for c in range(2):
                then(dve.tensor_tensor_scan(hs[:, c, :], tz[:, c, :], sq[:, c, :], 0.0, ALU.mult, ALU.add))
            sn = SN[:].rearrange("p (c g) -> p c g", c=2)
            then(dve.tensor_copy(sn[:, :, 0:1], hs[:, :, TP - 1:TP]))
            dve.tensor_copy(sn[:, :, 1:G9], hs[:, :, TP:T].rearrange("p c (b s) -> p c b s", s=NS)[:, :, :, NS - 1]).then_inc(S["lru_new"], 1)
            dve.wait_ge(S["lru_new"], l + 1)
            dve.wait_ge(S["gelu_ready"], 2 * (l + 1))
            for c in range(2):
                then(dve.tensor_tensor(hs[:, c, 0:TP], hs[:, c, 0:TP], pj[:, LRU_G + c, SO - TP:SO], ALU.mult))
                gs = pj[:, LRU_G + c, SO:CW].rearrange("p (b c) -> p b c", c=WQ - 1 + NS)[:, :, WQ - 1:]
                dve.tensor_tensor(pv_s(hs[:, c, TP:T]), pv_s(hs[:, c, TP:T]), gs, ALU.mult).then_inc(S["lru_scan"], 1)
            dve.wait_ge(S["lru_scan"], 2 * (l + 1))
            dve.wait_ge(S["yc_sqrt"], l + 1)
            then(dve.reciprocal(RS[:], RS[:]))
            for c in range(2):
                dve.scalar_tensor_tensor(hT[:, 6 + c, :], hs[:, c, :], par("lru_norm", l, c), RS[:], ALU.mult, ALU.mult).then_inc(S["yc_ready"], 1)
            dve.wait_ge(S["yc_ready"], 2 * (l + 1))
            for i in range(2 * H):
                dve.wait_ge(S["l2_sqrt"], 16 * l + 2 * (i + 1))
                then(dve.reciprocal(RS[:], RS[:]))
                dve.tensor_tensor(QC[:, i, :], QC[:, i, :], RS[:], ALU.mult).then_inc(S["l2_done"], 1)
            dve.wait_ge(S["l2_done"], 8 * (l + 1))
            dve.memset(SP_[:], 0.0).then_inc(S["sp_zero"], 1)
            for n in range(NCH):
                tok, m, levels = chunk(n)
                q = NCH * l + n
                b4 = lambda i, rows=P, w=P: PB[i][0:rows, 0:H * w].rearrange("p (h c) -> p h c", h=H)
                col = lambda i, hh, rows=m: SM[0:rows, i, n * H + hh:n * H + hh + 1]
                mask = tri if n < 4 else btri
                for hh in range(H):
                    then(dve.tensor_scalar(w4(7)[0:m, hh, 0:m], mask[0:m, :], col(3, hh), None, ALU.mult))
                    ins = dve.tensor_scalar(w4(8)[0:m, hh, 0:m], ident[0:m, 0:m], col(2, hh), None, ALU.mult)
                    if hh < H - 1:
                        then(ins)
                ins.then_inc(S["rhs_ready"], 1)
                mb = lambda ap: ap.unsqueeze(1).broadcast_to([m, H, m])
                dve.wait_ge(S["eg_ready"], q + 1)
                dd, uu, qd = w4(4)[0:m, :, 0:m], w4(5)[0:m, :, 0:m], w4(6)[0:m, :, 0:m]
                then(dve.tensor_tensor(dd, b4(4, m, m), SM[0:m, 4, n * H:(n + 1) * H].unsqueeze(2).broadcast_to([m, H, m]), ALU.subtract))
                dve.tensor_scalar(dd, dd, 0.0, None, ALU.min).then_inc(S["dd_min"], 1)
                dve.wait_ge(S["dd_exp"], q + 1)
                then(dve.tensor_tensor(dd, dd, mb(mask[0:m, :]), ALU.mult))
                then(dve.tensor_tensor(uu, b4(2, m, m), dd, ALU.mult))
                then(dve.tensor_tensor(uu, uu, b4(5, m, m), ALU.mult))
                dve.tensor_tensor(qd, b4(3, m, m), dd, ALU.mult).then_inc(S["dd_ready"], 1)
                T_, TT = w4(9)[0:m, :, 0:m], w4(10)[0:m, :, 0:m]
                for v in range(levels):
                    z = sum(chunk(i)[2] for i in range(n)) + v + len(LVL_ALL) * l
                    um = w4(7 + v % 2)[0:m, :, 0:m]
                    dve.tensor_tensor(um, uu, mb(lvl(v, m)), ALU.mult).then_inc(S["um_ready"], 1)
                    if v == 0:
                        dve.wait_ge(S["um_ready"], z + 1)
                        then(dve.tensor_tensor(TT, mb(ident[0:m, 0:m]), um, ALU.subtract))
                        dve.wait_ge(S["p_pe"], z + 1)
                        dve.tensor_tensor(T_, mb(ident[0:m, 0:m]), b4(6, m, m), ALU.subtract).then_inc(S["t_done"], 1)
                    else:
                        dve.wait_ge(S["t_pe"], z - q)
                        if v < levels - 1:
                            then(dve.tensor_tensor(T_, T_, b4(7, m, m), ALU.subtract))
                        dve.tensor_tensor(TT, TT, b4(0, m, m), ALU.subtract).then_inc(S["t_done"], 1)
                    dve.wait_ge(S["t_done"], z + 1)
                src = b4(1, m)
                if n < 4:
                    dve.wait_ge(S["ks_pe"], q + 1)
                else:
                    dve.wait_ge(S["ks_tr"], l + 1)
                    src = b4(5, m)
                for hh in range(H):
                    ins = dve.scalar_tensor_tensor(w4(12)[0:m, hh, :], src[:, hh, :], col(15, hh), w4(1)[0:m, hh, :], ALU.mult, ALU.add)
                ins.then_inc(S["r_ready"], 1)
                if n < 4:
                    dve.wait_ge(S["st_pe"], 4 * l + n + 1)
                    for hh in range(H):
                        dve.scalar_tensor_tensor(SP_[:, hh, :], SP_[:, hh, :], col(9, hh, P), b4(4)[:, hh, :], ALU.mult, ALU.add).then_inc(S["st_done"], 1)
                    dve.wait_ge(S["st_done"], H * (4 * l + n + 1))
                else:
                    for b in range(NB):
                        if b >= 2:
                            dve.wait_ge(S["sm_pe"], NB * l + b - 1)
                        dve.tensor_scalar(w4(7 + b % 2)[0:TS], w4(0)[0:TS], bm[:, b:b + 1], None, ALU.mult).then_inc(S["sm_mask"], 1)
                        if b > 0:
                            sample_state(dve, l, b - 1, b4)
                    sample_state(dve, l, NB - 1, b4)
            dve.wait_ge(S["silu_z"], l + 1)
            for hh in range(H):
                dve.wait_ge(S["on_sqrt"], 2 * (H * l + hh + 1))
                then(dve.reciprocal(RS[:], RS[:]))
                dve.scalar_tensor_tensor(hT[:, 2 + hh, :], hT[:, 2 + hh, :], par("gdn_norm", l), RS[:], ALU.mult, ALU.mult).then_inc(S["on_scaled"], 1)
                dve.wait_ge(S["on_scaled"], H * l + hh + 1)
                then(dve.tensor_tensor(hT[:, 2 + hh, 0:TP], hT[:, 2 + hh, 0:TP], pj[:, ZT + hh, SO - TP:SO], ALU.mult))
                zs = pj[:, ZT + hh, SO:CW].rearrange("p (b c) -> p b c", c=WQ - 1 + NS)[:, :, WQ - 1:]
                dve.tensor_tensor(pv_s(hT[:, 2 + hh, TP:T]), pv_s(hT[:, 2 + hh, TP:T]), zs, ALU.mult).then_inc(S["yb_ready"], 1)

        def sample_state(dve, l, b, b4):
            dve.wait_ge(S["sm_pe"], NB * l + b + 1)
            for hh in range(H):
                dve.scalar_tensor_tensor(SS[:, b, hh, :], SS[:, b, hh, :], ELS[:, b, hh:hh + 1], b4(6 + b % 2)[:, hh, :], ALU.mult, ALU.add).then_inc(S["sm_upd"], 1)

        def router_dve(dve, l, then):
            dve.wait_ge(S["lg_pe"], 1)
            then(dve.tensor_copy(LG[:, 0:4, :], PB[4][:, 0:4 * NE].rearrange("p (n e) -> p n e", e=NE)))
            then(dve.tensor_copy(LG[0:TS, 4, :], PB[4][0:TS, 4 * NE:5 * NE]))
            for n in range(NCH):
                then(dve.max(MX[:, n, :], LG[:, n, :]))
                then(dve.max_index(IX[:, n, :], MX[:, n, :], LG[:, n, :]))
            then(dve.tensor_copy(IXF[:], IX[:, :, 0:2]))
            dve.tensor_tensor(G12[:, 0, :], MX[:, :, 1], MX[:, :, 0], ALU.subtract).then_inc(S["lg_exp"], 1)
            dve.wait_ge(S["gate_exp"], 1)
            then(dve.tensor_scalar(G12[:, 2, :], G12[:, 1, :], 1.0, None, ALU.add))
            then(dve.reciprocal(G12[:, 2, :], G12[:, 2, :]))
            then(dve.tensor_tensor(G12[:, 3, :], G12[:, 1, :], G12[:, 2, :], ALU.mult))
            for n in range(NCH):
                then(dve.tensor_scalar(GG[:, 0, n, :], iota, IXF[:, n, 0:1], G12[:, 2, n:n + 1], ALU.is_equal, ALU.mult))
                then(dve.tensor_scalar(GG[:, 1, n, :], iota, IXF[:, n, 1:2], G12[:, 3, n:n + 1], ALU.is_equal, ALU.mult))
            dve.tensor_tensor(GG[:, 1], GG[:, 0], GG[:, 1], ALU.add).then_inc(S["lg_ready"], 1)

        @block.vector
        def _(dve):
            own = [0]

            def then(ins):
                own[0] += 1
                ins.then_inc(S["dve_own"], 1)
                dve.wait_ge(S["dve_own"], own[0])

            def log1p_steps(dst, y, s, s2, add):
                then(dve.tensor_scalar(s, y, 2.0, None, ALU.add))
                then(dve.reciprocal(s, s))
                then(dve.tensor_tensor(s, s, y, ALU.mult))
                then(dve.tensor_tensor(s2, s, s, ALU.mult))
                then(dve.tensor_scalar(dst, s2, LOG1P[0], None, ALU.mult))
                for c in LOG1P[1:]:
                    then(dve.scalar_tensor_tensor(dst, dst, c, s2, ALU.add, ALU.mult))
                then(dve.scalar_tensor_tensor(dst, dst, 1.0, s, ALU.add, ALU.mult))
                then(dve.scalar_tensor_tensor(dst, dst, 2.0, add, ALU.mult, ALU.add))

            def norm_apply(q):
                dve.wait_ge(S["rs_sqrt"], 2 * (q + 1))
                then(dve.reciprocal(RS[:], RS[:]))
                if q == 2 * L:
                    for k in range(KD):
                        dve.scalar_tensor_tensor(hT[:, k, :], xT[:, k, :], FN[:, k:k + 1], RS[:], ALU.mult, ALU.mult).then_inc(S["y_ready"], 1)
                    return
                l, w = q // 2, q % 2
                for k in range(KD):
                    dve.tensor_tensor(hT[:, k, :], xT[:, k, :], RS[:], ALU.mult).then_inc(S["h_mul"], 1)
                dve.wait_ge(S["h_mul"], KD * (q + 1))
                hs = hT[:, :, TP:T].rearrange("p k (b s) -> p k b s", s=NS)
                bc = lambda ap: ap.unsqueeze(3).broadcast_to([P, KD, NB, NS])
                then(dve.tensor_tensor(hs, hs, bc(AM[:, w, :, 1:G9]), ALU.mult))
                dve.tensor_tensor(hs, hs, bc(MOD[:, 3 * KD * w:3 * KD * w + KD, 1:G9]), ALU.add).then_inc(S["h_small"], 1)

            def residual(f, b, m, g0, add_wait):
                dve.wait_ge(S["w_used"], f)
                if add_wait is not None:
                    dve.wait_ge(S["x_ready"], add_wait)
                xm = xT[:, m, :] if isinstance(m, int) else xT[:, bass.ds(m, 1), :].rearrange("p a t -> p (a t)")
                gm = MOD[:, bass.ds(m + g0, 1), :].rearrange("p a t -> p (a t)")
                dve.scalar_tensor_tensor(xm[:, 0:TP], PM[b][:, :], gm[:, 0:1], xm[:, 0:TP], ALU.mult, ALU.add).then_inc(free_m[b], 1)
                tmp = TMP[:, b, :]
                dve.tensor_tensor(pv_s(tmp), pv_s(PS[b][:, 0:TS]), gm[:, 1:G9].unsqueeze(2).broadcast_to([P, NB, NS]), ALU.mult).then_inc(free_s[b], 1)
                return xm, tmp

            dve.memset(ONES[:], 1.0).then_inc(S["ones_ready"], 1)
            dve.memset(SM[:], 0.0).then_inc(S["ones_ready"], 1)
            then(dve.memset(ABt[:], 0.0))
            then(dve.memset(EPSC[:, 0:1], EPS))
            then(dve.memset(EPSC[:, 1:2], EPS * P))
            then(dve.memset(LG[:], 0.0))
            dve.wait_ge(S["consts"], 8 * 16)
            o = PC["lru_lambda"][0]
            lam = PA[:, :, o:o + 2]
            dve.scalar_tensor_tensor(LM[:, :, 0, :], lam, -1.0, lam, ALU.mult, ALU.min).then_inc(S["lam_abs"], 1)
            then(dve.tensor_scalar(LM[:, :, 2, :], lam, -1.0, 0.0, ALU.mult, ALU.max))
            dve.wait_ge(S["sp_exp"], 1)
            log1p_steps(LM[:, :, 5, :], LM[:, :, 1, :], LM[:, :, 3, :], LM[:, :, 4, :], LM[:, :, 2, :])
            then(dve.tensor_scalar(LM[:, :, 5, :], LM[:, :, 5, :], 2.0, None, ALU.mult))
            for a, nm in enumerate(("lru_b_a", "lru_b_i")):
                o = PC[nm][0]
                then(dve.tensor_scalar(LM[:, :, 6 + a, :], PA[:, :, o:o + 2], 0.5, None, ALU.mult))
            for l in range(L):
                dve.wait_ge(S["w_used"], FILL["ada", l] + F_ADA)
                then(dve.tensor_tensor(MOD[:], PB[4][:, 0:M_ADA * G9].rearrange("p (m g) -> p m g", g=G9),
                                       par("b_ada", l, 0, M_ADA).unsqueeze(2).broadcast_to([P, M_ADA, G9]), ALU.add))
                for w in range(2):
                    ins = dve.scalar_tensor_tensor(AM[:, w], MOD[:, KD * (3 * w + 1):KD * (3 * w + 2), :], 1.0,
                                                   par(f"norm{w + 1}", l, 0, KD).unsqueeze(2).broadcast_to([P, KD, G9]), ALU.add, ALU.mult)
                ins.then_inc(S["mod_done"], 1)
                dve.wait_ge(S["mod_done"], l + 1)
                norm_apply(2 * l)
                mixer_dve(dve, l, then, log1p_steps)
                f0 = FILL["out", l]
                base = X_DONE.get(2 * l, 0)
                with dve.Fori(0, 2) as j:
                    for s in range(4):
                        m = j * 4 + s
                        xm, tmp = residual(j * 4 + (f0 + s + 1), s % 2, m, 2 * KD, None)
                        dve.wait_ge(free_m[s % 2], j * 2 + (TILE["out", l] + s) // 2 + 1)
                        dve.wait_ge(free_s[s % 2], j * 2 + (TILE["out", l] + s) // 2 + 1)
                        dve.tensor_tensor(xm[:, TP:T], xm[:, TP:T], tmp, ALU.add).then_inc(S["x_ready"], 2)
                norm_apply(2 * l + 1)
                if l % 2 == 0:
                    f0, t0 = FILL["gu", l], TILE["gu", l]
                    with dve.Fori(0, FF // 2) as j:
                        for pr in range(2):
                            dve.wait_ge(S["w_used"], j * 4 + (f0 + 2 * pr + 2))
                            dve.wait_ge(free_s[0], j * 2 + (t0 // 2 + pr + 1))
                            row = PJ[:, bass.ds((j * 2 + pr) * T, T)]
                            dve.tensor_tensor(row[:, 0:TP], SQ[:, pr, 0:TP], PM[1][:, :], ALU.mult).then_inc(free_m[1], 1)
                            dve.tensor_tensor(row[:, TP:T], SQ[:, pr, TP:T], PS[1][:, 0:TS], ALU.mult).then_inc(free_s[1], 1)
                    f0, t0 = FILL["dn", l], TILE["dn", l]
                    with dve.Fori(0, KD // 2) as j:
                        for s in range(2):
                            m = j * 2 + s
                            xm, tmp = residual(j * 4 + (f0 + 2 * s + 2), s, m, 5 * KD, None)
                            dve.wait_ge(free_m[s], j + (t0 // 2 + 1))
                            dve.wait_ge(free_s[s], j + (t0 // 2 + 1))
                            dve.tensor_tensor(xm[:, TP:T], xm[:, TP:T], tmp, ALU.add).then_inc(S["x_ready"], 2)
                else:
                    router_dve(dve, l, then)
                    pair = 2 * FE + KD
                    f0, t0 = FILL["moe", l], TILE["moe", l]
                    dve.wait_ge(S["gb_ready"], NE)
                    with dve.Fori(0, NE // 2) as e2:
                        for e in range(2):
                            gb = QC[:, bass.ds(e2 * 2 + e, 1), :].rearrange("p a t -> p (a t)")
                            for i in range(FE):
                                f, t, g = f0 + e * pair + 2 * i, t0 + e * pair + 2 * i, e * FE + i
                                dve.wait_ge(free_m[0], e2 * pair + (t // 2 + 1))
                                dve.wait_ge(free_s[0], e2 * pair + (t // 2 + 1))
                                sg = SQ[:, i % 2, :]
                                dve.tensor_tensor(sg, sg, gb, ALU.mult).then_inc(S["sg_gated"], 1)
                                dve.wait_ge(S["sg_gated"], e2 * (2 * FE) + (g + 1))
                                dve.wait_ge(S["w_used"], e2 * (2 * pair) + (f + 2))
                                row = act_t[:, g, :]
                                dve.tensor_tensor(row[:, 0:TP], sg[:, 0:TP], PM[1][:, :], ALU.mult).then_inc(free_m[1], 1)
                                dve.tensor_tensor(row[:, TP:T], sg[:, TP:T], PS[1][:, 0:TS], ALU.mult).then_inc(free_s[1], 1)
                            for m in range(KD):
                                f, t = f0 + e * pair + 2 * FE + m, t0 + e * pair + 2 * FE + m
                                xm, tmp = residual(e2 * (2 * pair) + (f + 1), t % 2, m, 5 * KD, e2 * (4 * KD) + (48 + 2 * KD * e))
                                dve.wait_ge(free_m[t % 2], e2 * pair + (t // 2 + 1))
                                dve.wait_ge(free_s[t % 2], e2 * pair + (t // 2 + 1))
                                dve.tensor_tensor(xm[:, TP:T], xm[:, TP:T], tmp, ALU.add).then_inc(S["x_ready"], 2)
            norm_apply(2 * L)

        @block.gpsimd
        def _(pool):
            own = [0]

            def then(ins):
                own[0] += 1
                ins.then_inc(S["pool_own"], 1)
                pool.wait_ge(S["pool_own"], own[0])
            then(pool.memset(WL[:], 0.0))
            for l in range(L):
                for a, nm in enumerate(("lru_w_a", "lru_w_i")):
                    for b in range(4):
                        o = 64 * (b % 2)
                        pool.dma_start(WL[o:o + 64, l, a, b // 2, o:o + 64], io[nm][l, b]).then_inc(S["in_small"], 16)
            for l in range(L):
                if l > 0:
                    pool.wait_ge(S["out_states"], 16 * 7 * l)
                for dst, nm in ((SC[:], "st_a"), (SCQ[:], "st_q"), (ST[:], "st_l")):
                    pool.dma_start(dst, io[nm][l]).then_inc(S["states_in"], 16)
                for h2 in range(2):
                    pool.dma_start(SS[:, 4 * h2:4 * h2 + 4], io["st_d"][l, :, 4 * h2:4 * h2 + 4]).then_inc(S["states_in"], 16)
                pool.wait_ge(S["states_in"], 16 * 5 * (l + 1))
                if l > 0:
                    pool.wait_ge(S["x_ready"], X_DONE[2 * l])
                pads = pj[:, :, SO:CW].rearrange("p m (b c) -> p m b c", c=WQ - 1 + NS)[:, :, :, 0:WQ - 1]
                then(pool.memset(pj[:, :, 0:WQ - 1], 0.0))
                then(pool.memset(pads, 0.0))
                then(pool.tensor_copy(pads[:, LRU_X:LRU_X + 2], SCQ[:, 0:2]))
                then(pool.tensor_copy(pads[:, QKV:ZT], SCQ[:, 2:14]))
                for c in range(2):
                    then(pool.memset(UA[:, c, 0:WA - 1], 0.0))
                    then(pool.tensor_copy(UA[:, c, AO:CA].rearrange("p (b c) -> p b c", c=WA - 1 + NS)[:, :, 0:WA - 1], SC[:, c]))
                pool.sem_inc(S["pads_ready"], 1)
                pool.wait_ge(S["glu_ready"], 4 * (l + 1))
                for c in range(2):
                    then(pool.tensor_copy(NA[:, c], UA[:, c, AO:CA].rearrange("p (b c) -> p b c", c=WA - 1 + NS)[:, :, NS:]))
                pool.dma_start(io["n_a"][l], NA[:]).then_inc(S["out_states"], 16)
                pool.dma_start(io["n_ap"][l], UA[:, :, TP:AO]).then_inc(S["out_states"], 16)
                for i in range(14):
                    m = LRU_X + i if i < 2 else QKV + i - 2
                    pool.wait_ge(free_m[m % 2], (TILE["in", l] + m) // 2 + 1)
                    pool.wait_ge(free_s[m % 2], (TILE["in", l] + m) // 2 + 1)
                    then(pool.tensor_copy(NQ[:, i, 0, :], pj[:, m, TP:SO]))
                    then(pool.tensor_copy(NQ[:, i, 1:G9, :], pj[:, m, SO:CW].rearrange("p (b c) -> p b c", c=WQ - 1 + NS)[:, :, NS:]))
                pool.sem_inc(S["new_states"], 1)
                pool.dma_start(io["n_q"][l], NQ[:]).then_inc(S["out_states"], 16)
                pool.wait_ge(S["lru_new"], l + 1)
                pool.dma_start(io["n_l"][l], SN[:]).then_inc(S["out_states"], 16)
                for n in range(NCH):
                    tok, m, _ = chunk(n)
                    q = NCH * l + n
                    pool.wait_ge(S["eg_ready"], q + 1)
                    if q > 0:
                        pool.wait_ge(S["o_pe"], q)
                    pool.tensor_tensor(w4(2)[:, :, 0:m], QC[:, 0:H, tok], w4(3)[:, :, 0:m], ALU.mult).then_inc(S["qg_ready"], 1)
                pool.wait_ge(S["st_done"], H * 4 * (l + 1))
                pool.dma_start(io["n_dp"][l], SP_[:]).then_inc(S["out_states"], 16)
                pool.wait_ge(S["sm_upd"], H * NB * (l + 1))
                for h2 in range(2):
                    pool.dma_start(io["n_d"][l, :, 4 * h2:4 * h2 + 4], SS[:, 4 * h2:4 * h2 + 4]).then_inc(S["out_states"], 16)
            pool.wait_ge(S["out_states"], 16 * 7 * L)


def _constants(np):
    c = np.zeros((P, C_END), np.float32)
    i = np.arange(P)
    c[:, C_ID:C_ID + P] = np.eye(P)
    c[:, C_TRI:C_TRI + P] = i[:, None] <= i[None, :]
    t = np.arange(TS)
    same = (t[:, None] // NS) == (t[None, :] // NS)
    c[:TS, C_BTRI:C_BTRI + TS] = same & (t[:, None] <= t[None, :])
    c[:TS, C_BONE:C_BONE + TS] = same
    c[:TS, C_BM:C_BM + NB] = (t[:, None] // NS) == np.arange(NB)[None, :]
    c[:, C_IOTA:C_IOTA + NE] = np.arange(NE)
    for v in range(LEVELS):
        blk = i // (1 << v)
        c[:, C_LVL + v * P:C_LVL + (v + 1) * P] = (blk[:, None] % 2 == 0) & (blk[None, :] == blk[:, None] + 1)
    return c


def _tiles(np, w):
    *b, i, o = w.shape
    w = w.reshape(*b, i // P, P, o // P, P)
    n = len(b)
    return np.ascontiguousarray(np.moveaxis(w, (n + 2, n + 1, n), (n, n + 1, n + 2)))


def _layout(np, a):
    x = np.concatenate([a["x_prompt"][0], a["x_sample"].reshape(TS, D)], 0)
    feat = lambda v: np.moveaxis(v.reshape(*v.shape[:-1], -1, P), -1, 0)
    w_in = a["w_in"]
    parts = np.split(w_in, np.cumsum([256, 256, 1536, 512, H, H, 256]).tolist(), axis=-1)
    a_val, a_gate, qkv, z, b, aa, lx, lg = parts
    w24 = np.concatenate([a_val, a_gate, lx, lg, qkv, z], -1)
    wab = np.concatenate([b, aa], -1).reshape(L, KD, P, 2 * H).transpose(2, 0, 1, 3)
    params = np.zeros((P, L, PCOLS), np.float32)
    def put(name, v):
        o, w = PC[name]
        params[:, :, o:o + w] = v
    for name in ("b_ada", "norm1", "norm2", "conv_a_b", "ln_a_g", "ln_a_b", "conv_lru_b", "lru_b_a", "lru_b_i", "lru_lambda", "lru_norm", "gdn_norm"):
        put(name, feat(a[name]))
    for name in ("conv_a_w", "conv_qkv_w", "conv_lru_w"):
        put(name, feat(a[name]).transpose(0, 1, 3, 2).reshape(P, L, -1))
    put("a_log", np.broadcast_to(a["gdn_a_log"], (P, L, H)))
    put("dt_bias", np.broadcast_to(a["gdn_dt_bias"], (P, L, H)))
    gu = lambda g, u: np.stack([_tiles(np, g), _tiles(np, u)], -4)
    q = feat(np.concatenate([a["state_conv_lru"], a["state_conv_qkv"]], -1))
    dn = _tiles(np, a["ffn_wd"][0]).reshape(KD, P, 2, FE * P).transpose(0, 2, 1, 3)
    out = {
        "consts": _constants(np), "params": params,
        "cT": feat(np.concatenate([a["c_prompt"], a["c_sample"]], 0)).transpose(0, 2, 1),
        "x": feat(x).transpose(0, 2, 1), "wab": wab, "fnorm": feat(a["final_norm"]),
        "rw": a["router_w"][0].reshape(KD, P, NE).transpose(1, 0, 2), "rb": a["router_b"],
        "w_ada": _tiles(np, a["w_ada"]).reshape(L, M_ADA, P, KD * P), "w_in": _tiles(np, w24).reshape(L, M_IN, P, KD * P),
        "w_out": _tiles(np, a["w_out"]).reshape(L, KD, P, KD * P),
        "ffn_gu": gu(a["ffn_wg"][0], a["ffn_wu"][0]).reshape(F_GU, P, KD * P), "ffn_dn": dn.reshape(F_DN, P, SLOT),
        "moe_gu": gu(a["moe_wg"][0], a["moe_wu"][0]).reshape(NE, 2 * FE, P, KD * P),
        "moe_dn": _tiles(np, a["moe_wd"][0]).reshape(NE, KD, P, SLOT),
        "lru_w_a": a["lru_w_a"], "lru_w_i": a["lru_w_i"],
        "st_a": feat(a["state_conv_a"]).transpose(1, 0, 4, 2, 3), "st_q": q.transpose(1, 0, 4, 2, 3),
        "st_l": feat(a["state_lru"]).transpose(1, 0, 3, 2).reshape(L, P, 2 * NB),
        "st_d": a["state_delta"].transpose(0, 3, 1, 2, 4),
    }
    return {k: np.ascontiguousarray(v) for k, v in out.items()}


_OUT = {"y": (P, KD, T), "n_a": (L, P, 2, NB, WA - 1), "n_ap": (L, P, 2, WA - 1), "n_q": (L, P, 14, G9, WQ - 1),
        "n_l": (L, P, 2 * G9), "n_dp": (L, P, H, P), "n_d": (L, P, NB, H, P)}


def kernel(**inputs):
    import numpy as np
    from concourse import bacc
    from concourse.bass_utils import run_bass_kernel_spmd

    arrays = _layout(np, {k: np.asarray(v) for k, v in inputs.items()})
    nc = bacc.Bacc("TRN2", target_bir_lowering=False, num_devices=1)
    io = {k: nc.dram_tensor("in_" + k, v.shape, F32, kind="ExternalInput").ap() for k, v in arrays.items()}
    io.update({k: nc.dram_tensor("out_" + k, s, F32, kind="ExternalOutput").ap() for k, s in _OUT.items()})
    build(nc, io)
    r = run_bass_kernel_spmd(nc, [{"in_" + k: v for k, v in arrays.items()}], core_ids=[0]).results[0]
    o = {k: np.asarray(r["out_" + k]).reshape(s) for k, s in _OUT.items()}
    y = o["y"].transpose(2, 1, 0).reshape(T, D)
    unfeat = lambda v: v.reshape(*v.shape[:-2], -1)
    a_s = unfeat(o["n_a"].transpose(0, 3, 4, 2, 1))
    a_p = unfeat(o["n_ap"].transpose(0, 3, 2, 1))[:, None]
    q = unfeat(o["n_q"].transpose(0, 3, 4, 2, 1))
    lr = unfeat(o["n_l"].reshape(L, P, 2, G9).transpose(0, 3, 2, 1))
    c = np.ascontiguousarray
    return tuple(c(v) for v in (
        y[None, :TP], y[TP:].reshape(NB, NS, D), a_p, q[:, 0:1, :, 256:], o["n_dp"].transpose(0, 2, 1, 3)[:, None],
        q[:, 0:1, :, :256], lr[:, 0:1], a_s, q[:, 1:, :, 256:], o["n_d"].transpose(0, 2, 3, 1, 4), q[:, 1:, :, :256], lr[:, 1:]))
```

```python
from contextlib import ExitStack

import concourse.bass as bass
from concourse import mybir

F32 = mybir.dt.float32
U32 = mybir.dt.uint32
F32R = mybir.dt.float32r
ALU = mybir.AluOpType
ACT = mybir.ActivationFunctionType
AX_X = mybir.AxisListType.X

P = 128
L = 2
TP = 512
NB = 8
NS = 8
TS = NB * NS
T = TP + TS
HN = T // 2
HP = TP - HN
G9 = NB + 1
D = 1024
KD = D // P
M_ADA = 6 * KD
M_IN = 24
FF = 22
NE = 8
FE = 11
H = 4
WA = 31
WQ = 4
EPS = 1e-6
RING = 4
SLOT = FE * P
WK = KD * P
RING3 = 3
G3 = 2 * FE + KD
GX = 3 * FE
AHEAD = 2
B_MOE = 2 * G3 + AHEAD
CAP = 256
ROUNDS = 3
NPASS = ROUNDS * NE
CW = WQ - 1 + TP + NB * (WQ - 1 + NS)
SO = WQ - 1 + TP
CA = WA - 1 + TP + NB * (WA - 1 + NS)
AO = WA - 1 + TP
A_VAL, A_GATE, LRU_X, LRU_G, QKV, ZT = 0, 2, 4, 6, 8, 20
LEVELS = 7
SLEVELS = 3
NCH = 5
C_ID, C_TRI, C_BTRI, C_BONE, C_BM, C_IOTA, C_LVL = 0, 128, 256, 320, 384, 392, 400
C_SLOT = C_LVL + LEVELS * P
C_END = C_SLOT + CAP + 2
PC = {}
_n = 0
for _name, _w in (("b_ada", M_ADA), ("norm1", KD), ("norm2", KD), ("conv_a_w", 2 * WA), ("conv_qkv_w", 12 * WQ),
                  ("conv_lru_w", 2 * WQ), ("conv_a_b", 2), ("ln_a_g", 2), ("ln_a_b", 2), ("conv_lru_b", 2),
                  ("lru_b_a", 2), ("lru_b_i", 2), ("lru_lambda", 2), ("lru_norm", 2), ("gdn_norm", 1),
                  ("a_log", H), ("dt_bias", H)):
    PC[_name] = (_n, _w)
    _n += _w
PCOLS = _n

ADA_FIRST = 2 * KD
ADA_IN, ADA_OUT = (2, 1), (0, 1)
ADA_BATCH = (0, ADA_FIRST, ADA_FIRST + ADA_IN[0] * M_IN, L * M_ADA - ADA_OUT[1] * KD, L * M_ADA)
PER = {(s, l): 1 + n for s, v in (("in", ADA_IN), ("out", ADA_OUT)) for l, n in enumerate(v)}
ADA0 = {("in", 0): ADA_BATCH[1], ("in", 1): ADA_BATCH[2], ("out", 1): ADA_BATCH[3]}
FILL, TILE = {}, {}
_f = _t = 0
for _l in range(L):
    _stages = [("ada", ADA_FIRST, 0)] if _l == 0 else []
    _stages += [("in", PER["in", _l] * M_IN, M_IN), ("out", PER["out", _l] * KD, KD)]
    _stages += [("ffn", 0, 2 * G3)] if _l % 2 == 0 else []
    for _s, _nf, _nt in _stages:
        FILL[_s, _l], TILE[_s, _l] = _f, _t
        _f += _nf
        _t += _nt
LOG1P = [1.0 / (2 * i + 1) for i in range(9, 0, -1)]


def build(nc, io):
    ctx = ExitStack()
    with ctx:
        sb = lambda name, shape, dt=F32: ctx.enter_context(nc.sbuf_tensor(name, shape, dt))
        sem = lambda name: ctx.enter_context(nc.semaphore(name))

        xT = sb("xT", [P, KD, T])
        hT = sb("hT", [P, KD, T])
        ring_f = sb("ring", [P, RING3 * SLOT])
        RS = sb("RS", [P, T])
        EPSC = sb("EPSC", [P, 2])
        SQ = sb("SQ", [P, 2, T])
        CO = sb("CO", [P, C_END])
        ONES = sb("ONES", [P, P])
        PA = sb("PA", [P, L, PCOLS])
        CT = sb("CT", [P, KD, G9])
        MOD = sb("MOD", [P, L, M_ADA, G9])
        AM = sb("AM", [P, 2 * L, KD, G9])
        TMP = sb("TMP", [P, 2, TS])
        WAB = sb("WAB", [P, L, KD, 2 * H])
        FN = sb("FN", [P, KD])
        RW = sb("RW", [P, KD, NE])
        RB = sb("RB", [1, NE])
        ST = sb("ST", [P, 2 * NB])
        SN = sb("SN", [P, 2 * G9])
        ABt = sb("ABt", [P, NCH, 2 * H])
        SM = sb("SM", [P, 16, NCH * H])
        LM = sb("LM", [P, L, 8, 2])
        LG = sb("LG", [P, NCH, NE])
        MX = sb("MX", [P, NCH, NE])
        IX = sb("IX", [P, NCH, NE], U32)
        IXF = sb("IXF", [P, NCH, 2])
        GG = sb("GG", [P, 2, NCH, NE])
        G12 = sb("G12", [P, 4, NCH])
        ELS = sb("ELS", [P, NB, H])
        GSEL = sb("GSEL", [TS, NB, H])
        MK = sb("MK", [P, NCH, NE])
        PF = sb("PF", [P, 2, NCH, NE])
        OV = sb("OV", [P, 4])
        NR = sb("NR", [1, 1], U32)
        PG = sb("PG", [P, NCH, 2, NPASS + 1])
        GS = sb("GS", [P, 2])

        with ExitStack() as mixers:
            mb_ = lambda name, shape: mixers.enter_context(nc.sbuf_tensor(name, shape, F32))
            PJ = mb_("PJ", [P, M_IN * CW])
            UA = mb_("UA", [P, 2, CA])
            QC = mb_("QC", [P, 12, T])
            XA = mb_("XA", [P, 2, T])
            XL = mb_("XL", [P, 2, T])
            SP_ = mb_("SP_", [P, H, P])
            SS = mb_("SS", [P, NB, H, P])
            SC = mb_("SC", [P, 2, NB, WA - 1])
            SCQ = mb_("SCQ", [P, 14, NB, WQ - 1])
            NA = mb_("NA", [P, 2, NB, WA - 1])
            NQ = mb_("NQ", [P, 14, G9, WQ - 1])
            MROW = mb_("MROW", [G9, 2, P])
            WL = mb_("WL", [P, 2, 2, P])
        with ExitStack() as dense:
            fb_ = lambda name, shape: dense.enter_context(nc.sbuf_tensor(name, shape, F32R))
            HH, HL = fb_("HH", [P, KD, T]), fb_("HL", [P, KD, T])
            AH, AL = fb_("AH", [P, FE, T]), fb_("AL", [P, FE, T])
            VH, VL = fb_("VH", [P, RING3, SLOT]), fb_("VL", [P, RING3, SLOT])
        HTH, HTL = sb("HTH", [P, NCH, D], F32R), sb("HTL", [P, NCH, D], F32R)
        XH, XLo = sb("XH", [P, KD, CAP], F32R), sb("XLo", [P, KD, CAP], F32R)
        BH, BL = sb("BH", [P, FE, CAP], F32R), sb("BL", [P, FE, CAP], F32R)
        YH, YL = sb("YH", [P, 2, D], F32R), sb("YL", [P, 2, D], F32R)
        SG_ = sb("SG_", [P, NCH, CAP], F32R)
        SGT = sb("SGT", [P, 2, T], F32R)
        UH, UL = sb("UH", [P, RING3, WK], F32R), sb("UL", [P, RING3, WK], F32R)
        scratch = nc.dram_tensor("gate_rows", (2 * (NPASS + 1), T), F32, kind="Internal").ap()

        PB = [ctx.enter_context(nc.psum_tensor(f"PB{i}", [P, 512], F32)) for i in range(8)]
        ROW = [PB[7 - b][0:G9, 0:P] for b in range(2)]
        PM, PS = [PB[0], PB[2]], [PB[1], PB[3]]

        pj = PJ[:, :].rearrange("p (m c) -> p m c", c=CW)
        ring = ring_f[:, 0:RING * WK].rearrange("p (s c) -> p s c", s=RING)
        raw3 = lambda s, w: ring_f[:, s * SLOT:s * SLOT + w]
        hf = hT[:].rearrange("p k t -> p (k t)")
        AF = hf[:, 0:2 * T].rearrange("p (b t) -> p b t", b=2)
        BR = hf[:, 2 * T:4 * T].rearrange("p (a t) -> p a t", a=2)
        JUNK = hf[:, 4 * T:5 * T]
        ROWS = hf[0:2 * (NPASS + 1), 5 * T:6 * T]
        f32 = lambda ap: ap.bitcast(F32)
        work0 = QKV * CW
        def wk(i, n=1):
            return PJ[:, work0 + i * 512:work0 + (i + n) * 512]
        w4 = lambda i: wk(i).rearrange("p (h c) -> p h c", h=H)
        lw = lambda i: PJ[:, work0 + i * 2 * T:work0 + (i + 1) * 2 * T].rearrange("p (c t) -> p c t", c=2)
        ident, tri = CO[:, C_ID:C_ID + P], CO[:, C_TRI:C_TRI + P]
        btri, bone = CO[0:TS, C_BTRI:C_BTRI + TS], CO[0:TS, C_BONE:C_BONE + TS]
        bm, iota = CO[0:TS, C_BM:C_BM + NB], CO[:, C_IOTA:C_IOTA + NE]
        lvl = lambda v, n: CO[0:n, C_LVL + v * P:C_LVL + v * P + n]
        par = lambda name, l, i=0, w=1: PA[:, l, PC[name][0] + i:PC[name][0] + i + w]
        pv_s = lambda ap: ap.rearrange("p (b s) -> p b s", s=NS)

        names = """row_out mod_pe ab_gates ab_pe act_own af_ready ah_ready al_ready bf_ready bh_ready bl_ready br_landed c_act
            cnt_pe consts conv_a conv_l conv_q dd_exp dd_min dd_ready dve_own eg_ready free_m0 free_m1
            free_s0 free_s1 gat_pe gate_exp gc_pe gelu_ready glu_ready gt_copied gt_pe h_main h_mul h_small
            hh_ready hl_ready ht_pe hth_ready htl_ready in_small ks_copied ks_pe ks_tr l2_done l2_pe l2_sq
            l2_sqrt lam_abs lg_exp lg_pe ln_done ln_mean ln_sq ln_sub ln_sum ln_used lru_g_pe lru_new
            lru_scan lru_sqrt lru_t lru_tz mat_pe mk_ready mod_done moe_done new_states nr_ready o_copied
            o_pe on_pe on_scaled on_sq on_sqrt ones_ready out_done out_states p_copied p_pe pads_ready
            pg_ready pool_own q_silu qg_ready r_ready rhs_ready rows_out rs_sqrt s_ready sc_pe silu_z
            sm_mask sm_pe sm_upd small_exp small_exp2 small_ready small_tanh sp_exp sp_zero sq_ready
            sq_used st_done st_own st_pe st_ready states_in t_done t_pe tr_evac tr_pe um_ready vn_copied
            vn_pe w3_used w_used wh_ready wl_ready x_ready y_ready ya_ready yb_ready yc_pe yc_ready yc_sq
            yc_sqrt yh_ready yl_ready""".split()
        S = {n: sem(n) for n in names}
        landed = [sem(f"landed{i}") for i in range(RING)]
        landed3 = [sem(f"landed3_{i}") for i in range(RING3)]
        fb = [sem(f"bank_free{i}") for i in range(4)]
        free_m, free_s = [S["free_m0"], S["free_m1"]], [S["free_s0"], S["free_s1"]]
        block = ctx.enter_context(nc.Block())

        def slot_of(f0, s):
            return (f0 + s) % RING

        def wait_landed(eng, f0, s, j):
            eng.wait_ge(landed[(f0 + s) % RING], (j + ((f0 + s) // RING + 1)) * 16)

        @block.sync
        def _(sp):
            first = (("consts", CO), ("params", PA), ("cT", CT), ("x", xT), ("wab", WAB), ("fnorm", FN), ("rw", RW), ("rb", RB))
            for name, dst in first:
                sp.dma_start(dst[:], io[name]).then_inc(S["consts"], 16)

            def stream(src, f0, nf, rnd, guard=True):
                with sp.Fori(0, nf // rnd) as j:
                    for s in range(rnd):
                        if guard:
                            sp.wait_ge(S["w_used"], j * rnd + (f0 + s - RING + 1))
                        sp.dma_start(ring[:, slot_of(f0, s), :], src(j, s)).then_inc(landed[slot_of(f0, s)], 16)
            for l in range(L):
                if l == 0:
                    stream(lambda j, s: io["w_ada"][s], 0, RING, RING, guard=False)
                    stream(lambda j, s: io["w_ada"][j * RING + (RING + s)], RING, ADA_FIRST - RING, RING)
                for stage, nt in (("in", M_IN), ("out", KD)):
                    per = PER[stage, l]
                    def source(j, s):
                        if s % per == per - 1:
                            return io["w_" + stage][l, j * 4 + s // per]
                        return io["w_ada"][j * (4 * (per - 1)) + (ADA0[stage, l] + s // per * (per - 1) + s % per)]
                    stream(source, FILL[stage, l], per * nt, 4 * per)
                def fill3(src, w, s, used):
                    if used is not None:
                        sp.wait_ge(S["wl_ready"], used)
                    sp.dma_start(raw3(s % RING3, w), src).then_inc(landed3[s % RING3], 16)

                sp.wait_ge(S["w_used"], FILL["out", l] + PER["out", l] * KD)
                if l % 2 == 0:
                    for hv in range(2):
                        for i in range(G3):
                            g = hv * G3 + i
                            src, w = (io["ffn_gu"][hv * 2 * FE + i], WK) if i < 2 * FE else (io["ffn_dn"][hv, i - 2 * FE], SLOT)
                            fill3(src, w, g, g - 2 if g > 2 else None)
                    for i in range(AHEAD):
                        fill3(io["ffn_gu"][i], WK, 2 * G3 + i, 2 * G3 + i - 2)
                    sp.wait_ge(S["wl_ready"], B_MOE)
                else:
                    sp.wait_ge(S["nr_ready"], 1)
                    rounds = sp.value_load(NR[0:1, 0:1], min_val=1, max_val=ROUNDS)
                    with sp.Fori(0, rounds) as rd:
                        with sp.Fori(0, NE) as e:
                            for i in range(GX):
                                src = io["moe_gu"][e, i] if i < 2 * FE else io["moe_dn"][e, i - 2 * FE]
                                fill3(src, WK, B_MOE + i, rd * (NE * GX) + e * GX + (B_MOE + i - 2))
                    for i in range(AHEAD):
                        sp.wait_ge(S["wl_ready"], rounds * (NE * GX) + (B_MOE + i - 2))
                        sp.dma_start(raw3((B_MOE + i) % RING3, WK), io["moe_gu"][0, i]).then_inc(landed3[(B_MOE + i) % RING3], 16)
            sp.wait_ge(S["y_ready"], KD)
            sp.dma_start(io["y"], hT[:]).then_inc(S["out_done"], 16)
            sp.wait_ge(S["out_done"], 16)

        def chunk(n):
            return (slice(n * P, n * P + P), P, LEVELS) if n < 4 else (slice(TP, T), TS, SLEVELS)

        BANK_P, BANK_T = (6, 4), (7, 0)
        pair = lambda ap: ap.rearrange("p (a h c) -> p a h c", a=2, h=2)
        tg = lambda g: pair(wk(9 + g))
        inv_t = lambda hh: tg(hh // 2)[:, 0, hh % 2, :]
        inv_tt = lambda hh: tg(hh // 2)[:, 1, hh % 2, :]

        LVL_ALL = [(n, v) for n in range(NCH) for v in range(chunk(n)[2])]

        def ada_mms(pe, slot, b):
            for k in range(KD):
                end = pe.matmul(ROW[b], CT[:, k, :], ring[:, slot, k * P:(k + 1) * P], start=(k == 0), stop=(k == KD - 1))
            end.then_inc(S["w_used"], 1)

        def ada_turn(pe, b, done, col):
            pe.wait_ge(S["row_out"], done)
            pe.matmul(PB[4][:, col], MROW[:, b, :], ident[0:G9, 0:G9], start=True, stop=True).then_inc(S["mod_pe"], 1)

        def mixer_pe(pe, l):
            mm = pe.matmul
            t1 = TILE["in", l] + M_IN
            for b in range(2):
                pe.wait_ge(free_m[b], t1 // 2)
                pe.wait_ge(free_s[b], t1 // 2)
            for r in range(2):
                for c in range(2):
                    if r == 0:
                        pe.wait_ge(S["conv_a"], 2 * l + c + 1)
                        src = XA[:, c, :]
                    else:
                        pe.wait_ge(S["ln_sq"], 2 * l + c + 1)
                        src = SQ[:, c, :]
                    mm(PB[2 * r][:, 0:HN], ONES[:], src[:, 0:HN], start=(c == 0), stop=(c == 1))
                    end = mm(PB[2 * r + 1][:, 0:HN], ONES[:], src[:, HN:T], start=(c == 0), stop=(c == 1))
                end.then_inc(S["ln_sum"], 1)
            pe.wait_ge(S["small_ready"], 4 * l + 2)
            g = SM[:, 3, :]
            mm(PB[7][:, 64:80], tri, g[:, 0:16], start=True, stop=True)
            mm(PB[7][0:TS, 80:84], btri, g[0:TS, 16:20], start=True, stop=True)
            mm(PB[7][:, 84:100], ONES[:], g[:, 0:16], start=True, stop=True)
            mm(PB[7][0:TS, 100:104], bone, g[0:TS, 16:20], start=True, stop=True)
            mm(PB[7][:, 104:136], ONES[0:TS, :], GSEL[:].rearrange("p b h -> p (b h)"), start=True, stop=True).then_inc(S["gc_pe"], 1)
            pe.wait_ge(S["conv_l"], 2 * (l + 1))
            pe.wait_ge(S["in_small"], 16 * 8 * (l + 1))
            for c in range(2):
                for a in range(2):
                    if 2 * c + a > 0:
                        pe.wait_ge(S["lru_t"], 4 * l + 2 * c + a)
                    mm(PB[5][:, 0:HN], WL[:, a, c, :], XL[:, c, 0:HN], start=True, stop=True)
                    mm(PB[6][:, 0:HN], WL[:, a, c, :], XL[:, c, HN:T], start=True, stop=True).then_inc(S["lru_g_pe"], 1)
            for c in range(2):
                pe.wait_ge(S["yc_sq"], 2 * l + c + 1)
                mm(PB[5][:, 0:HN], ONES[:], SQ[:, c, 0:HN], start=(c == 0), stop=(c == 1))
                end = mm(PB[6][:, 0:HN], ONES[:], SQ[:, c, HN:T], start=(c == 0), stop=(c == 1))
            end.then_inc(S["yc_pe"], 1)
            for i in range(2 * H):
                pe.wait_ge(S["l2_sq"], 8 * l + i + 1)
                mm(PM[i % 2][:, 0:HN], ONES[:], SQ[:, i % 2, 0:HN], start=True, stop=True)
                mm(PS[i % 2][:, 0:HN], ONES[:], SQ[:, i % 2, HN:T], start=True, stop=True).then_inc(S["l2_pe"], 1)
            pe.wait_ge(S["mod_done"], l + 2)
            pe.wait_ge(S["l2_done"], 8 * (l + 1))
            pe.wait_ge(S["yc_sqrt"], l + 1)
            for n in range(NCH):
                tok, m, levels = chunk(n)
                q = NCH * l + n
                b4 = lambda i, rows=P, w=P: PB[i][0:rows, 0:H * w].rearrange("p (h c) -> p h c", h=H)
                kT = lambda hh: QC[:, H + hh, tok]
                qT = lambda hh: QC[:, hh, tok]
                pe.wait_ge(S["q_silu"], 12 * (l + 1))
                if n > 0:
                    pe.wait_ge(S["st_done"], H * 4 * l + H * n)
                    pe.wait_ge(S["o_copied"], q)
                for hh in range(H):
                    pe.transpose(b4(0, m)[:, hh, :], kT(hh), ident)
                for hh in range(H):
                    end = pe.transpose(b4(1, m)[:, hh, :], QC[:, 2 * H + hh, tok], ident)
                end.then_inc(S["tr_pe"], 1)
                for hh in range(H):
                    mm(b4(2, m, m)[:, hh, :], kT(hh), kT(hh), start=True, stop=True)
                    mm(b4(3, m, m)[:, hh, :], kT(hh), qT(hh), start=True, stop=True)
                pe.wait_ge(S["rhs_ready"], q + 1)
                mm(PB[4][:, 0:H * m], ONES[0:m, :], w4(7)[0:m, :, 0:m], start=True, stop=True)
                mm(PB[5][0:m, 0:H * m], ONES[0:m, 0:m], w4(8)[0:m, :, 0:m], start=True, stop=True).then_inc(S["mat_pe"], 1)
                for v in range(levels):
                    z = sum(chunk(i)[2] for i in range(n)) + v + len(LVL_ALL) * l
                    pe.wait_ge(S["um_ready"], z + 1)
                    if v == 0:
                        pe.wait_ge(S["tr_evac"], 2 * (q + 1))
                    um = w4(7 + v % 2)
                    for g in range(2):
                        if v > 0:
                            pe.wait_ge(S["t_done"], 2 * z + g - 1)
                        for hh in (2 * g, 2 * g + 1):
                            end = mm(PB[BANK_P[g]][0:m, hh % 2 * P:hh % 2 * P + m], um[0:m, hh, 0:m],
                                     ident[0:m, 0:m] if v == 0 else inv_t(hh)[0:m, 0:m], start=True, stop=True)
                        end.then_inc(S["p_pe"], 1)
                    if v == 0:
                        continue
                    for g in range(2):
                        pe.wait_ge(S["p_copied"], 2 * (z - q) + g - 1)
                        out = pair(PB[BANK_T[g]])
                        for hh in (2 * g, 2 * g + 1):
                            if v < levels - 1:
                                mm(out[0:m, 0, hh % 2, 0:m], inv_tt(hh)[0:m, 0:m], w4(11)[0:m, hh, 0:m], start=True, stop=True)
                            end = mm(out[0:m, 1, hh % 2, 0:m], w4(11)[0:m, hh, 0:m], inv_tt(hh)[0:m, 0:m], start=True, stop=True)
                        end.then_inc(S["t_pe"], 1)
                z1 = sum(chunk(i)[2] for i in range(n + 1)) + len(LVL_ALL) * l
                pe.wait_ge(S["t_done"], 2 * z1)
                pe.wait_ge(S["dd_ready"], q + 1)
                if n < 4:
                    if n == 0:
                        pe.wait_ge(S["sp_zero"], l + 1)
                    for hh in range(H):
                        end = mm(b4(1, m)[:, hh, :], kT(hh), SP_[:, hh, :], start=True, stop=True)
                    end.then_inc(S["ks_pe"], 1)
                    kb = 1
                else:
                    pe.wait_ge(S["states_in"], 16 * 5 * (l + 1))
                    for hh in range(H):
                        for b in range(NB):
                            end = mm(b4(1, P, m)[:, hh, b * NS:(b + 1) * NS], SS[:, b, hh, :], QC[:, H + hh, TP + b * NS:TP + (b + 1) * NS],
                                     start=True, stop=True)
                    end.then_inc(S["ks_pe"], 1)
                    pe.wait_ge(S["ks_copied"], l + 1)
                    for hh in range(H):
                        end = pe.transpose(b4(5, m)[:, hh, :], w4(11)[:, hh, 0:m], ident)
                    end.then_inc(S["ks_tr"], 1)
                pe.wait_ge(S["r_ready"], q + 1)
                for hh in range(H):
                    end = mm(b4(2, m)[:, hh, :], inv_tt(hh)[0:m, 0:m], w4(12)[0:m, hh, :], start=True, stop=True)
                end.then_inc(S["vn_pe"], 1)
                pe.wait_ge(S["vn_copied"], q + 1)
                pe.wait_ge(S["qg_ready"], q + 1)
                for hh in range(H):
                    o = b4(3, P, m)[:, hh, :]
                    end = mm(o, w4(13)[0:m, hh, :], w4(6)[0:m, hh, 0:m], start=True, stop=False, skip_group_check=True)
                    if n < 4:
                        end = mm(o, SP_[:, hh, :], w4(2)[:, hh, 0:m], start=False, stop=True, skip_group_check=True)
                    else:
                        for b in range(NB):
                            end = mm(o[:, b * NS:(b + 1) * NS], SS[:, b, hh, :], w4(2)[:, hh, b * NS:(b + 1) * NS],
                                     start=False, stop=True, skip_group_check=True)
                end.then_inc(S["o_pe"], 1)
                if n < 4:
                    for hh in range(H):
                        end = mm(b4(4)[:, hh, :], w4(0)[:, hh, :], w4(13)[:, hh, :], start=True, stop=True)
                    end.then_inc(S["st_pe"], 1)
                else:
                    for b in range(NB):
                        pe.wait_ge(S["sm_mask"], NB * l + b + 1)
                        if b >= 2:
                            pe.wait_ge(S["sm_upd"], H * (NB * l + b - 1))
                        for hh in range(H):
                            end = mm(b4(6 + b % 2)[:, hh, :], w4(7 + b % 2)[0:TS, hh, :], w4(13)[0:TS, hh, :], start=True, stop=True)
                        end.then_inc(S["sm_pe"], 1)
            for hh in range(H):
                pe.wait_ge(S["on_sq"], H * l + hh + 1)
                mm(PM[hh % 2][:, 0:HN], ONES[:], SQ[:, hh % 2, 0:HN], start=True, stop=True)
                mm(PS[hh % 2][:, 0:HN], ONES[:], SQ[:, hh % 2, HN:T], start=True, stop=True).then_inc(S["on_pe"], 1)
            pe.wait_ge(S["on_sqrt"], 2 * H * (l + 1))

        def three(pe, out, a, b, first, last):
            pe.matmul(out, a[0], b[0], start=first, stop=False)
            pe.matmul(out, a[0], b[1], start=False, stop=False)
            return pe.matmul(out, a[1], b[0], start=False, stop=last)

        def ffn_pe(pe, l):
            t0 = TILE["ffn", l]
            with pe.Fori(0, 2) as hv:
                for i in range(G3):
                    b, s, t = i % 2, i % RING3, t0 + i
                    pe.wait_ge(S["wl_ready"], hv * G3 + (i + 1))
                    pe.wait_ge(free_m[b], hv * (G3 // 2) + t // 2)
                    pe.wait_ge(free_s[b], hv * (G3 // 2) + t // 2)
                    gu = i < 2 * FE
                    nk, ah, al = (KD, HH, HL) if gu else (FE, AH, AL)
                    for k in range(nk):
                        if gu and i == 0:
                            pe.wait_ge(S["hl_ready"], k + 1)
                        if i == 2 * FE:
                            pe.wait_ge(S["al_ready"], hv * FE + (k + 1))
                        w = [v[:, s, k * P:(k + 1) * P] for v in (VH, VL)]
                        for c, bank in ((slice(0, HN), PM[b]), (slice(HN, T), PS[b])):
                            end = three(pe, bank[:, 0:HN], w, (ah[:, k, c], al[:, k, c]), k == 0, k == nk - 1)
                    end.then_inc(S["w3_used"], 1)
            pe.wait_ge(S["wl_ready"], B_MOE)
            pe.wait_ge(S["w3_used"], 2 * G3)
            pe.sem_inc(S["w3_used"], AHEAD)

        def router_pe(pe, l):
            mm = pe.matmul
            for n in range(NCH):
                tok = slice(n * P, min((n + 1) * P, T))
                m = tok.stop - tok.start
                for k in range(KD):
                    mm(PB[4][0:m, n * NE:(n + 1) * NE], hT[:, k, tok], RW[:, k, :], start=(k == 0), stop=False)
                end = mm(PB[4][0:m, n * NE:(n + 1) * NE], ONES[0:1, 0:m], RB[:], start=False, stop=True)
            end.then_inc(S["lg_pe"], 1)
            for n in range(NCH):
                tok = slice(n * P, min((n + 1) * P, T))
                m = tok.stop - tok.start
                if n > 1:
                    pe.wait_ge(S["htl_ready"], 2 * (n - 1))
                for k in range(KD):
                    bank = PB[2 * (n % 2) + k // 4]
                    end = pe.transpose(bank[0:m, (k % 4) * P:(k % 4 + 1) * P], hT[:, k, tok], ident)
                end.then_inc(S["ht_pe"], 1)
            pe.wait_ge(S["mk_ready"], 1)
            for n in range(NCH):
                for j in range(n + 1):
                    mm(PB[5][:, n * NE:(n + 1) * NE], tri if j == n else ONES[:], MK[:, j, :], start=(j == 0), stop=(j == n))
                for j in range(n - n % 2, n + 1):
                    mm(PB[5][:, (5 + n) * NE:(6 + n) * NE], tri if j == n else ONES[:], MK[:, j, :], start=(j == n - n % 2), stop=(j == n))
            for j in range(NCH):
                end = mm(PB[5][:, 80:88], ONES[:], MK[:, j, :], start=(j == 0), stop=(j == NCH - 1))
            end.then_inc(S["cnt_pe"], 1)
            pe.wait_ge(S["pg_ready"], 1)
            for n in range(NCH):
                m = min((n + 1) * P, T) - n * P
                w = 2 * (NPASS + 1)
                out = PB[6][0:w, n * P:n * P + m] if n < 4 else PB[7][0:w, 0:m]
                end = pe.transpose(out, PG[0:m, n].rearrange("p a c -> p (a c)"), ident[0:m, 0:m])
            end.then_inc(S["gt_pe"], 1)

        def bank_uses():
            n, uses = [0] * 4, {}
            def use(key, b):
                uses[key] = (b, n[b])
                n[b] += 1
            for i in range(2 * FE):
                use(("gu", i), i % 4)
            for k in range(KD):
                use(("hi", k), k % 2)
                use(("lo", k), 2 + k % 2)
            for m in range(KD):
                use(("sa", m), 2 * (m % 2))
                use(("sb", m), 2 * (m % 2) + 1)
            return uses, n
        USE, USES = bank_uses()
        FIRST = [KD // 2] * 4

        def gather_pe(pe, p, first=False):
            for k in range(KD):
                for part, src in (("hi", HTH), ("lo", HTL)):
                    b, u = USE[part, k]
                    if not first:
                        pe.wait_ge(fb[b], p * USES[b] + (FIRST[b] + u))
                    elif k > 1:
                        pe.wait_ge(fb[b], k // 2)
                    for n in range(NCH):
                        end = pe.matmul(PB[b][:, 0:CAP], src[:, n, k * P:(k + 1) * P], SG_[:, n, :], start=(n == 0), stop=(n == NCH - 1))
                    end.then_inc(S["gat_pe"], 1)

        def gather_done(pe, p, k):
            for b in (k % 2, 2 + k % 2):
                pe.wait_ge(fb[b], p * USES[b] + (FIRST[b] - KD // 2 + k // 2 + 1))

        def moe_pe(pe, l):
            pe.wait_ge(S["hth_ready"], 2 * NCH)
            pe.wait_ge(S["htl_ready"], 2 * NCH)
            pe.wait_ge(S["nr_ready"], 1)
            rounds = pe.value_load(NR[0:1, 0:1], min_val=1, max_val=ROUNDS)
            pe.wait_ge(S["s_ready"], 1)
            gather_pe(pe, 0, first=True)
            with pe.Fori(0, rounds) as rd:
                with pe.Fori(0, NE) as e:
                    p = pe.snap(rd * NE + e)
                    for i in range(GX):
                        s = (B_MOE + i) % RING3
                        pe.wait_ge(S["wl_ready"], p * GX + (B_MOE + i + 1))
                        w = (UH[:, s, :], UL[:, s, :])
                        if i < 2 * FE:
                            b, u = USE["gu", i]
                            pe.wait_ge(fb[b], p * USES[b] + (FIRST[b] + u))
                            for k in range(KD):
                                if i == 0:
                                    gather_done(pe, p, k)
                                wk_ = [v[:, k * P:(k + 1) * P] for v in w]
                                end = three(pe, PB[b][:, 0:CAP], wk_, (XH[:, k, :], XLo[:, k, :]), k == 0, k == KD - 1)
                        else:
                            kk = i - 2 * FE
                            pe.wait_ge(S["bl_ready"], p * FE + (kk + 1))
                            for j in range(2):
                                a = [v[:, kk, j * P:(j + 1) * P] for v in (BH, BL)]
                                for c in range(2):
                                    end = three(pe, PB[4 + 2 * j + c][:, :], a, [v[:, c * 512:(c + 1) * 512] for v in w], kk == 0, kk == FE - 1)
                        end.then_inc(S["w3_used"], 1)
                    pe.wait_ge(S["s_ready"], p + 2)
                    gather_pe(pe, p)
                    pe.wait_ge(S["st_ready"], p + 1)
                    pe.wait_ge(S["yh_ready"], p * 4 + 4)
                    pe.wait_ge(S["yl_ready"], p * 4 + 4)
                    for m in range(KD):
                        for part, c in (("sa", slice(0, HN)), ("sb", slice(HN, T))):
                            b, u = USE[part, m]
                            pe.wait_ge(fb[b], p * USES[b] + (FIRST[b] + u))
                            for j in range(2):
                                pe.matmul(PB[b][:, 0:HN], YH[:, j, m * P:(m + 1) * P], SGT[:, j, c], start=(j == 0), stop=False)
                                end = pe.matmul(PB[b][:, 0:HN], YL[:, j, m * P:(m + 1) * P], SGT[:, j, c], start=False, stop=(j == 1))
                        end.then_inc(S["sc_pe"], 1)

        @block.tensor
        def _(pe):
            mm = pe.matmul

            def norm_sums(q):
                if q == 0:
                    pe.wait_ge(S["ones_ready"], 2)
                for k in range(KD):
                    pe.wait_ge(S["sq_ready"], KD * q + k + 1)
                    mm(PB[5][:, 0:HN], ONES[:], SQ[:, k % 2, 0:HN], start=(k == 0), stop=(k == KD - 1))
                    mm(PB[6][:, 0:HN], ONES[:], SQ[:, k % 2, HN:T], start=(k == 0), stop=(k == KD - 1)).then_inc(S["sq_used"], 1)

            def tile_mms(slot, b, nk, rhs, first=True, last=True, k0=0):
                for k in range(nk):
                    w = ring[:, slot, k * P:(k + 1) * P]
                    a, z = first and k == 0, last and k == nk - 1
                    mm(PM[b][:, 0:HN], w, rhs(k0 + k)[:, 0:HN], start=a, stop=z)
                    end = mm(PS[b][:, 0:HN], w, rhs(k0 + k)[:, HN:T], start=a, stop=z)
                end.then_inc(S["w_used"], 1)

            def wait_free(b, count):
                pe.wait_ge(free_m[b], count)
                pe.wait_ge(free_s[b], count)

            def gemm(l, stage, nf, rhs):
                f0, t0, per = FILL[stage, l], TILE[stage, l], PER[stage, l]
                na = per - 1
                def rnd(j, peeled):
                    for s in range(4):
                        for i in range(na):
                            wait_landed(pe, f0, per * s + i, j * per)
                            ada_mms(pe, slot_of(f0, per * s + i), (na * s + i) % 2)
                        wait_landed(pe, f0, per * s + na, j * per)
                        if not (peeled and t0 + s < 2):
                            wait_free(s % 2, j * 2 + (t0 + s) // 2)
                        tile_mms(slot_of(f0, per * s + na), s % 2, KD, rhs)
                        for i in range(na):
                            n = na * s + i
                            ada_turn(pe, n % 2, j * (4 * na) + (ADA0[stage, l] + n + 1), bass.ds(j * (4 * na * G9) + n * G9, G9))
                if t0 == 0:
                    rnd(0, True)
                with pe.Fori(1 if t0 == 0 else 0, nf // RING) as j:
                    rnd(j, False)

            h = lambda k: hT[:, k, :]
            for l in range(L):
                norm_sums(2 * l)
                if l == 0:
                    pe.wait_ge(S["c_act"], 1)
                    pe.wait_ge(S["rs_sqrt"], 2)
                    for i in range(ADA_FIRST):
                        wait_landed(pe, 0, i, 0)
                        ada_mms(pe, i % RING, i % 2)
                        if i > 0:
                            ada_turn(pe, (i - 1) % 2, i, slice((i - 1) * G9, i * G9))
                    ada_turn(pe, i % 2, i + 1, slice(i * G9, (i + 1) * G9))
                pe.wait_ge(S["h_main"], KD * (2 * l + 1))
                pe.wait_ge(S["h_small"], 2 * l + 1)
                gemm(l, "in", M_IN, h)
                for n in range(NCH):
                    tok = slice(n * P, min((n + 1) * P, T))
                    m = tok.stop - tok.start
                    for k in range(KD):
                        end = mm(PB[7][0:m, n * 8:n * 8 + 8], hT[:, k, tok], WAB[:, l, k, :], start=(k == 0), stop=(k == KD - 1))
                end.then_inc(S["ab_pe"], 1)
                mixer_pe(pe, l)
                pe.wait_ge(S["ya_ready"], 2 * (l + 1))
                pe.wait_ge(S["yb_ready"], H * (l + 1))
                pe.wait_ge(S["yc_ready"], 2 * (l + 1))
                gemm(l, "out", KD, h)
                norm_sums(2 * l + 1)
                pe.wait_ge(S["h_main"], KD * (2 * l + 2))
                pe.wait_ge(S["h_small"], 2 * l + 2)
                if l % 2 == 0:
                    ffn_pe(pe, l)
                else:
                    router_pe(pe, l)
                    moe_pe(pe, l)
            norm_sums(2 * L)

        def mixer_act(act, l):
            fn = act.activation
            t1 = TILE["in", l] + M_IN
            for fr in free_m + free_s:
                act.wait_ge(fr, t1 // 2)
            act.wait_ge(S["ab_gates"], l + 1)
            fn(SM[:, 1, :], SM[:, 0, :], ACT.Exp).then_inc(S["small_exp"], 1)
            fn(SM[:, 11, :].rearrange("p (n h) -> p n h", h=H), ABt[:, :, 0:H], ACT.Tanh, scale=0.5).then_inc(S["small_tanh"], 1)
            fn(SM[:, 12, 0:H], par("a_log", l, 0, H), ACT.Exp).then_inc(S["small_tanh"], 1)
            for c in range(2):
                act.wait_ge(S["ln_sub"], 2 * l + c + 1)
                fn(SQ[:, c, :], XA[:, c, :], ACT.Square).then_inc(S["ln_sq"], 1)
            act.wait_ge(S["ln_sum"], 2 * l + 2)
            fn(RS[:, 0:HN], PB[2][:, 0:HN], ACT.Sqrt, scale=1.0 / 256, bias=EPSC[:, 0:1]).then_inc(S["ln_mean"], 1)
            fn(RS[:, HN:T], PB[3][:, 0:HN], ACT.Sqrt, scale=1.0 / 256, bias=EPSC[:, 0:1]).then_inc(S["ln_mean"], 1)
            act.wait_ge(S["conv_q"], 12 * (l + 1))
            act.wait_ge(S["new_states"], l + 1)
            for c in range(2):
                for a in range(2):
                    act.wait_ge(S["lru_g_pe"], 4 * l + 2 * c + a + 1)
                    bias = LM[:, l, 6 + a, c:c + 1]
                    fn(lw(a)[:, c, 0:HN], PB[5][:, 0:HN], ACT.Tanh, scale=0.5, bias=bias).then_inc(S["act_own"], 1)
                    fn(lw(a)[:, c, HN:T], PB[6][:, 0:HN], ACT.Tanh, scale=0.5, bias=bias).then_inc(S["lru_t"], 1)
            act.wait_ge(S["lru_t"], 4 * (l + 1))
            for c in range(2):
                fn(lw(2)[:, c, :], lw(0)[:, c, :], ACT.Tanh, scale=LM[:, l, 5, c:c + 1], bias=LM[:, l, 5, c:c + 1]).then_inc(S["lru_tz"], 1)
            act.wait_ge(S["small_ready"], 4 * l + 3)
            fn(SM[:, 6, :], SM[:, 4, :], ACT.Exp).then_inc(S["small_exp2"], 1)
            fn(SM[:, 8, :], SM[:, 7, :], ACT.Exp).then_inc(S["small_exp2"], 1)
            fn(SM[:, 9, :], SM[:, 5, :], ACT.Exp).then_inc(S["small_exp2"], 1)
            fn(ELS[:], ELS[:], ACT.Exp).then_inc(S["small_exp2"], 1)
            for c in range(2):
                fn(pj[:, LRU_G + c, SO - TP:CW], pj[:, LRU_G + c, SO - TP:CW], ACT.Gelu_apprx_tanh).then_inc(S["gelu_ready"], 1)
            act.wait_ge(S["lru_tz"], 2 * (l + 1))
            fn(lw(4)[:], lw(2)[:], ACT.Sqrt).then_inc(S["lru_sqrt"], 1)
            for c in range(2):
                act.wait_ge(S["ln_done"], 2 * l + c + 1)
                fn(hT[:, c, :], XA[:, c, :], ACT.Silu, scale=par("ln_a_g", l, c), bias=par("ln_a_b", l, c)).then_inc(S["ya_ready"], 1)
            for i in range(12):
                act.wait_ge(S["conv_q"], 12 * l + i + 1)
                fn(QC[:, i, :], QC[:, i, :], ACT.Silu).then_inc(S["q_silu"], 1)
            fn(pj[:, ZT:ZT + H, SO - TP:CW], pj[:, ZT:ZT + H, SO - TP:CW], ACT.Silu).then_inc(S["silu_z"], 1)
            for c in range(2):
                act.wait_ge(S["lru_scan"], 2 * l + c + 1)
                fn(SQ[:, c, :], lw(3)[:, c, :], ACT.Square).then_inc(S["yc_sq"], 1)
            act.wait_ge(S["yc_pe"], l + 1)
            act.wait_ge(S["ln_used"], l + 1)
            fn(RS[:, 0:HN], PB[5][:, 0:HN], ACT.Sqrt, scale=1.0 / 256, bias=EPSC[:, 0:1]).then_inc(S["act_own"], 1)
            fn(RS[:, HN:T], PB[6][:, 0:HN], ACT.Sqrt, scale=1.0 / 256, bias=EPSC[:, 0:1]).then_inc(S["yc_sqrt"], 1)
            for i in range(2 * H):
                act.wait_ge(S["q_silu"], 12 * (l + 1))
                if i >= 2:
                    act.wait_ge(S["l2_pe"], 8 * l + i - 1)
                else:
                    act.wait_ge(S["yc_pe"], l + 1)
                fn(SQ[:, i % 2, :], QC[:, i, :], ACT.Square).then_inc(S["l2_sq"], 1)
                if i > 0:
                    l2_root(act, l, i - 1)
            l2_root(act, l, 2 * H - 1)
            for n in range(NCH):
                tok, m, levels = chunk(n)
                q = NCH * l + n
                act.wait_ge(S["tr_pe"], q + 1)
                b4 = lambda i, rows=P, w=P: PB[i][0:rows, 0:H * w].rearrange("p (h c) -> p h c", h=H)
                act.wait_ge(S["small_exp2"], 4 * (l + 1))
                for hh in range(H):
                    e = fn(w4(0)[0:m, hh, :], b4(0, m)[:, hh, :], ACT.Copy, scale=SM[0:m, 8, n * H + hh:n * H + hh + 1])
                e.then_inc(S["tr_evac"], 1)
                for hh in range(H):
                    e = fn(w4(1)[0:m, hh, :], b4(1, m)[:, hh, :], ACT.Copy, scale=SM[0:m, 2, n * H + hh:n * H + hh + 1])
                e.then_inc(S["tr_evac"], 1)
                act.wait_ge(S["mat_pe"], q + 1)
                fn(w4(3)[:, :, 0:m], b4(4, P, m), ACT.Exp).then_inc(S["eg_ready"], 1)
                act.wait_ge(S["dd_min"], q + 1)
                fn(w4(4)[0:m, :, 0:m], w4(4)[0:m, :, 0:m], ACT.Exp).then_inc(S["dd_exp"], 1)
                for v in range(1, levels):
                    z = sum(chunk(i)[2] for i in range(n)) + v + len(LVL_ALL) * l
                    for g in range(2):
                        act.wait_ge(S["p_pe"], 2 * z + g + 1)
                        fn(w4(11)[0:m, 2 * g:2 * g + 2, 0:m], PB[BANK_P[g]][0:m, 0:2 * P].rearrange("p (h c) -> p h c", h=2)[:, :, 0:m],
                           ACT.Copy).then_inc(S["p_copied"], 1)
                if n == 4:
                    act.wait_ge(S["ks_pe"], q + 1)
                    fn(w4(11)[:, :, 0:m], b4(1, P, m), ACT.Copy).then_inc(S["ks_copied"], 1)
                act.wait_ge(S["vn_pe"], q + 1)
                fn(w4(13)[0:m], b4(2, m), ACT.Copy).then_inc(S["vn_copied"], 1)
                act.wait_ge(S["o_pe"], q + 1)
                fn(hT[:, 2:2 + H, tok], b4(3, P, m), ACT.Copy).then_inc(S["o_copied"], 1)
            for hh in range(H):
                act.wait_ge(S["o_copied"], NCH * (l + 1))
                if hh >= 2:
                    act.wait_ge(S["on_pe"], H * l + hh - 1)
                fn(SQ[:, hh % 2, :], hT[:, 2 + hh, :], ACT.Square).then_inc(S["on_sq"], 1)
                if hh > 0:
                    on_root(act, l, hh - 1)
            on_root(act, l, H - 1)

        def l2_root(act, l, i):
            s = float(P) if i < H else 1.0
            act.wait_ge(S["l2_pe"], 8 * l + i + 1)
            if i > 0:
                act.wait_ge(S["l2_done"], 8 * l + i)
            else:
                act.wait_ge(S["yc_ready"], 2 * (l + 1))
            bias = EPSC[:, 1:2] if i < H else EPSC[:, 0:1]
            act.activation(RS[:, 0:HN], PM[i % 2][:, 0:HN], ACT.Sqrt, scale=s, bias=bias).then_inc(S["l2_sqrt"], 1)
            act.activation(RS[:, HN:T], PS[i % 2][:, 0:HN], ACT.Sqrt, scale=s, bias=bias).then_inc(S["l2_sqrt"], 1)

        def on_root(act, l, hh):
            act.wait_ge(S["on_pe"], H * l + hh + 1)
            if hh > 0:
                act.wait_ge(S["on_scaled"], H * l + hh)
            act.activation(RS[:, 0:HN], PM[hh % 2][:, 0:HN], ACT.Sqrt, scale=1.0 / P, bias=EPSC[:, 0:1]).then_inc(S["on_sqrt"], 1)
            act.activation(RS[:, HN:T], PS[hh % 2][:, 0:HN], ACT.Sqrt, scale=1.0 / P, bias=EPSC[:, 0:1]).then_inc(S["on_sqrt"], 1)


        MOD_BATCH = {0: 1, 1: 2, 2: 2, 3: 3}
        X_DONE = {1: 2 * KD, 2: 6 * KD, 3: 8 * KD}

        def split_high(act, raw, high, s, g, last_use):
            act.wait_ge(landed3[s], g[1])
            if last_use is not None:
                act.wait_ge(S["w3_used"], last_use)
            act.activation(high, raw, ACT.Copy).then_inc(S["wh_ready"], 1)

        def ffn_act(act, l):
            fn, t0, q = act.activation, TILE["ffn", l], 2 * l + 1
            act.wait_ge(S["h_small"], q + 1)
            act.wait_ge(S["out_states"], 16 * 7 * (l + 1))
            for k in range(KD):
                act.wait_ge(S["h_main"], KD * q + k + 1)
                fn(HH[:, k, :], hT[:, k, :], ACT.Copy).then_inc(S["hh_ready"], 1)
            act.wait_ge(S["x_ready"], X_DONE[q])

            def high(hv, i, first=False):
                s, w = i % RING3, WK if i % G3 < 2 * FE else SLOT
                split_high(act, raw3(s, w), VH[:, s, 0:w], s, (None, (hv * (G3 // RING3) + (i // RING3 + 1)) * 16),
                           None if first else hv * G3 + (i - 2))
            for i in range(AHEAD):
                high(0, i, first=True)
            with act.Fori(0, 2) as hv:
                for i in range(G3):
                    if i > 0:
                        high(hv, i + AHEAD)
                    if i >= 2 * FE:
                        continue
                    pair, t = i // 2, t0 + i
                    if i % 2 == 0:
                        act.wait_ge(S["w3_used"], hv * G3 + (i + 1))
                        act.wait_ge(free_m[1], hv * (G3 // 2) + (t // 2 - 1))
                        act.wait_ge(free_s[1], hv * (G3 // 2) + (t // 2 - 1))
                        fn(SQ[:, pair % 2, 0:HN], PM[0][:, 0:HN], ACT.Silu).then_inc(free_m[0], 1)
                        fn(SQ[:, pair % 2, HN:T], PS[0][:, 0:HN], ACT.Silu).then_inc(free_s[0], 1)
                        if i == 0:
                            high(hv, AHEAD, first=True)
                    else:
                        act.wait_ge(S["af_ready"], hv * FE + (pair + 1))
                        fn(AH[:, pair, :], AF[:, pair % 2, :], ACT.Copy).then_inc(S["ah_ready"], 1)

        def moe_act(act, l):
            fn, q = act.activation, 2 * l + 1
            act.wait_ge(S["lg_exp"], 1)
            act.wait_ge(S["out_states"], 16 * 7 * (l + 1))
            fn(G12[:, 1, :], G12[:, 0, :], ACT.Exp).then_inc(S["gate_exp"], 1)
            for n in range(NCH):
                m = min((n + 1) * P, T) - n * P
                act.wait_ge(S["ht_pe"], n + 1)
                for c in range(2):
                    fn(HTH[0:m, n, c * 512:(c + 1) * 512], PB[2 * (n % 2) + c][0:m, :], ACT.Copy).then_inc(S["hth_ready"], 1)
            act.wait_ge(S["nr_ready"], 1)
            rounds = act.value_load(NR[0:1, 0:1], min_val=1, max_val=ROUNDS)

            def high(p, i):
                s = (B_MOE + i) % RING3
                split_high(act, raw3(s, WK), UH[:, s, :], s, (None, (p * (GX // RING3) + ((B_MOE + i) // RING3 + 1)) * 16), p * GX + (B_MOE + i - 2))

            def gather_high(p1):
                for k in range(KD):
                    act.wait_ge(S["gat_pe"], p1 * (2 * KD) + (2 * k + 1))
                    fn(XH[:, k, :], PB[k % 2][:, 0:CAP], ACT.Copy).then_inc(fb[k % 2], 1)
            for i in range(AHEAD):
                s = (B_MOE + i) % RING3
                split_high(act, raw3(s, WK), UH[:, s, :], s, (None, ((B_MOE + i) // RING3 + 1) * 16), B_MOE + i - 2)
            gather_high(0)
            with act.Fori(0, rounds) as rd:
                with act.Fori(0, NE) as e:
                    p = act.snap(rd * NE + e)
                    for i in range(GX):
                        high(p, i + AHEAD)
                        if i >= 2 * FE:
                            continue
                        pair = i // 2
                        if i % 2 == 0:
                            act.wait_ge(S["w3_used"], p * GX + (B_MOE + i + 1))
                            if pair >= 2:
                                act.wait_ge(S["bf_ready"], p * FE + (pair - 1))
                            fn(SQ[:, pair % 2, 0:CAP], PB[i % 4][:, 0:CAP], ACT.Silu).then_inc(fb[i % 4], 1)
                        else:
                            act.wait_ge(S["bf_ready"], p * FE + (pair + 1))
                            fn(BH[:, pair, :], AF[:, pair % 2, 0:CAP], ACT.Copy).then_inc(S["bh_ready"], 1)
                    act.wait_ge(S["w3_used"], p * GX + (B_MOE + GX))
                    act.wait_ge(S["st_ready"], p + 1)
                    for j in range(2):
                        for c in range(2):
                            fn(YH[:, j, c * 512:(c + 1) * 512], PB[4 + 2 * j + c][:, :], ACT.Copy, scale=GS[:, j:j + 1]).then_inc(S["yh_ready"], 1)
                    gather_high(p + 1)

        @block.scalar
        def _(act):
            fn = act.activation

            def squares(q):
                if q == 0:
                    act.wait_ge(S["consts"], 8 * 16)
                else:
                    if q < 2 * L:
                        act.wait_ge(S["x_ready"], X_DONE[q])
                    else:
                        act.wait_ge(S["moe_done"], 1)
                for k in range(KD):
                    if KD * q + k >= 2:
                        act.wait_ge(S["sq_used"], KD * q + k - 1)
                    fn(SQ[:, k % 2, :], xT[:, k, :], ACT.Square).then_inc(S["sq_ready"], 1)

            def root(q):
                act.wait_ge(S["sq_used"], KD * (q + 1))
                fn(RS[:, 0:HN], PB[5][:, 0:HN], ACT.Sqrt, scale=1.0 / D, bias=EPSC[:, 0:1]).then_inc(S["rs_sqrt"], 1)
                fn(RS[:, HN:T], PB[6][:, 0:HN], ACT.Sqrt, scale=1.0 / D, bias=EPSC[:, 0:1]).then_inc(S["rs_sqrt"], 1)

            def row_out(b, used):
                act.wait_ge(S["w_used"], used)
                fn(MROW[:, b, :], ROW[b], ACT.Copy).then_inc(S["row_out"], 1)

            def modulate(q):
                l, w = q // 2, q % 2
                act.wait_ge(S["mod_done"], MOD_BATCH[q])
                for k in range(KD):
                    act.wait_ge(S["h_mul"], KD * q + k + 1)
                    fn(hT[:, k, 0:TP], hT[:, k, 0:TP], ACT.Identity, scale=AM[:, q, k, 0:1], bias=MOD[:, l, 3 * KD * w + k, 0:1]).then_inc(S["h_main"], 1)

            act.wait_ge(S["consts"], 8 * 16)
            act.wait_ge(S["ones_ready"], 2)
            fn(CT[:], CT[:], ACT.Silu).then_inc(S["c_act"], 1)
            act.wait_ge(S["lam_abs"], 1)
            fn(LM[:, :, 1, :], LM[:, :, 0, :], ACT.Exp).then_inc(S["sp_exp"], 1)
            for l in range(L):
                squares(2 * l)
                root(2 * l)
                if l == 0:
                    for i in range(ADA_FIRST):
                        row_out(i % 2, i + 1)
                modulate(2 * l)
                f0 = FILL["in", l]
                act.wait_ge(S["pads_ready"], l + 1)
                per = PER["in", l]
                na = per - 1
                for s in range(4):
                    for i in range(na):
                        row_out((na * s + i) % 2, f0 + per * s + i + 1)
                    act.wait_ge(S["w_used"], f0 + per * (s + 1))
                    func = ACT.Copy if s < 2 else ACT.Tanh
                    smp = pj[:, s, SO:CW].rearrange("p (b c) -> p b c", c=WQ - 1 + NS)[:, :, WQ - 1:]
                    fn(pj[:, s, WQ - 1:WQ - 1 + HN], PM[s % 2][:, 0:HN], func, scale=0.5).then_inc(free_m[s % 2], 1)
                    fn(pj[:, s, WQ - 1 + HN:SO], PS[s % 2][:, 0:HP], func, scale=0.5)
                    fn(smp, pv_s(PS[s % 2][:, HP:HN]), func, scale=0.5).then_inc(free_s[s % 2], 1)
                with act.Fori(1, M_IN // RING) as j:
                    for s in range(RING):
                        for i in range(na):
                            row_out((na * s + i) % 2, j * (4 * per) + (f0 + per * s + i + 1))
                        act.wait_ge(S["w_used"], j * (4 * per) + (f0 + per * (s + 1)))
                        row = PJ[:, bass.ds((j * RING + s) * CW, CW)]
                        fn(row[:, WQ - 1:WQ - 1 + HN], PM[s % 2][:, 0:HN], ACT.Copy).then_inc(free_m[s % 2], 1)
                        fn(row[:, WQ - 1 + HN:SO], PS[s % 2][:, 0:HP], ACT.Copy)
                        smp = row[:, SO:CW].rearrange("p (b c) -> p b c", c=WQ - 1 + NS)[:, :, WQ - 1:]
                        fn(smp, pv_s(PS[s % 2][:, HP:HN]), ACT.Copy).then_inc(free_s[s % 2], 1)
                mixer_act(act, l)
                for i in range(ADA_OUT[l] * KD):
                    row_out(i % 2, FILL["out", l] + 2 * i + 1)
                squares(2 * l + 1)
                root(2 * l + 1)
                modulate(2 * l + 1)
                if l % 2 == 0:
                    ffn_act(act, l)
                else:
                    moe_act(act, l)
            squares(2 * L)
            root(2 * L)

        def mixer_dve(dve, l, then, log1p_steps, modulation):
            t0 = TILE["in", l]
            for c in range(2):
                dve.wait_ge(free_s[c], t0 // 2 + 2)
                sv = lambda ap: ap.rearrange("p (b c) -> p b c", c=WQ - 1 + NS)[:, :, WQ - 1:]
                dve.scalar_tensor_tensor(UA[:, c, WA - 1:AO], pj[:, A_GATE + c, WQ - 1:SO], 1.0, pj[:, A_VAL + c, WQ - 1:SO], ALU.add, ALU.mult).then_inc(S["glu_ready"], 1)
                us = UA[:, c, AO:CA].rearrange("p (b c) -> p b c", c=WA - 1 + NS)[:, :, WA - 1:]
                dve.scalar_tensor_tensor(us, sv(pj[:, A_GATE + c, SO:CW]), 1.0, sv(pj[:, A_VAL + c, SO:CW]), ALU.add, ALU.mult).then_inc(S["glu_ready"], 1)
            dve.wait_ge(S["glu_ready"], 4 * (l + 1))
            dve.wait_ge(S["pads_ready"], l + 1)

            def conv(dst, src, so, width, w, bias, last_sem):
                step = width - 1 + NS
                for k in range(width):
                    smp = src[:, so:].rearrange("p (b c) -> p b c", c=step)[:, :, k:k + NS]
                    wk_ = w[:, k:k + 1]
                    if k == 0 and bias is not None:
                        a = dve.tensor_scalar(dst[:, 0:TP], src[:, 0:TP], wk_, bias, ALU.mult, ALU.add)
                        then(a)
                        a = dve.tensor_scalar(pv_s(dst[:, TP:T]), smp, wk_, bias, ALU.mult, ALU.add)
                    elif k == 0:
                        a = dve.tensor_scalar(dst[:, 0:TP], src[:, 0:TP], wk_, None, ALU.mult)
                        then(a)
                        a = dve.tensor_scalar(pv_s(dst[:, TP:T]), smp, wk_, None, ALU.mult)
                    else:
                        a = dve.scalar_tensor_tensor(dst[:, 0:TP], src[:, k:k + TP], wk_, dst[:, 0:TP], ALU.mult, ALU.add)
                        then(a)
                        a = dve.scalar_tensor_tensor(pv_s(dst[:, TP:T]), smp, wk_, pv_s(dst[:, TP:T]), ALU.mult, ALU.add)
                    if k < width - 1:
                        then(a)
                a.then_inc(last_sem, 1)

            for c in range(2):
                o = PC["conv_a_w"][0] + c * WA
                conv(XA[:, c, :], UA[:, c, :], AO, WA, PA[:, l, o:o + WA], par("conv_a_b", l, c), S["conv_a"])
            for c in range(2):
                dve.wait_ge(free_s[c], t0 // 2 + 3)
                o = PC["conv_lru_w"][0] + c * WQ
                conv(XL[:, c, :], pj[:, LRU_X + c, :], SO, WQ, PA[:, l, o:o + WQ], par("conv_lru_b", l, c), S["conv_l"])
            for i in range(12):
                dve.wait_ge(free_s[i % 2], (t0 + QKV + i) // 2 + 1)
                o = PC["conv_qkv_w"][0] + i * WQ
                conv(QC[:, i, :], pj[:, QKV + i, :], SO, WQ, PA[:, l, o:o + WQ], None, S["conv_q"])
            dve.wait_ge(S["conv_q"], 12 * (l + 1))
            modulation(l + 1)
            dve.wait_ge(S["ab_pe"], l + 1)
            then(dve.tensor_copy(ABt[:, 0:4, :], PB[7][:, 0:32].rearrange("p (n c) -> p n c", c=8)))
            then(dve.tensor_copy(ABt[0:TS, 4, :], PB[7][0:TS, 32:40]))
            sm = lambda i: SM[:, i, :]
            v3 = lambda i: SM[:, i, :].rearrange("p (n h) -> p n h", h=H)
            b3 = lambda ap: ap.unsqueeze(1).broadcast_to([P, NCH, H])
            then(dve.tensor_tensor(v3(10), ABt[:, :, H:2 * H], b3(par("dt_bias", l, 0, H)), ALU.add))
            dve.scalar_tensor_tensor(sm(0), sm(10), -1.0, sm(10), ALU.mult, ALU.min).then_inc(S["ab_gates"], 1)
            then(dve.tensor_scalar(sm(10), sm(10), 0.0, None, ALU.max))
            dve.wait_ge(S["small_exp"], l + 1)
            dve.wait_ge(S["small_tanh"], 2 * (l + 1))
            log1p_steps(sm(3), sm(1), sm(13), sm(14), sm(10))
            then(dve.tensor_tensor(v3(3), v3(3), b3(SM[:, 12, 0:H]), ALU.mult))
            then(dve.tensor_scalar(sm(3), sm(3), -1.0, None, ALU.mult))
            dve.tensor_scalar(sm(2), sm(11), 0.5, 0.5, ALU.mult, ALU.add).then_inc(S["small_ready"], 1)
            dve.tensor_tensor(GSEL[:], SM[0:TS, 3, 16:20].unsqueeze(1).broadcast_to([TS, NB, H]),
                              bm.unsqueeze(2).broadcast_to([TS, NB, H]), ALU.mult).then_inc(S["small_ready"], 1)
            dve.wait_ge(S["ln_sum"], 2 * l + 1)
            for c in range(2):
                then(dve.scalar_tensor_tensor(XA[:, c, 0:HN], PB[0][:, 0:HN], -1.0 / 256, XA[:, c, 0:HN], ALU.mult, ALU.add))
                dve.scalar_tensor_tensor(XA[:, c, HN:T], PB[1][:, 0:HN], -1.0 / 256, XA[:, c, HN:T], ALU.mult, ALU.add).then_inc(S["ln_sub"], 1)
            dve.wait_ge(S["ln_mean"], 2 * (l + 1))
            then(dve.reciprocal(RS[:], RS[:]))
            for c in range(2):
                ins = dve.tensor_tensor(XA[:, c, :], XA[:, c, :], RS[:], ALU.mult)
                ins.then_inc(S["ln_done"], 1)
            dve.wait_ge(S["ln_done"], 2 * (l + 1))
            dve.sem_inc(S["ln_used"], 1)
            dve.wait_ge(S["gc_pe"], l + 1)
            then(dve.tensor_copy(SM[:, 4, 0:16], PB[7][:, 64:80]))
            then(dve.tensor_copy(SM[0:TS, 4, 16:20], PB[7][0:TS, 80:84]))
            then(dve.tensor_copy(SM[:, 5, 0:16], PB[7][:, 84:100]))
            then(dve.tensor_copy(SM[0:TS, 5, 16:20], PB[7][0:TS, 100:104]))
            then(dve.tensor_copy(ELS[:].rearrange("p b h -> p (b h)"), PB[7][:, 104:136]))
            dve.tensor_tensor(sm(7), sm(5), sm(4), ALU.subtract).then_inc(S["small_ready"], 1)
            dve.wait_ge(S["small_exp2"], 4 * (l + 1))
            dve.scalar_tensor_tensor(sm(15), sm(2), -1.0, sm(6), ALU.mult, ALU.mult).then_inc(S["small_ready"], 1)
            dve.wait_ge(S["lru_sqrt"], l + 1)
            tr, ti, tz, hs, sq = lw(0), lw(1), lw(2), lw(3), lw(4)
            then(dve.tensor_scalar(tr, tz, 1.0, None, ALU.add))
            then(dve.reciprocal(tr, tr))
            then(dve.tensor_scalar(tz, tz, -1.0, 1.0, ALU.mult, ALU.add))
            then(dve.tensor_tensor(tz, tz, tr, ALU.mult))
            then(dve.tensor_tensor(sq, sq, tr, ALU.mult))
            then(dve.scalar_tensor_tensor(ti, ti, 1.0, XL[:], ALU.add, ALU.mult))
            then(dve.tensor_tensor(sq, sq, ti, ALU.mult))
            a0 = tz[:, :, TP:T].rearrange("p c (b s) -> p c b s", s=NS)[:, :, :, 0]
            b0 = sq[:, :, TP:T].rearrange("p c (b s) -> p c b s", s=NS)[:, :, :, 0]
            t0_ = SN[:, 0:2 * NB].rearrange("p (c b) -> p c b", c=2)
            dve.wait_ge(S["states_in"], 16 * 5 * (l + 1))
            then(dve.tensor_tensor(t0_, a0, ST[:].rearrange("p (c b) -> p c b", c=2), ALU.mult))
            then(dve.tensor_tensor(b0, b0, t0_, ALU.add))
            then(dve.memset(a0, 0.0))
            for c in range(2):
                then(dve.tensor_tensor_scan(hs[:, c, :], tz[:, c, :], sq[:, c, :], 0.0, ALU.mult, ALU.add))
            sn = SN[:].rearrange("p (c g) -> p c g", c=2)
            then(dve.tensor_copy(sn[:, :, 0:1], hs[:, :, TP - 1:TP]))
            dve.tensor_copy(sn[:, :, 1:G9], hs[:, :, TP:T].rearrange("p c (b s) -> p c b s", s=NS)[:, :, :, NS - 1]).then_inc(S["lru_new"], 1)
            dve.wait_ge(S["lru_new"], l + 1)
            dve.wait_ge(S["gelu_ready"], 2 * (l + 1))
            for c in range(2):
                then(dve.tensor_tensor(hs[:, c, 0:TP], hs[:, c, 0:TP], pj[:, LRU_G + c, SO - TP:SO], ALU.mult))
                gs = pj[:, LRU_G + c, SO:CW].rearrange("p (b c) -> p b c", c=WQ - 1 + NS)[:, :, WQ - 1:]
                dve.tensor_tensor(pv_s(hs[:, c, TP:T]), pv_s(hs[:, c, TP:T]), gs, ALU.mult).then_inc(S["lru_scan"], 1)
            dve.wait_ge(S["lru_scan"], 2 * (l + 1))
            dve.wait_ge(S["yc_sqrt"], l + 1)
            then(dve.reciprocal(RS[:], RS[:]))
            for c in range(2):
                dve.scalar_tensor_tensor(hT[:, 6 + c, :], hs[:, c, :], par("lru_norm", l, c), RS[:], ALU.mult, ALU.mult).then_inc(S["yc_ready"], 1)
            dve.wait_ge(S["yc_ready"], 2 * (l + 1))
            for i in range(2 * H):
                dve.wait_ge(S["l2_sqrt"], 16 * l + 2 * (i + 1))
                then(dve.reciprocal(RS[:], RS[:]))
                dve.tensor_tensor(QC[:, i, :], QC[:, i, :], RS[:], ALU.mult).then_inc(S["l2_done"], 1)
            dve.wait_ge(S["l2_done"], 8 * (l + 1))
            dve.memset(SP_[:], 0.0).then_inc(S["sp_zero"], 1)
            for n in range(NCH):
                tok, m, levels = chunk(n)
                q = NCH * l + n
                b4 = lambda i, rows=P, w=P: PB[i][0:rows, 0:H * w].rearrange("p (h c) -> p h c", h=H)
                col = lambda i, hh, rows=m: SM[0:rows, i, n * H + hh:n * H + hh + 1]
                mask = tri if n < 4 else btri
                for hh in range(H):
                    then(dve.tensor_scalar(w4(7)[0:m, hh, 0:m], mask[0:m, :], col(3, hh), None, ALU.mult))
                    ins = dve.tensor_scalar(w4(8)[0:m, hh, 0:m], ident[0:m, 0:m], col(2, hh), None, ALU.mult)
                    if hh < H - 1:
                        then(ins)
                ins.then_inc(S["rhs_ready"], 1)
                mb = lambda ap: ap.unsqueeze(1).broadcast_to([m, H, m])
                dve.wait_ge(S["eg_ready"], q + 1)
                dd, uu, qd = w4(4)[0:m, :, 0:m], w4(5)[0:m, :, 0:m], w4(6)[0:m, :, 0:m]
                then(dve.tensor_tensor(dd, b4(4, m, m), SM[0:m, 4, n * H:(n + 1) * H].unsqueeze(2).broadcast_to([m, H, m]), ALU.subtract))
                dve.tensor_scalar(dd, dd, 0.0, None, ALU.min).then_inc(S["dd_min"], 1)
                dve.wait_ge(S["dd_exp"], q + 1)
                then(dve.tensor_tensor(dd, dd, mb(mask[0:m, :]), ALU.mult))
                then(dve.tensor_tensor(uu, b4(2, m, m), dd, ALU.mult))
                then(dve.tensor_tensor(uu, uu, b4(5, m, m), ALU.mult))
                dve.tensor_tensor(qd, b4(3, m, m), dd, ALU.mult).then_inc(S["dd_ready"], 1)
                mb2 = lambda ap: ap.unsqueeze(1).broadcast_to([m, 2, m])

                def um_level(v):
                    dve.tensor_tensor(w4(7 + v % 2)[0:m, :, 0:m], uu, mb(lvl(v, m)), ALU.mult).then_inc(S["um_ready"], 1)
                um_level(0)
                for v in range(levels):
                    z = sum(chunk(i)[2] for i in range(n)) + v + len(LVL_ALL) * l
                    dve.wait_ge(S["um_ready"], z + 1)
                    if v + 1 < levels:
                        um_level(v + 1)
                    for g in range(2):
                        if v == 0:
                            then(dve.tensor_tensor(tg(g)[0:m, 1, :, 0:m], mb2(ident[0:m, 0:m]), w4(7)[0:m, 2 * g:2 * g + 2, 0:m], ALU.subtract))
                            dve.wait_ge(S["p_pe"], 2 * z + g + 1)
                            p = PB[BANK_P[g]][0:m, 0:2 * P].rearrange("p (h c) -> p h c", h=2)[:, :, 0:m]
                            dve.tensor_tensor(tg(g)[0:m, 0, :, 0:m], mb2(ident[0:m, 0:m]), p, ALU.subtract).then_inc(S["t_done"], 1)
                            continue
                        a = slice(0, 2) if v < levels - 1 else slice(1, 2)
                        dve.wait_ge(S["t_pe"], 2 * (z - q) + g - 1)
                        dve.wait_ge(S["t_done"], 2 * z + g - 1)
                        t = tg(g)[0:m, a, :, 0:m]
                        dve.tensor_tensor(t, t, pair(PB[BANK_T[g]])[0:m, a, :, 0:m], ALU.subtract).then_inc(S["t_done"], 1)
                dve.wait_ge(S["t_done"], 2 * (z + 1))
                src = b4(1, m)
                if n < 4:
                    dve.wait_ge(S["ks_pe"], q + 1)
                else:
                    dve.wait_ge(S["ks_tr"], l + 1)
                    src = b4(5, m)
                for hh in range(H):
                    ins = dve.scalar_tensor_tensor(w4(12)[0:m, hh, :], src[:, hh, :], col(15, hh), w4(1)[0:m, hh, :], ALU.mult, ALU.add)
                ins.then_inc(S["r_ready"], 1)
                if n < 4:
                    dve.wait_ge(S["st_pe"], 4 * l + n + 1)
                    for hh in range(H):
                        dve.scalar_tensor_tensor(SP_[:, hh, :], SP_[:, hh, :], col(9, hh, P), b4(4)[:, hh, :], ALU.mult, ALU.add).then_inc(S["st_done"], 1)
                    dve.wait_ge(S["st_done"], H * (4 * l + n + 1))
                else:
                    for b in range(NB):
                        if b >= 2:
                            dve.wait_ge(S["sm_pe"], NB * l + b - 1)
                        dve.tensor_scalar(w4(7 + b % 2)[0:TS], w4(0)[0:TS], bm[:, b:b + 1], None, ALU.mult).then_inc(S["sm_mask"], 1)
                        if b > 0:
                            sample_state(dve, l, b - 1, b4)
                    sample_state(dve, l, NB - 1, b4)
            dve.wait_ge(S["silu_z"], l + 1)
            for hh in range(H):
                dve.wait_ge(S["on_sqrt"], 2 * (H * l + hh + 1))
                then(dve.reciprocal(RS[:], RS[:]))
                dve.scalar_tensor_tensor(hT[:, 2 + hh, :], hT[:, 2 + hh, :], par("gdn_norm", l), RS[:], ALU.mult, ALU.mult).then_inc(S["on_scaled"], 1)
                dve.wait_ge(S["on_scaled"], H * l + hh + 1)
                then(dve.tensor_tensor(hT[:, 2 + hh, 0:TP], hT[:, 2 + hh, 0:TP], pj[:, ZT + hh, SO - TP:SO], ALU.mult))
                zs = pj[:, ZT + hh, SO:CW].rearrange("p (b c) -> p b c", c=WQ - 1 + NS)[:, :, WQ - 1:]
                dve.tensor_tensor(pv_s(hT[:, 2 + hh, TP:T]), pv_s(hT[:, 2 + hh, TP:T]), zs, ALU.mult).then_inc(S["yb_ready"], 1)

        def sample_state(dve, l, b, b4):
            dve.wait_ge(S["sm_pe"], NB * l + b + 1)
            for hh in range(H):
                dve.scalar_tensor_tensor(SS[:, b, hh, :], SS[:, b, hh, :], ELS[:, b, hh:hh + 1], b4(6 + b % 2)[:, hh, :], ALU.mult, ALU.add).then_inc(S["sm_upd"], 1)

        def ffn_dve(dve, l, residual_at):
            t0, q = TILE["ffn", l], 2 * l + 1
            for k in range(KD):
                dve.wait_ge(S["hh_ready"], k + 1)
                dve.tensor_tensor(HL[:, k, :], hT[:, k, :], f32(HH[:, k, :]), ALU.subtract).then_inc(S["hl_ready"], 1)

            def low(hv, i):
                s, w = i % RING3, WK if i % G3 < 2 * FE else SLOT
                dve.wait_ge(S["wh_ready"], hv * G3 + (i + 1))
                dve.tensor_tensor(VL[:, s, 0:w], raw3(s, w), f32(VH[:, s, 0:w]), ALU.subtract).then_inc(S["wl_ready"], 1)

            def act_low(hv, pair):
                dve.wait_ge(S["ah_ready"], hv * FE + (pair + 1))
                dve.tensor_tensor(AL[:, pair, :], AF[:, pair % 2, :], f32(AH[:, pair, :]), ALU.subtract).then_inc(S["al_ready"], 1)
            for i in range(AHEAD):
                low(0, i)
            with dve.Fori(0, 2) as hv:
                for i in range(G3):
                    low(hv, i + AHEAD)
                    pair, t = i // 2, t0 + i
                    if i < 2 * FE and i % 2 == 1:
                        dve.wait_ge(S["w3_used"], hv * G3 + (i + 1))
                        for fr in (free_m[0], free_s[0]):
                            dve.wait_ge(fr, hv * (G3 // 2) + (t // 2 + 1))
                        dve.tensor_tensor(AF[:, pair % 2, 0:HN], SQ[:, pair % 2, 0:HN], PM[1][:, 0:HN], ALU.mult).then_inc(free_m[1], 1)
                        dve.tensor_tensor(AF[:, pair % 2, HN:T], SQ[:, pair % 2, HN:T], PS[1][:, 0:HN], ALU.mult).then_inc(free_s[1], 1)
                        dve.wait_ge(free_m[1], hv * (G3 // 2) + (t // 2 + 1))
                        dve.wait_ge(free_s[1], hv * (G3 // 2) + (t // 2 + 1))
                        dve.sem_inc(S["af_ready"], 1)
                    elif 2 <= i <= 2 * FE:
                        act_low(hv, pair - 1)
                    if i >= 2 * FE:
                        m = i - 2 * FE
                        dve.wait_ge(S["w3_used"], hv * G3 + (i + 1))
                        dve.wait_ge(S["x_ready"], hv * (2 * KD) + X_DONE[q])
                        xm, tmp = residual_at(l, i % 2, m, 5 * KD)
                        dve.wait_ge(free_m[i % 2], hv * (G3 // 2) + (t // 2 + 1))
                        dve.wait_ge(free_s[i % 2], hv * (G3 // 2) + (t // 2 + 1))
                        dve.tensor_tensor(xm[:, TP:T], xm[:, TP:T], tmp, ALU.add).then_inc(S["x_ready"], 2)

        def moe_dve(dve, l, then):
            q = 2 * l + 1
            dve.wait_ge(S["out_states"], 16 * 7 * (l + 1))
            for v in (HTH, HTL):
                then(dve.memset(f32(v[TS:P, NCH - 1, :]), 0.0))
            for n in range(NCH):
                m = min((n + 1) * P, T) - n * P
                for c in range(2):
                    dve.wait_ge(S["hth_ready"], 2 * n + c + 1)
                    dve.tensor_tensor(HTL[0:m, n, c * 512:(c + 1) * 512], PB[2 * (n % 2) + c][0:m, :], f32(HTH[0:m, n, c * 512:(c + 1) * 512]),
                                      ALU.subtract).then_inc(S["htl_ready"], 1)
            dve.wait_ge(S["cnt_pe"], 1)
            pf = PF[:].rearrange("p a n e -> p a (n e)")
            mk = MK[:].rearrange("p n e -> p (n e)")
            for a in range(2):
                then(dve.tensor_tensor(pf[:, a], PB[5][:, a * NCH * NE:(a + 1) * NCH * NE], mk, ALU.mult))
            then(dve.tensor_reduce(OV[:, 0:1], PB[5][:, 80:88], AX_X, ALU.max))
            then(dve.tensor_scalar(OV[:, 1:2], OV[:, 0:1], float(CAP), None, ALU.is_gt))
            then(dve.tensor_scalar(OV[:, 2:3], OV[:, 1:2], -1.0, 1.0, ALU.mult, ALU.add))
            dve.tensor_scalar(NR[:], OV[0:1, 1:2], float(ROUNDS - 1), 1.0, ALU.mult, ALU.add).then_inc(S["nr_ready"], 1)
            then(dve.memset(PG[:], 0.0))
            then(dve.tensor_scalar(pf[:, 1], pf[:, 1], OV[:, 1:2], None, ALU.mult))
            for rd in range(ROUNDS):
                n = slice(2 * rd, min(2 * rd + 2, NCH))
                then(dve.tensor_copy(PG[:, n, 0, rd * NE:(rd + 1) * NE], PF[:, 1, n]))
                then(dve.tensor_copy(PG[:, :, 1, rd * NE:(rd + 1) * NE], GG[:, 1]))
            dve.scalar_tensor_tensor(PG[:, :, 0, 0:NE], PF[:, 0], OV[:, 2:3], PG[:, :, 0, 0:NE], ALU.mult, ALU.add).then_inc(S["pg_ready"], 1)
            dve.wait_ge(S["pg_ready"], 1)
            dve.wait_ge(S["gt_pe"], 1)
            w = 2 * (NPASS + 1)
            then(dve.tensor_copy(ROWS[:, 0:TP], PB[6][0:w, :]))
            dve.tensor_copy(ROWS[:, TP:T], PB[7][0:w, 0:TS]).then_inc(S["gt_copied"], 1)
            rounds = dve.value_load(NR[0:1, 0:1], min_val=1, max_val=ROUNDS)

            def select(p):
                for n in range(NCH):
                    col = PG[:, n, 0, bass.ds(p, 1)]
                    ins = dve.tensor_scalar(SG_[:, n, :], CO[:, C_SLOT:C_SLOT + CAP], col, None, ALU.is_equal)
                ins.then_inc(S["s_ready"], 1)

            def low(p, i):
                s = (B_MOE + i) % RING3
                dve.wait_ge(S["wh_ready"], p * GX + (B_MOE + i + 1))
                dve.tensor_tensor(UL[:, s, :], raw3(s, WK), f32(UH[:, s, :]), ALU.subtract).then_inc(S["wl_ready"], 1)

            def act_low(p, pair):
                dve.wait_ge(S["bh_ready"], p * FE + (pair + 1))
                dve.tensor_tensor(BL[:, pair, :], AF[:, pair % 2, 0:CAP], f32(BH[:, pair, :]), ALU.subtract).then_inc(S["bl_ready"], 1)

            def gather_low(p1):
                for k in range(KD):
                    dve.wait_ge(S["gat_pe"], p1 * (2 * KD) + (2 * k + 2))
                    dve.tensor_copy(XLo[:, k, :], PB[2 + k % 2][:, 0:CAP]).then_inc(fb[2 + k % 2], 1)
            select(0)
            for i in range(AHEAD):
                s = (B_MOE + i) % RING3
                dve.wait_ge(S["wh_ready"], B_MOE + i + 1)
                dve.tensor_tensor(UL[:, s, :], raw3(s, WK), f32(UH[:, s, :]), ALU.subtract).then_inc(S["wl_ready"], 1)
            gather_low(0)
            with dve.Fori(0, rounds) as rd:
                with dve.Fori(0, NE) as e:
                    p = dve.snap(rd * NE + e)
                    for i in range(GX):
                        low(p, i + AHEAD)
                        pair = i // 2
                        if i == 2:
                            dve.wait_ge(S["br_landed"], p * 16 + 16)
                            for j in range(2):
                                ins = dve.tensor_scalar(SGT[:, j, :], BR[:, 0, :], CO[:, C_SLOT + CAP + j:C_SLOT + CAP + j + 1], None, ALU.is_equal)
                                ins.then_inc(S["st_own"], 1)
                            dve.wait_ge(S["st_own"], p * 2 + 2)
                        if i in (4, 6):
                            j = i // 2 - 2
                            ins = dve.tensor_tensor_reduce(JUNK, f32(SGT[:, j, :]), BR[:, 1, :], 1.0, 0.0, ALU.mult, ALU.add, GS[:, j:j + 1])
                            if j == 1:
                                ins.then_inc(S["st_ready"], 1)
                        if i == 8:
                            select(p + 1)
                        if i < 2 * FE and i % 2 == 1:
                            dve.wait_ge(S["w3_used"], p * GX + (B_MOE + i + 1))
                            b, u = USE["gu", i - 1]
                            dve.wait_ge(fb[b], p * USES[b] + (FIRST[b] + u + 1))
                            dve.tensor_tensor(AF[:, pair % 2, 0:CAP], SQ[:, pair % 2, 0:CAP], PB[i % 4][:, 0:CAP], ALU.mult).then_inc(fb[i % 4], 1)
                            b, u = USE["gu", i]
                            dve.wait_ge(fb[b], p * USES[b] + (FIRST[b] + u + 1))
                            dve.sem_inc(S["bf_ready"], 1)
                        elif 2 <= i <= 2 * FE:
                            act_low(p, pair - 1)
                    for j in range(2):
                        for c in range(2):
                            dve.wait_ge(S["yh_ready"], p * 4 + (2 * j + c + 1))
                            cols = slice(c * 512, (c + 1) * 512)
                            dve.scalar_tensor_tensor(YL[:, j, cols], PB[4 + 2 * j + c][:, :], GS[:, j:j + 1], f32(YH[:, j, cols]), ALU.mult,
                                                     ALU.subtract).then_inc(S["yl_ready"], 1)
                    gather_low(p + 1)
                    for m in range(KD):
                        dve.wait_ge(S["sc_pe"], p * KD + (m + 1))
                        dve.wait_ge(S["x_ready"], p * (2 * KD) + X_DONE[q])
                        xm, gm = xT[:, m, :], MOD[:, l, 5 * KD + m, :]
                        (ba, ua), (bb, ub) = USE["sa", m], USE["sb", m]
                        dve.scalar_tensor_tensor(xm[:, 0:HN], PB[ba][:, 0:HN], gm[:, 0:1], xm[:, 0:HN], ALU.mult, ALU.add).then_inc(fb[ba], 1)
                        dve.scalar_tensor_tensor(xm[:, HN:TP], PB[bb][:, 0:HP], gm[:, 0:1], xm[:, HN:TP], ALU.mult, ALU.add)
                        tmp = TMP[:, m % 2, :]
                        dve.tensor_tensor(pv_s(tmp), pv_s(PB[bb][:, HP:HN]), gm[:, 1:G9].unsqueeze(2).broadcast_to([P, NB, NS]), ALU.mult).then_inc(fb[bb], 1)
                        dve.wait_ge(fb[ba], p * USES[ba] + (FIRST[ba] + ua + 1))
                        dve.wait_ge(fb[bb], p * USES[bb] + (FIRST[bb] + ub + 1))
                        dve.tensor_tensor(xm[:, TP:T], xm[:, TP:T], tmp, ALU.add).then_inc(S["x_ready"], 2)
            dve.wait_ge(S["x_ready"], rounds * (2 * KD * NE) + X_DONE[q])
            dve.wait_ge(S["br_landed"], rounds * (16 * NE) + 16)
            dve.sem_inc(S["moe_done"], 1)

        def router_dve(dve, l, then):
            dve.wait_ge(S["lg_pe"], 1)
            then(dve.tensor_copy(LG[:, 0:4, :], PB[4][:, 0:4 * NE].rearrange("p (n e) -> p n e", e=NE)))
            then(dve.tensor_copy(LG[0:TS, 4, :], PB[4][0:TS, 4 * NE:5 * NE]))
            for n in range(NCH):
                then(dve.max(MX[:, n, :], LG[:, n, :]))
                then(dve.max_index(IX[:, n, :], MX[:, n, :], LG[:, n, :]))
            then(dve.tensor_copy(IXF[:], IX[:, :, 0:2]))
            dve.tensor_tensor(G12[:, 0, :], MX[:, :, 1], MX[:, :, 0], ALU.subtract).then_inc(S["lg_exp"], 1)
            dve.wait_ge(S["gate_exp"], 1)
            then(dve.tensor_scalar(G12[:, 2, :], G12[:, 1, :], 1.0, None, ALU.add))
            then(dve.reciprocal(G12[:, 2, :], G12[:, 2, :]))
            then(dve.tensor_tensor(G12[:, 3, :], G12[:, 1, :], G12[:, 2, :], ALU.mult))
            for n in range(NCH):
                then(dve.tensor_scalar(GG[:, 0, n, :], iota, IXF[:, n, 0:1], G12[:, 2, n:n + 1], ALU.is_equal, ALU.mult))
                then(dve.tensor_scalar(GG[:, 1, n, :], iota, IXF[:, n, 1:2], G12[:, 3, n:n + 1], ALU.is_equal, ALU.mult))
            for n in range(NCH):
                then(dve.tensor_scalar(MK[:, n, :], iota, IXF[:, n, 0:1], None, ALU.is_equal))
                then(dve.scalar_tensor_tensor(MK[:, n, :], iota, IXF[:, n, 1:2], MK[:, n, :], ALU.is_equal, ALU.add))
            then(dve.memset(MK[TS:P, 4, :], 0.0))
            dve.tensor_tensor(GG[:, 1], GG[:, 0], GG[:, 1], ALU.add).then_inc(S["mk_ready"], 1)
            dve.wait_ge(S["mk_ready"], 1)

        @block.vector
        def _(dve):
            own = [0]

            def then(ins):
                own[0] += 1
                ins.then_inc(S["dve_own"], 1)
                dve.wait_ge(S["dve_own"], own[0])

            def log1p_steps(dst, y, s, s2, add):
                then(dve.tensor_scalar(s, y, 2.0, None, ALU.add))
                then(dve.reciprocal(s, s))
                then(dve.tensor_tensor(s, s, y, ALU.mult))
                then(dve.tensor_tensor(s2, s, s, ALU.mult))
                then(dve.tensor_scalar(dst, s2, LOG1P[0], None, ALU.mult))
                for c in LOG1P[1:]:
                    then(dve.scalar_tensor_tensor(dst, dst, c, s2, ALU.add, ALU.mult))
                then(dve.scalar_tensor_tensor(dst, dst, 1.0, s, ALU.add, ALU.mult))
                then(dve.scalar_tensor_tensor(dst, dst, 2.0, add, ALU.mult, ALU.add))

            def modulation(b):
                dve.wait_ge(S["mod_pe"], ADA_BATCH[b + 1])
                for l in range(L):
                    lo, hi = max(ADA_BATCH[b], l * M_ADA), min(ADA_BATCH[b + 1], (l + 1) * M_ADA)
                    if lo < hi:
                        w = hi - lo
                        tiles = PB[4][:, (lo - ADA_BATCH[b]) * G9:(hi - ADA_BATCH[b]) * G9].rearrange("p (m g) -> p m g", g=G9)
                        lo -= l * M_ADA
                        then(dve.tensor_tensor(MOD[:, l, lo:lo + w], tiles, par("b_ada", l, lo, w).unsqueeze(2).broadcast_to([P, w, G9]), ALU.add))
                for q in [q for q in range(2 * L) if MOD_BATCH[q] == b + 1]:
                    l, w = q // 2, q % 2
                    then(dve.scalar_tensor_tensor(AM[:, q], MOD[:, l, KD * (3 * w + 1):KD * (3 * w + 2), :], 1.0,
                                                  par(f"norm{w + 1}", l, 0, KD).unsqueeze(2).broadcast_to([P, KD, G9]), ALU.add, ALU.mult))
                dve.sem_inc(S["mod_done"], 1)

            def norm_apply(q):
                dve.wait_ge(S["rs_sqrt"], 2 * (q + 1))
                then(dve.reciprocal(RS[:], RS[:]))
                if q == 2 * L:
                    for k in range(KD):
                        dve.scalar_tensor_tensor(hT[:, k, :], xT[:, k, :], FN[:, k:k + 1], RS[:], ALU.mult, ALU.mult).then_inc(S["y_ready"], 1)
                    return
                l, w = q // 2, q % 2
                for k in range(KD):
                    dve.tensor_tensor(hT[:, k, :], xT[:, k, :], RS[:], ALU.mult).then_inc(S["h_mul"], 1)
                dve.wait_ge(S["h_mul"], KD * (q + 1))
                if q == 0:
                    modulation(0)
                hs = hT[:, :, TP:T].rearrange("p k (b s) -> p k b s", s=NS)
                bc = lambda ap: ap.unsqueeze(3).broadcast_to([P, KD, NB, NS])
                then(dve.tensor_tensor(hs, hs, bc(AM[:, q, :, 1:G9]), ALU.mult))
                dve.tensor_tensor(hs, hs, bc(MOD[:, l, 3 * KD * w:3 * KD * w + KD, 1:G9]), ALU.add).then_inc(S["h_small"], 1)

            def residual_at(l, b, m, g0):
                xm = xT[:, m, :] if isinstance(m, int) else xT[:, bass.ds(m, 1), :].rearrange("p a t -> p (a t)")
                gm = MOD[:, l, bass.ds(m + g0, 1), :].rearrange("p a t -> p (a t)")
                dve.scalar_tensor_tensor(xm[:, 0:HN], PM[b][:, 0:HN], gm[:, 0:1], xm[:, 0:HN], ALU.mult, ALU.add).then_inc(free_m[b], 1)
                dve.scalar_tensor_tensor(xm[:, HN:TP], PS[b][:, 0:HP], gm[:, 0:1], xm[:, HN:TP], ALU.mult, ALU.add)
                tmp = TMP[:, b, :]
                dve.tensor_tensor(pv_s(tmp), pv_s(PS[b][:, HP:HN]), gm[:, 1:G9].unsqueeze(2).broadcast_to([P, NB, NS]), ALU.mult).then_inc(free_s[b], 1)
                return xm, tmp

            dve.memset(ONES[:], 1.0).then_inc(S["ones_ready"], 1)
            dve.memset(SM[:], 0.0).then_inc(S["ones_ready"], 1)
            then(dve.memset(ABt[:], 0.0))
            then(dve.memset(EPSC[:, 0:1], EPS))
            then(dve.memset(EPSC[:, 1:2], EPS * P))
            then(dve.memset(LG[:], 0.0))
            dve.wait_ge(S["consts"], 8 * 16)
            o = PC["lru_lambda"][0]
            lam = PA[:, :, o:o + 2]
            dve.scalar_tensor_tensor(LM[:, :, 0, :], lam, -1.0, lam, ALU.mult, ALU.min).then_inc(S["lam_abs"], 1)
            then(dve.tensor_scalar(LM[:, :, 2, :], lam, -1.0, 0.0, ALU.mult, ALU.max))
            dve.wait_ge(S["sp_exp"], 1)
            log1p_steps(LM[:, :, 5, :], LM[:, :, 1, :], LM[:, :, 3, :], LM[:, :, 4, :], LM[:, :, 2, :])
            then(dve.tensor_scalar(LM[:, :, 5, :], LM[:, :, 5, :], 2.0, None, ALU.mult))
            for a, nm in enumerate(("lru_b_a", "lru_b_i")):
                o = PC[nm][0]
                then(dve.tensor_scalar(LM[:, :, 6 + a, :], PA[:, :, o:o + 2], 0.5, None, ALU.mult))
            for l in range(L):
                norm_apply(2 * l)
                mixer_dve(dve, l, then, log1p_steps, modulation)
                f0, per = FILL["out", l], PER["out", l]
                with dve.Fori(0, 2) as j:
                    for s in range(4):
                        m = j * 4 + s
                        dve.wait_ge(S["w_used"], j * (4 * per) + (f0 + per * (s + 1)))
                        xm, tmp = residual_at(l, s % 2, m, 2 * KD)
                        dve.wait_ge(free_m[s % 2], j * 2 + (TILE["out", l] + s) // 2 + 1)
                        dve.wait_ge(free_s[s % 2], j * 2 + (TILE["out", l] + s) // 2 + 1)
                        dve.tensor_tensor(xm[:, TP:T], xm[:, TP:T], tmp, ALU.add).then_inc(S["x_ready"], 2)
                if ADA_OUT[l]:
                    modulation(l + 2)
                norm_apply(2 * l + 1)
                if l % 2 == 0:
                    ffn_dve(dve, l, residual_at)
                else:
                    router_dve(dve, l, then)
                    moe_dve(dve, l, then)
            norm_apply(2 * L)

        @block.gpsimd
        def _(pool):
            own = [0]

            def then(ins):
                own[0] += 1
                ins.then_inc(S["pool_own"], 1)
                pool.wait_ge(S["pool_own"], own[0])
            for l in range(L):
                if l > 0:
                    pool.wait_ge(S["out_states"], 16 * 7 * l)
                    pool.wait_ge(S["x_ready"], X_DONE[2 * l])
                for dst, nm in ((SC[:], "st_a"), (SCQ[:], "st_q"), (ST[:], "st_l")):
                    pool.dma_start(dst, io[nm][l]).then_inc(S["states_in"], 16)
                for h2 in range(2):
                    pool.dma_start(SS[:, 4 * h2:4 * h2 + 4], io["st_d"][l, :, 4 * h2:4 * h2 + 4]).then_inc(S["states_in"], 16)
                then(pool.memset(WL[:], 0.0))
                for a, nm in enumerate(("lru_w_a", "lru_w_i")):
                    for b in range(4):
                        o = 64 * (b % 2)
                        pool.dma_start(WL[o:o + 64, a, b // 2, o:o + 64], io[nm][l, b]).then_inc(S["in_small"], 16)
                pool.wait_ge(S["states_in"], 16 * 5 * (l + 1))
                pads = pj[:, :, SO:CW].rearrange("p m (b c) -> p m b c", c=WQ - 1 + NS)[:, :, :, 0:WQ - 1]
                then(pool.memset(pj[:, :, 0:WQ - 1], 0.0))
                then(pool.memset(pads, 0.0))
                then(pool.tensor_copy(pads[:, LRU_X:LRU_X + 2], SCQ[:, 0:2]))
                then(pool.tensor_copy(pads[:, QKV:ZT], SCQ[:, 2:14]))
                for c in range(2):
                    then(pool.memset(UA[:, c, 0:WA - 1], 0.0))
                    then(pool.tensor_copy(UA[:, c, AO:CA].rearrange("p (b c) -> p b c", c=WA - 1 + NS)[:, :, 0:WA - 1], SC[:, c]))
                pool.sem_inc(S["pads_ready"], 1)
                pool.wait_ge(S["glu_ready"], 4 * (l + 1))
                for c in range(2):
                    then(pool.tensor_copy(NA[:, c], UA[:, c, AO:CA].rearrange("p (b c) -> p b c", c=WA - 1 + NS)[:, :, NS:]))
                pool.dma_start(io["n_a"][l], NA[:]).then_inc(S["out_states"], 16)
                pool.dma_start(io["n_ap"][l], UA[:, :, TP:AO]).then_inc(S["out_states"], 16)
                for i in range(14):
                    m = LRU_X + i if i < 2 else QKV + i - 2
                    pool.wait_ge(free_m[m % 2], (TILE["in", l] + m) // 2 + 1)
                    pool.wait_ge(free_s[m % 2], (TILE["in", l] + m) // 2 + 1)
                    then(pool.tensor_copy(NQ[:, i, 0, :], pj[:, m, TP:SO]))
                    then(pool.tensor_copy(NQ[:, i, 1:G9, :], pj[:, m, SO:CW].rearrange("p (b c) -> p b c", c=WQ - 1 + NS)[:, :, NS:]))
                pool.sem_inc(S["new_states"], 1)
                pool.dma_start(io["n_q"][l], NQ[:]).then_inc(S["out_states"], 16)
                pool.wait_ge(S["lru_new"], l + 1)
                pool.dma_start(io["n_l"][l], SN[:]).then_inc(S["out_states"], 16)
                for n in range(NCH):
                    tok, m, _ = chunk(n)
                    q = NCH * l + n
                    pool.wait_ge(S["eg_ready"], q + 1)
                    if q > 0:
                        pool.wait_ge(S["o_pe"], q)
                    pool.tensor_tensor(w4(2)[:, :, 0:m], QC[:, 0:H, tok], w4(3)[:, :, 0:m], ALU.mult).then_inc(S["qg_ready"], 1)
                pool.wait_ge(S["st_done"], H * 4 * (l + 1))
                pool.dma_start(io["n_dp"][l], SP_[:]).then_inc(S["out_states"], 16)
                pool.wait_ge(S["sm_upd"], H * NB * (l + 1))
                for h2 in range(2):
                    pool.dma_start(io["n_d"][l, :, 4 * h2:4 * h2 + 4], SS[:, 4 * h2:4 * h2 + 4]).then_inc(S["out_states"], 16)
            pool.wait_ge(S["gt_copied"], 1)
            pool.dma_start(scratch, ROWS).then_inc(S["rows_out"], 16)
            pool.wait_ge(S["rows_out"], 16)
            rows = scratch.rearrange("(a p) t -> p a t", a=2)
            pool.dma_start(BR[:, :, :], rows[0:1].broadcast_to([P, 2, T])).then_inc(S["br_landed"], 16)
            rounds = pool.value_load(NR[0:1, 0:1], min_val=1, max_val=ROUNDS)
            with pool.Fori(0, rounds) as rd:
                with pool.Fori(0, NE) as e:
                    p = pool.snap(rd * NE + e)
                    pool.wait_ge(S["st_ready"], p + 1)
                    pool.dma_start(BR[:, :, :], rows[bass.ds(p + 1, 1)].broadcast_to([P, 2, T])).then_inc(S["br_landed"], 16)
            pool.wait_ge(S["out_states"], 16 * 7 * L)
            pool.wait_ge(S["br_landed"], rounds * (16 * NE) + 16)


def _constants(np):
    c = np.zeros((P, C_END), np.float32)
    i = np.arange(P)
    c[:, C_ID:C_ID + P] = np.eye(P)
    c[:, C_TRI:C_TRI + P] = i[:, None] <= i[None, :]
    t = np.arange(TS)
    same = (t[:, None] // NS) == (t[None, :] // NS)
    c[:TS, C_BTRI:C_BTRI + TS] = same & (t[:, None] <= t[None, :])
    c[:TS, C_BONE:C_BONE + TS] = same
    c[:TS, C_BM:C_BM + NB] = (t[:, None] // NS) == np.arange(NB)[None, :]
    c[:, C_IOTA:C_IOTA + NE] = np.arange(NE)
    for v in range(LEVELS):
        blk = i // (1 << v)
        c[:, C_LVL + v * P:C_LVL + (v + 1) * P] = (blk[:, None] % 2 == 0) & (blk[None, :] == blk[:, None] + 1)
    c[:, C_SLOT:C_SLOT + CAP] = np.arange(1, CAP + 1)
    c[:, C_SLOT + CAP:] = np.stack([i + 1, i + 1 + P], 1)
    return c


def _tiles(np, w):
    *b, i, o = w.shape
    w = w.reshape(*b, i // P, P, o // P, P)
    n = len(b)
    return np.ascontiguousarray(np.moveaxis(w, (n + 2, n + 1, n), (n, n + 1, n + 2)))


def _layout(np, a):
    x = np.concatenate([a["x_prompt"][0], a["x_sample"].reshape(TS, D)], 0)
    feat = lambda v: np.moveaxis(v.reshape(*v.shape[:-1], -1, P), -1, 0)
    w_in = a["w_in"]
    parts = np.split(w_in, np.cumsum([256, 256, 1536, 512, H, H, 256]).tolist(), axis=-1)
    a_val, a_gate, qkv, z, b, aa, lx, lg = parts
    w24 = np.concatenate([a_val, a_gate, lx, lg, qkv, z], -1)
    wab = np.concatenate([b, aa], -1).reshape(L, KD, P, 2 * H).transpose(2, 0, 1, 3)
    params = np.zeros((P, L, PCOLS), np.float32)
    def put(name, v):
        o, w = PC[name]
        params[:, :, o:o + w] = v
    for name in ("b_ada", "norm1", "norm2", "conv_a_b", "ln_a_g", "ln_a_b", "conv_lru_b", "lru_b_a", "lru_b_i", "lru_lambda", "lru_norm", "gdn_norm"):
        put(name, feat(a[name]))
    for name in ("conv_a_w", "conv_qkv_w", "conv_lru_w"):
        put(name, feat(a[name]).transpose(0, 1, 3, 2).reshape(P, L, -1))
    put("a_log", np.broadcast_to(a["gdn_a_log"], (P, L, H)))
    put("dt_bias", np.broadcast_to(a["gdn_dt_bias"], (P, L, H)))
    gu = lambda g, u: np.stack([_tiles(np, g), _tiles(np, u)], -4)
    q = feat(np.concatenate([a["state_conv_lru"], a["state_conv_qkv"]], -1))
    dn = _tiles(np, a["ffn_wd"][0]).reshape(KD, P, 2, FE * P).transpose(2, 0, 1, 3)
    out = {
        "consts": _constants(np), "params": params,
        "cT": feat(np.concatenate([a["c_prompt"], a["c_sample"]], 0)).transpose(0, 2, 1),
        "x": feat(x).transpose(0, 2, 1), "wab": wab, "fnorm": feat(a["final_norm"]),
        "rw": a["router_w"][0].reshape(KD, P, NE).transpose(1, 0, 2), "rb": a["router_b"],
        "w_ada": _tiles(np, a["w_ada"]).reshape(L * M_ADA, P, KD * P), "w_in": _tiles(np, w24).reshape(L, M_IN, P, KD * P),
        "w_out": _tiles(np, a["w_out"]).reshape(L, KD, P, KD * P),
        "ffn_gu": gu(a["ffn_wg"][0], a["ffn_wu"][0]).reshape(2 * FF, P, KD * P), "ffn_dn": dn,
        "moe_gu": gu(a["moe_wg"][0], a["moe_wu"][0]).reshape(NE, 2 * FE, P, KD * P),
        "moe_dn": a["moe_wd"][0].reshape(NE, FE, P, D),
        "lru_w_a": a["lru_w_a"], "lru_w_i": a["lru_w_i"],
        "st_a": feat(a["state_conv_a"]).transpose(1, 0, 4, 2, 3), "st_q": q.transpose(1, 0, 4, 2, 3),
        "st_l": feat(a["state_lru"]).transpose(1, 0, 3, 2).reshape(L, P, 2 * NB),
        "st_d": a["state_delta"].transpose(0, 3, 1, 2, 4),
    }
    return {k: np.ascontiguousarray(v) for k, v in out.items()}


_OUT = {"y": (P, KD, T), "n_a": (L, P, 2, NB, WA - 1), "n_ap": (L, P, 2, WA - 1), "n_q": (L, P, 14, G9, WQ - 1),
        "n_l": (L, P, 2 * G9), "n_dp": (L, P, H, P), "n_d": (L, P, NB, H, P)}


def kernel(**inputs):
    import numpy as np
    from concourse import bacc
    from concourse.bass_utils import run_bass_kernel_spmd

    arrays = _layout(np, {k: np.asarray(v) for k, v in inputs.items()})
    nc = bacc.Bacc("TRN2", target_bir_lowering=False, num_devices=1)
    io = {k: nc.dram_tensor("in_" + k, v.shape, F32, kind="ExternalInput").ap() for k, v in arrays.items()}
    io.update({k: nc.dram_tensor("out_" + k, s, F32, kind="ExternalOutput").ap() for k, s in _OUT.items()})
    build(nc, io)
    r = run_bass_kernel_spmd(nc, [{"in_" + k: v for k, v in arrays.items()}], core_ids=[0]).results[0]
    o = {k: np.asarray(r["out_" + k]).reshape(s) for k, s in _OUT.items()}
    y = o["y"].transpose(2, 1, 0).reshape(T, D)
    unfeat = lambda v: v.reshape(*v.shape[:-2], -1)
    a_s = unfeat(o["n_a"].transpose(0, 3, 4, 2, 1))
    a_p = unfeat(o["n_ap"].transpose(0, 3, 2, 1))[:, None]
    q = unfeat(o["n_q"].transpose(0, 3, 4, 2, 1))
    lr = unfeat(o["n_l"].reshape(L, P, 2, G9).transpose(0, 3, 2, 1))
    c = np.ascontiguousarray
    return tuple(c(v) for v in (
        y[None, :TP], y[TP:].reshape(NB, NS, D), a_p, q[:, 0:1, :, 256:], o["n_dp"].transpose(0, 2, 1, 3)[:, None],
        q[:, 0:1, :, :256], lr[:, 0:1], a_s, q[:, 1:, :, 256:], o["n_d"].transpose(0, 2, 3, 1, 4), q[:, 1:, :, :256], lr[:, 1:]))
```

```python
from contextlib import ExitStack

import concourse.bass as bass
from concourse import mybir

F32 = mybir.dt.float32
U32 = mybir.dt.uint32
F32R = mybir.dt.float32r
ALU = mybir.AluOpType
ACT = mybir.ActivationFunctionType
AX_X = mybir.AxisListType.X

P = 128
L = 2
TP = 512
NB = 8
NS = 8
TS = NB * NS
T = TP + TS
HN = T // 2
HP = TP - HN
G9 = NB + 1
D = 1024
KD = D // P
M_ADA = 6 * KD
M_IN = 24
FF = 22
NE = 8
FE = 11
H = 4
WA = 31
WQ = 4
EPS = 1e-6
RING = 4
SLOT = FE * P
WK = KD * P
RING3 = 3
G3 = 2 * FE + KD
GX = 3 * FE
AHEAD = 2
B_MOE = 2 * G3 + AHEAD
CAP = 256
ROUNDS = 3
NPASS = ROUNDS * NE
CW = WQ - 1 + TP + NB * (WQ - 1 + NS)
SO = WQ - 1 + TP
CA = WA - 1 + TP + NB * (WA - 1 + NS)
AO = WA - 1 + TP
A_VAL, A_GATE, LRU_X, LRU_G, QKV, ZT = 0, 2, 4, 6, 8, 20
LEVELS = 7
SLEVELS = 3
NCH = 5
C_ID, C_TRI, C_BTRI, C_BONE, C_BM, C_IOTA, C_LVL = 0, 128, 256, 320, 384, 392, 400
C_SLOT = C_LVL + LEVELS * P
C_END = C_SLOT + CAP + 2
PC = {}
_n = 0
for _name, _w in (("b_ada", M_ADA), ("norm1", KD), ("norm2", KD), ("conv_a_w", 2 * WA), ("conv_qkv_w", 12 * WQ),
                  ("conv_lru_w", 2 * WQ), ("conv_a_b", 2), ("ln_a_g", 2), ("ln_a_b", 2), ("conv_lru_b", 2),
                  ("lru_b_a", 2), ("lru_b_i", 2), ("lru_lambda", 2), ("lru_norm", 2), ("gdn_norm", 1),
                  ("a_log", H), ("dt_bias", H)):
    PC[_name] = (_n, _w)
    _n += _w
PCOLS = _n

M_Z = H
M_CONV = M_IN - M_Z
ADA_WITH, ADA_MID = (2, 1), (KD * 2, 0)
ADA_FIRST = L * M_ADA - sum(ADA_WITH) * M_CONV - sum(ADA_MID)
ADA_BATCH = (0, ADA_FIRST, ADA_FIRST + ADA_WITH[0] * M_CONV, L * M_ADA - ADA_WITH[1] * M_CONV, L * M_ADA)
ADA0 = (ADA_BATCH[1], ADA_BATCH[3])
IN_BATCH = (1, 3)
MOD_BATCH = {0: 1, 1: 2, 2: 3, 3: 4}
FILL, TILE = {}, {}
_f = _t = 0
for _l in range(L):
    _stages = [("ada", ADA_FIRST, 0)] if _l == 0 else []
    _stages += [("in", (1 + ADA_WITH[_l]) * M_CONV, M_CONV), ("z", M_Z, M_Z), ("mid", ADA_MID[_l], 0), ("out", KD, KD)]
    _stages += [("ffn", 0, 2 * G3)] if _l % 2 == 0 else []
    for _s, _nf, _nt in _stages:
        FILL[_s, _l], TILE[_s, _l] = _f, _t
        _f += _nf
        _t += _nt
LOG1P = [1.0 / (2 * i + 1) for i in range(9, 0, -1)]


def build(nc, io):
    ctx = ExitStack()
    with ctx:
        sb = lambda name, shape, dt=F32: ctx.enter_context(nc.sbuf_tensor(name, shape, dt))
        sem = lambda name: ctx.enter_context(nc.semaphore(name))

        xT = sb("xT", [P, KD, T])
        hT = sb("hT", [P, KD, T])
        ring_f = sb("ring", [P, RING3 * SLOT])
        RS = sb("RS", [P, T])
        EPSC = sb("EPSC", [P, 2])
        SQ = sb("SQ", [P, 2, T])
        CO = sb("CO", [P, C_END])
        ONES = sb("ONES", [P, P])
        PA = sb("PA", [P, L, PCOLS])
        CT = sb("CT", [P, KD, G9])
        MOD = sb("MOD", [P, L, M_ADA, G9])
        AM = sb("AM", [P, 2 * L, KD, G9])
        TMP = sb("TMP", [P, 2, TS])
        WAB = sb("WAB", [P, L, KD, 2 * H])
        FN = sb("FN", [P, KD])
        RW = sb("RW", [P, KD, NE])
        RB = sb("RB", [1, NE])
        ST = sb("ST", [P, 2 * NB])
        SN = sb("SN", [P, 2 * G9])
        ABt = sb("ABt", [P, NCH, 2 * H])
        SM = sb("SM", [P, 16, NCH * H])
        LM = sb("LM", [P, L, 8, 2])
        LG = sb("LG", [P, NCH, NE])
        MX = sb("MX", [P, NCH, NE])
        IX = sb("IX", [P, NCH, NE], U32)
        IXF = sb("IXF", [P, NCH, 2])
        GG = sb("GG", [P, 2, NCH, NE])
        G12 = sb("G12", [P, 4, NCH])
        ELS = sb("ELS", [P, NB, H])
        GSEL = sb("GSEL", [TS, NB, H])
        MK = sb("MK", [P, NCH, NE])
        PF = sb("PF", [P, 2, NCH, NE])
        OV = sb("OV", [P, 4])
        NR = sb("NR", [1, 1], U32)
        PG = sb("PG", [P, NCH, 2, NPASS + 1])
        GS = sb("GS", [P, 2])

        with ExitStack() as mixers:
            mixer_sb = lambda name, shape: mixers.enter_context(nc.sbuf_tensor(name, shape, F32))
            PJ = mixer_sb("PJ", [P, M_IN * CW])
            UA = mixer_sb("UA", [P, 2, CA])
            QC = mixer_sb("QC", [P, 12, T])
            XA = mixer_sb("XA", [P, 2, T])
            XL = mixer_sb("XL", [P, 2, T])
            SPR = mixer_sb("SPR", [P, H, P])
            SS = mixer_sb("SS", [P, NB, H, P])
            SC = mixer_sb("SC", [P, 2, NB, WA - 1])
            SCQ = mixer_sb("SCQ", [P, 14, NB, WQ - 1])
            NA = mixer_sb("NA", [P, 2, NB, WA - 1])
            NQ = mixer_sb("NQ", [P, 14, G9, WQ - 1])
            MROW = mixer_sb("MROW", [G9, 2, P])
            WL = mixer_sb("WL", [P, 2, 2, P])
        with ExitStack() as dense:
            split_sb = lambda name, shape: dense.enter_context(nc.sbuf_tensor(name, shape, F32R))
            HH, HL = split_sb("HH", [P, KD, T]), split_sb("HL", [P, KD, T])
            AH, AL = split_sb("AH", [P, FE, T]), split_sb("AL", [P, FE, T])
            VH, VL = split_sb("VH", [P, RING3, SLOT]), split_sb("VL", [P, RING3, SLOT])
        HTH, HTL = sb("HTH", [P, NCH, D], F32R), sb("HTL", [P, NCH, D], F32R)
        XH, XLow = sb("XH", [P, KD, CAP], F32R), sb("XLow", [P, KD, CAP], F32R)
        BH, BL = sb("BH", [P, FE, CAP], F32R), sb("BL", [P, FE, CAP], F32R)
        YH, YL = sb("YH", [P, 2, D], F32R), sb("YL", [P, 2, D], F32R)
        TOK_SLOT = sb("TOK_SLOT", [P, NCH, CAP], F32R)
        SLOT_TOK = sb("SLOT_TOK", [P, 2, T], F32R)
        UH, UL = sb("UH", [P, RING3, WK], F32R), sb("UL", [P, RING3, WK], F32R)
        scratch = nc.dram_tensor("gate_rows", (2 * (NPASS + 1), T), F32, kind="Internal").ap()

        PB = [ctx.enter_context(nc.psum_tensor(f"PB{i}", [P, 512], F32)) for i in range(8)]
        ROW = [PB[7 - b][0:G9, 0:P] for b in range(2)]
        MID_ROW = [PB[2 * b][0:G9, 0:P] for b in range(2)]
        PM, PS = [PB[0], PB[2]], [PB[1], PB[3]]

        pj = PJ[:, :].rearrange("p (m c) -> p m c", c=CW)
        ring = ring_f[:, 0:RING * WK].rearrange("p (s c) -> p s c", s=RING)
        raw3 = lambda s, w: ring_f[:, s * SLOT:s * SLOT + w]
        hf = hT[:].rearrange("p k t -> p (k t)")
        AF = hf[:, 0:2 * T].rearrange("p (b t) -> p b t", b=2)
        BR = hf[:, 2 * T:4 * T].rearrange("p (a t) -> p a t", a=2)
        JUNK = hf[:, 4 * T:5 * T]
        ROWS = hf[0:2 * (NPASS + 1), 5 * T:6 * T]
        f32 = lambda ap: ap.bitcast(F32)
        work0 = QKV * CW
        def wk(i, n=1):
            return PJ[:, work0 + i * 512:work0 + (i + n) * 512]
        w4 = lambda i: wk(i).rearrange("p (h c) -> p h c", h=H)
        diag_g, diag_b = [PJ[:, i * 512:(i + 1) * 512].rearrange("p (h c) -> p h c", h=H) for i in range(2)]
        NORMS = H + 1

        def norm_part(u):
            w = TP if u < H else H * TS
            sq = SQ[:, :, 0:w] if u % 2 == 0 else PJ[:, 2 * 512:2 * 512 + 2 * w].rearrange("p (i t) -> p i t", i=2)
            root = RS[:, 0:w] if u % 2 == 0 else PJ[:, 4 * 512:4 * 512 + w]
            return w, sq, root, PB[(0, 4, 0, 4, 5)[u]]
        lw = lambda i: PJ[:, work0 + i * 2 * T:work0 + (i + 1) * 2 * T].rearrange("p (c t) -> p c t", c=2)
        ident, tri = CO[:, C_ID:C_ID + P], CO[:, C_TRI:C_TRI + P]
        btri, bone = CO[0:TS, C_BTRI:C_BTRI + TS], CO[0:TS, C_BONE:C_BONE + TS]
        bm, iota = CO[0:TS, C_BM:C_BM + NB], CO[:, C_IOTA:C_IOTA + NE]
        lvl = lambda v, n: CO[0:n, C_LVL + v * P:C_LVL + v * P + n]
        par = lambda name, l, i=0, w=1: PA[:, l, PC[name][0] + i:PC[name][0] + i + w]
        pv_s = lambda ap: ap.rearrange("p (b s) -> p b s", s=NS)

        names = """ab_gates ab_pe af_ready ah_ready al_ready bc_pe bf_ready bh_ready bl_ready br_landed c_act cnt_pe
            consts conv_a conv_l conv_q dd_exp dd_min dd_ready diag_ready dve_own eg_ready free_m0 free_m1
            free_s0 free_s1 gat_pe gate_exp gc_pe gelu_ready glu_ready gt_copied gt_pe h_main h_mul h_small
            hh_ready hl_ready ht_pe hth_ready htl_ready in_small kq_pe ks_copied ks_pe ks_tr kt_pe l2_pe l2_sq
            l2_sqrt lam_abs lg_copied lg_exp lg_pe lg_rows ln_done ln_mean ln_sq ln_sub ln_sum ln_used lru_g_pe
            lru_new lru_scan lru_sqrt lru_t lru_tz mat_pe mk_ready mod_done mod_pe moe_done new_states nr_ready
            o_copied o_pe on_pe on_scaled on_sq on_sqrt ones_ready out_done out_states p_copied p_pe pads_ready
            pg_ready pool_own q_silu qg_ready r_ready rk_ready row_out rows_out rs_sqrt s_ready sc_pe silu_z
            sm_mask sm_pe sm_upd small_exp small_exp2 small_ready small_tanh sp_exp sp_zero sq_ready sq_used
            st_done st_own st_pe st_ready states_in t_done t_pe tr_evac um_ready vn_copied vn_pe vt_pe w3_used
            w_used wh_ready wl_ready x_ready y_ready ya_ready yb_ready yc_pe yc_ready yc_sq yc_sqrt yh_ready
            yl_ready""".split()
        S = {n: sem(n) for n in names}
        landed = [sem(f"landed{i}") for i in range(RING)]
        landed3 = [sem(f"landed3_{i}") for i in range(RING3)]
        fb = [sem(f"bank_free{i}") for i in range(4)]
        free_m, free_s = [S["free_m0"], S["free_m1"]], [S["free_s0"], S["free_s1"]]
        block = ctx.enter_context(nc.Block())

        def slot_of(f0, s):
            return (f0 + s) % RING

        def wait_landed(eng, f0, s, j):
            eng.wait_ge(landed[(f0 + s) % RING], (j + ((f0 + s) // RING + 1)) * 16)

        @block.sync
        def _(sp):
            first = (("consts", CO), ("params", PA), ("cT", CT), ("x", xT), ("wab", WAB), ("fnorm", FN), ("rw", RW), ("rb", RB))
            for name, dst in first:
                sp.dma_start(dst[:], io[name]).then_inc(S["consts"], 16)

            def stream(src, f0, nf, rnd, guard=True):
                with sp.Fori(0, nf // rnd) as j:
                    for s in range(rnd):
                        if guard:
                            sp.wait_ge(S["w_used"], j * rnd + (f0 + s - RING + 1))
                        sp.dma_start(ring[:, slot_of(f0, s), :], src(j, s)).then_inc(landed[slot_of(f0, s)], 16)
            for l in range(L):
                if l == 0:
                    stream(lambda j, s: io["w_ada"][s], 0, RING, RING, guard=False)
                    stream(lambda j, s: io["w_ada"][j * RING + (RING + s)], RING, ADA_FIRST - RING, RING)
                na = ADA_WITH[l]
                def source(j, s):
                    if s % (na + 1) == na:
                        return io["w_in"][l, j * 4 + s // (na + 1)]
                    return io["w_ada"][j * (4 * na) + (ADA0[l] + s // (na + 1) * na + s % (na + 1))]
                stream(source, FILL["in", l], (na + 1) * M_CONV, 4 * (na + 1))
                stream(lambda j, s: io["w_in"][l, M_CONV + s], FILL["z", l], M_Z, M_Z)
                if ADA_MID[l]:
                    stream(lambda j, s: io["w_ada"][j * 4 + (ADA_BATCH[2] + s)], FILL["mid", l], ADA_MID[l], 4)
                stream(lambda j, s: io["w_out"][l, j * 4 + s], FILL["out", l], KD, 4)
                def fill3(src, w, s, used):
                    if used is not None:
                        sp.wait_ge(S["wl_ready"], used)
                    sp.dma_start(raw3(s % RING3, w), src).then_inc(landed3[s % RING3], 16)

                sp.wait_ge(S["w_used"], FILL["out", l] + KD)
                if l % 2 == 0:
                    for hv in range(2):
                        for i in range(G3):
                            g = hv * G3 + i
                            src, w = (io["ffn_gu"][hv * 2 * FE + i], WK) if i < 2 * FE else (io["ffn_dn"][hv, i - 2 * FE], SLOT)
                            fill3(src, w, g, g - 2 if g > 2 else None)
                    for i in range(AHEAD):
                        fill3(io["ffn_gu"][i], WK, 2 * G3 + i, 2 * G3 + i - 2)
                    sp.wait_ge(S["wl_ready"], B_MOE)
                else:
                    sp.wait_ge(S["nr_ready"], 1)
                    rounds = sp.value_load(NR[0:1, 0:1], min_val=1, max_val=ROUNDS)
                    with sp.Fori(0, rounds) as rd:
                        with sp.Fori(0, NE) as e:
                            for i in range(GX):
                                src = io["moe_gu"][e, i] if i < 2 * FE else io["moe_dn"][e, i - 2 * FE]
                                fill3(src, WK, B_MOE + i, rd * (NE * GX) + e * GX + (B_MOE + i - 2))
                    for i in range(AHEAD):
                        sp.wait_ge(S["wl_ready"], rounds * (NE * GX) + (B_MOE + i - 2))
                        sp.dma_start(raw3((B_MOE + i) % RING3, WK), io["moe_gu"][0, i]).then_inc(landed3[(B_MOE + i) % RING3], 16)
            sp.wait_ge(S["y_ready"], KD)
            sp.dma_start(io["y"], hT[:]).then_inc(S["out_done"], 16)
            sp.wait_ge(S["out_done"], 16)

        def chunk(n):
            return (slice(n * P, n * P + P), P, LEVELS) if n < 4 else (slice(TP, T), TS, SLEVELS)

        BANK_P, BANK_T = (6, 4), (7, 0)
        pair = lambda ap: ap.rearrange("p (a h c) -> p a h c", a=2, h=2)
        tg = lambda g: pair(wk(9 + g))
        inv_t = lambda hh: tg(hh // 2)[:, 0, hh % 2, :]
        inv_tt = lambda hh: tg(hh // 2)[:, 1, hh % 2, :]

        LVL_ALL = [(n, v) for n in range(NCH) for v in range(chunk(n)[2])]

        def ada_mms(pe, slot, b, row=None):
            for k in range(KD):
                end = pe.matmul((row or ROW)[b], CT[:, k, :], ring[:, slot, k * P:(k + 1) * P], start=(k == 0), stop=(k == KD - 1))
            end.then_inc(S["w_used"], 1)

        def ada_turn(pe, b, done, col):
            pe.wait_ge(S["row_out"], done)
            pe.matmul(PB[4][:, col], MROW[:, b, :], ident[0:G9, 0:G9], start=True, stop=True).then_inc(S["mod_pe"], 1)

        def mixer_pe(pe, l, z_tile):
            mm = pe.matmul
            pe.wait_ge(S["conv_l"], 2 * (l + 1))
            pe.wait_ge(S["in_small"], 16 * 8 * (l + 1))
            for c in range(2):
                for a in range(2):
                    if 2 * c + a > 0:
                        pe.wait_ge(S["lru_t"], 4 * l + 2 * c + a)
                    mm(PB[5][:, 0:HN], WL[:, a, c, :], XL[:, c, 0:HN], start=True, stop=True)
                    mm(PB[6][:, 0:HN], WL[:, a, c, :], XL[:, c, HN:T], start=True, stop=True).then_inc(S["lru_g_pe"], 1)
                if c == 0:
                    z_tile(0)
            pe.wait_ge(S["lru_t"], 4 * (l + 1))
            for r in range(2):
                for c in range(2):
                    if r == 0:
                        pe.wait_ge(S["conv_a"], 2 * l + c + 1)
                        src = XA[:, c, :]
                    else:
                        pe.wait_ge(S["ln_sub"], 2 * (l + 1))
                        pe.wait_ge(S["ln_sq"], 2 * l + c + 1)
                        src = SQ[:, c, :]
                    mm(PB[5][:, 0:HN], ONES[:], src[:, 0:HN], start=(c == 0), stop=(c == 1))
                    end = mm(PB[6][:, 0:HN], ONES[:], src[:, HN:T], start=(c == 0), stop=(c == 1))
                end.then_inc(S["ln_sum"], 1)
                if r == 0:
                    z_tile(1)
            pe.wait_ge(S["small_ready"], 4 * l + 2)
            g = SM[:, 3, :]
            mm(PB[7][:, 64:80], tri, g[:, 0:16], start=True, stop=True)
            mm(PB[7][0:TS, 80:84], btri, g[0:TS, 16:20], start=True, stop=True)
            mm(PB[7][:, 84:100], ONES[:], g[:, 0:16], start=True, stop=True)
            mm(PB[7][0:TS, 100:104], bone, g[0:TS, 16:20], start=True, stop=True)
            mm(PB[7][:, 104:136], ONES[0:TS, :], GSEL[:].rearrange("p b h -> p (b h)"), start=True, stop=True).then_inc(S["gc_pe"], 1)
            z_tile(2)
            z_tile(3)
            pe.wait_ge(S["ln_mean"], 2 * (l + 1))
            for c in range(2):
                pe.wait_ge(S["yc_sq"], 2 * l + c + 1)
                mm(PB[5][:, 0:HN], ONES[:], SQ[:, c, 0:HN], start=(c == 0), stop=(c == 1))
                end = mm(PB[6][:, 0:HN], ONES[:], SQ[:, c, HN:T], start=(c == 0), stop=(c == 1))
            end.then_inc(S["yc_pe"], 1)
            for b in range(2):
                pe.wait_ge(free_m[b], (TILE["z", l] + M_Z) // 2)
                pe.wait_ge(free_s[b], (TILE["z", l] + M_Z) // 2)
            for hh in range(H):
                pe.wait_ge(S["l2_sq"], H * l + hh + 1)
                for n in range(NCH):
                    tok, m, _ = chunk(n)
                    end = mm(PB[1][0:m, n * H + hh:n * H + hh + 1], SQ[:, hh % 2, tok], ONES[:, 0:1], start=True, stop=True)
                end.then_inc(S["l2_pe"], 1)
            for i in range(ADA_MID[l]):
                if i == 0:
                    pe.wait_ge(S["mod_done"], IN_BATCH[l] + 1)
                wait_landed(pe, FILL["mid", l], i, 0)
                ada_mms(pe, slot_of(FILL["mid", l], i), i % 2, MID_ROW)
                if i > 0:
                    ada_turn(pe, (i - 1) % 2, ADA_BATCH[2] + i, slice((i - 1) * G9, i * G9))
                if i == ADA_MID[l] - 1:
                    ada_turn(pe, i % 2, ADA_BATCH[2] + i + 1, slice(i * G9, (i + 1) * G9))
            pe.wait_ge(S["l2_sqrt"], 2 * (l + 1))
            pe.wait_ge(S["yc_sqrt"], 2 * (l + 1))
            pe.wait_ge(S["q_silu"], 12 * (l + 1))
            b4 = lambda i, rows=P, w=P: PB[i][0:rows, 0:H * w].rearrange("p (h c) -> p h c", h=H)

            def decays_and_k(n):
                tok, m, _ = chunk(n)
                pe.wait_ge(S["diag_ready"], NCH * l + n + 1)
                mm(PB[6][:, 0:H * m], ONES[0:m, :], diag_g[0:m, :, 0:m], start=True, stop=True).then_inc(S["bc_pe"], 1)
                for hh in range(H):
                    end = pe.transpose(b4(0, m)[:, hh, :], QC[:, H + hh, tok], ident)
                end.then_inc(S["kt_pe"], 1)

            def kk_and_v(n):
                tok, m, _ = chunk(n)
                mm(PB[5][0:m, 0:H * m], ONES[0:m, 0:m], diag_b[0:m, :, 0:m], start=True, stop=True)
                for hh in range(H):
                    end = mm(b4(7, m, m)[:, hh, :], QC[:, H + hh, tok], QC[:, H + hh, tok], start=True, stop=True)
                end.then_inc(S["mat_pe"], 1)
                for hh in range(H):
                    end = pe.transpose(b4(1, m)[:, hh, :], QC[:, 2 * H + hh, tok], ident)
                end.then_inc(S["vt_pe"], 1)

            def kq(n):
                tok, m, _ = chunk(n)
                for hh in range(H):
                    end = mm(b4(2, m, m)[:, hh, :], QC[:, H + hh, tok], QC[:, hh, tok], start=True, stop=True)
                end.then_inc(S["kq_pe"], 1)

            def norm_sum(u):
                w, sq, _, bank = norm_part(u)
                pe.wait_ge(S["on_sq"], NORMS * l + u + 1)
                mm(bank[:, 0:w], ONES[:], sq[:, 0], start=True, stop=False)
                mm(bank[:, 0:w], ONES[:], sq[:, 1], start=False, stop=True).then_inc(S["on_pe"], 1)
            decays_and_k(0)
            kk_and_v(0)
            kq(0)
            for n in range(NCH):
                tok, m, levels = chunk(n)
                q = NCH * l + n
                kT = lambda hh: QC[:, H + hh, tok]
                for v in range(levels):
                    z = sum(chunk(i)[2] for i in range(n)) + v + len(LVL_ALL) * l
                    pe.wait_ge(S["um_ready"], z + 1)
                    if v == 0:
                        pe.wait_ge(S["tr_evac"], 2 * (q + 1))
                        if n > 0:
                            pe.wait_ge(S["st_done"], H * 4 * l + H * n)
                    um = w4(7 + v % 2)
                    for g in range(2):
                        if v > 0:
                            pe.wait_ge(S["t_done"], 2 * z + g - 1)
                        for hh in (2 * g, 2 * g + 1):
                            end = mm(PB[BANK_P[g]][0:m, hh % 2 * P:hh % 2 * P + m], um[0:m, hh, 0:m],
                                     ident[0:m, 0:m] if v == 0 else inv_t(hh)[0:m, 0:m], start=True, stop=True)
                        end.then_inc(S["p_pe"], 1)
                    if v == 0:
                        continue
                    for g in range(2):
                        pe.wait_ge(S["p_copied"], 2 * (z - q) + g - 1)
                        out = pair(PB[BANK_T[g]])
                        for hh in (2 * g, 2 * g + 1):
                            if v < levels - 1:
                                mm(out[0:m, 0, hh % 2, 0:m], inv_tt(hh)[0:m, 0:m], w4(11)[0:m, hh, 0:m], start=True, stop=True)
                            end = mm(out[0:m, 1, hh % 2, 0:m], w4(11)[0:m, hh, 0:m], inv_tt(hh)[0:m, 0:m], start=True, stop=True)
                        end.then_inc(S["t_pe"], 1)
                z1 = sum(chunk(i)[2] for i in range(n + 1)) + len(LVL_ALL) * l
                pe.wait_ge(S["t_done"], 2 * z1)
                pe.wait_ge(S["dd_ready"], q + 1)
                if n < 4:
                    if n == 0:
                        pe.wait_ge(S["sp_zero"], l + 1)
                    for hh in range(H):
                        end = mm(b4(1, m)[:, hh, :], kT(hh), SPR[:, hh, :], start=True, stop=True)
                    end.then_inc(S["ks_pe"], 1)
                else:
                    pe.wait_ge(S["states_in"], 16 * 5 * (l + 1))
                    for hh in range(H):
                        if hh == 2:
                            norm_sum(0)
                            norm_sum(1)
                        for b in range(NB):
                            end = mm(b4(1, P, m)[:, hh, b * NS:(b + 1) * NS], SS[:, b, hh, :], QC[:, H + hh, TP + b * NS:TP + (b + 1) * NS],
                                     start=True, stop=True)
                    end.then_inc(S["ks_pe"], 1)
                    pe.wait_ge(S["ks_copied"], l + 1)
                    for hh in range(H):
                        end = pe.transpose(b4(5, m)[:, hh, :], w4(11)[:, hh, 0:m], ident)
                    end.then_inc(S["ks_tr"], 1)
                if n < 4:
                    decays_and_k(n + 1)
                pe.wait_ge(S["r_ready"], q + 1)
                for hh in range(H):
                    end = mm(b4(2, m)[:, hh, :], inv_tt(hh)[0:m, 0:m], w4(12)[0:m, hh, :], start=True, stop=True)
                end.then_inc(S["vn_pe"], 1)
                if n < 4:
                    kk_and_v(n + 1)
                else:
                    norm_sum(2)
                    norm_sum(3)
                pe.wait_ge(S["vn_copied"], q + 1)
                pe.wait_ge(S["qg_ready"], q + 1)
                if q > 0:
                    pe.wait_ge(S["o_copied"], q)
                for hh in range(H):
                    o = b4(3, P, m)[:, hh, :]
                    end = mm(o, w4(13)[0:m, hh, :], w4(6)[0:m, hh, 0:m], start=True, stop=False, skip_group_check=True)
                    if n < 4:
                        end = mm(o, SPR[:, hh, :], w4(2)[:, hh, 0:m], start=False, stop=True, skip_group_check=True)
                    else:
                        for b in range(NB):
                            end = mm(o[:, b * NS:(b + 1) * NS], SS[:, b, hh, :], w4(2)[:, hh, b * NS:(b + 1) * NS],
                                     start=False, stop=True, skip_group_check=True)
                end.then_inc(S["o_pe"], 1)
                if n < 4:
                    for hh in range(H):
                        end = mm(b4(4)[:, hh, :], w4(0)[:, hh, :], w4(13)[:, hh, :], start=True, stop=True)
                    end.then_inc(S["st_pe"], 1)
                    kq(n + 1)
                else:
                    for b in range(NB):
                        pe.wait_ge(S["sm_mask"], NB * l + b + 1)
                        if b >= 2:
                            pe.wait_ge(S["sm_upd"], H * (NB * l + b - 1))
                        for hh in range(H):
                            end = mm(b4(6 + b % 2)[:, hh, :], w4(7 + b % 2)[0:TS, hh, :], w4(13)[0:TS, hh, :], start=True, stop=True)
                        end.then_inc(S["sm_pe"], 1)
                        if b == 2:
                            norm_sum(4)
            pe.wait_ge(S["on_sqrt"], NORMS * (l + 1))
            pe.wait_ge(S["o_copied"], NCH * (l + 1))

        def three(pe, out, a, b, first, last):
            pe.matmul(out, a[0], b[0], start=first, stop=False)
            pe.matmul(out, a[0], b[1], start=False, stop=False)
            return pe.matmul(out, a[1], b[0], start=False, stop=last)

        def ffn_pe(pe, l):
            t0 = TILE["ffn", l]
            with pe.Fori(0, 2) as hv:
                for i in range(G3):
                    b, s, t = i % 2, i % RING3, t0 + i
                    pe.wait_ge(S["wl_ready"], hv * G3 + (i + 1))
                    pe.wait_ge(free_m[b], hv * (G3 // 2) + t // 2)
                    pe.wait_ge(free_s[b], hv * (G3 // 2) + t // 2)
                    gu = i < 2 * FE
                    nk, ah, al = (KD, HH, HL) if gu else (FE, AH, AL)
                    for k in range(nk):
                        if gu and i == 0:
                            pe.wait_ge(S["hl_ready"], k + 1)
                        if i == 2 * FE:
                            pe.wait_ge(S["al_ready"], hv * FE + (k + 1))
                        w = [v[:, s, k * P:(k + 1) * P] for v in (VH, VL)]
                        for c, bank in ((slice(0, HN), PM[b]), (slice(HN, T), PS[b])):
                            end = three(pe, bank[:, 0:HN], w, (ah[:, k, c], al[:, k, c]), k == 0, k == nk - 1)
                    end.then_inc(S["w3_used"], 1)
            pe.wait_ge(S["wl_ready"], B_MOE)
            pe.wait_ge(S["w3_used"], 2 * G3)
            pe.sem_inc(S["w3_used"], AHEAD)

        def router_pe(pe, l):
            mm = pe.matmul
            for h2, (bank, tok) in enumerate(((PB[5], slice(0, HN)), (PB[6], slice(HN, T)))):
                for k in range(KD):
                    if h2 == 0:
                        pe.wait_ge(S["rs_sqrt"], 2 * (2 * l + 2))
                        pe.wait_ge(S["h_main"], KD * (2 * l + 1) + k + 1)
                    else:
                        pe.wait_ge(S["h_small"], 2 * l + 2)
                    end = mm(bank[0:NE, 0:HN], RW[:, k, :], hT[:, k, tok], start=(k == 0), stop=(k == KD - 1))
                end.then_inc(S["lg_rows"], 1)

            def by_token(n):
                tok = slice(n * P, min((n + 1) * P, T))
                m = tok.stop - tok.start
                if n > 1:
                    pe.wait_ge(S["htl_ready"], 2 * (n - 1))
                for k in range(KD):
                    bank = PB[2 * (n % 2) + k // 4]
                    end = pe.transpose(bank[0:m, (k % 4) * P:(k % 4 + 1) * P], hT[:, k, tok], ident)
                end.then_inc(S["ht_pe"], 1)
            by_token(0)
            pe.wait_ge(S["lg_copied"], 2)
            for n in range(NCH):
                tok = slice(n * P, min((n + 1) * P, T))
                out = PB[4][0:tok.stop - tok.start, n * NE:(n + 1) * NE]
                mm(out, SQ[0:NE, 0, tok], ident[0:NE, 0:NE], start=True, stop=False)
                end = mm(out, ONES[0:1, 0:tok.stop - tok.start], RB[:], start=False, stop=True)
            end.then_inc(S["lg_pe"], 1)
            for n in range(1, NCH):
                by_token(n)
            pe.wait_ge(S["mk_ready"], 1)
            for n in range(NCH):
                for j in range(n + 1):
                    mm(PB[5][:, n * NE:(n + 1) * NE], tri if j == n else ONES[:], MK[:, j, :], start=(j == 0), stop=(j == n))
                for j in range(n - n % 2, n + 1):
                    mm(PB[5][:, (5 + n) * NE:(6 + n) * NE], tri if j == n else ONES[:], MK[:, j, :], start=(j == n - n % 2), stop=(j == n))
            for j in range(NCH):
                end = mm(PB[5][:, 80:88], ONES[:], MK[:, j, :], start=(j == 0), stop=(j == NCH - 1))
            end.then_inc(S["cnt_pe"], 1)
            pe.wait_ge(S["pg_ready"], 1)
            for n in range(NCH):
                m = min((n + 1) * P, T) - n * P
                w = 2 * (NPASS + 1)
                out = PB[6][0:w, n * P:n * P + m] if n < 4 else PB[7][0:w, 0:m]
                end = pe.transpose(out, PG[0:m, n].rearrange("p a c -> p (a c)"), ident[0:m, 0:m])
            end.then_inc(S["gt_pe"], 1)

        def bank_uses():
            n, uses = [0] * 4, {}
            def use(key, b):
                uses[key] = (b, n[b])
                n[b] += 1
            for i in range(2 * FE):
                use(("gu", i), i % 4)
            for k in range(KD):
                use(("hi", k), k % 2)
                use(("lo", k), 2 + k % 2)
            for m in range(KD):
                use(("sa", m), 2 * (m % 2))
                use(("sb", m), 2 * (m % 2) + 1)
            return uses, n
        USE, USES = bank_uses()
        FIRST = [KD // 2] * 4

        def gather_pe(pe, p, first=False):
            for k in range(KD):
                for part, src in (("hi", HTH), ("lo", HTL)):
                    b, u = USE[part, k]
                    if not first:
                        pe.wait_ge(fb[b], p * USES[b] + (FIRST[b] + u))
                    elif k > 1:
                        pe.wait_ge(fb[b], k // 2)
                    for n in range(NCH):
                        end = pe.matmul(PB[b][:, 0:CAP], src[:, n, k * P:(k + 1) * P], TOK_SLOT[:, n, :], start=(n == 0), stop=(n == NCH - 1))
                    end.then_inc(S["gat_pe"], 1)

        def gather_done(pe, p, k):
            for b in (k % 2, 2 + k % 2):
                pe.wait_ge(fb[b], p * USES[b] + (FIRST[b] - KD // 2 + k // 2 + 1))

        def moe_pe(pe, l):
            pe.wait_ge(S["hth_ready"], 2 * NCH)
            pe.wait_ge(S["htl_ready"], 2 * NCH)
            pe.wait_ge(S["nr_ready"], 1)
            rounds = pe.value_load(NR[0:1, 0:1], min_val=1, max_val=ROUNDS)
            pe.wait_ge(S["s_ready"], 1)
            gather_pe(pe, 0, first=True)
            with pe.Fori(0, rounds) as rd:
                with pe.Fori(0, NE) as e:
                    p = pe.snap(rd * NE + e)
                    for i in range(GX):
                        s = (B_MOE + i) % RING3
                        pe.wait_ge(S["wl_ready"], p * GX + (B_MOE + i + 1))
                        w = (UH[:, s, :], UL[:, s, :])
                        if i < 2 * FE:
                            b, u = USE["gu", i]
                            pe.wait_ge(fb[b], p * USES[b] + (FIRST[b] + u))
                            for k in range(KD):
                                if i == 0:
                                    gather_done(pe, p, k)
                                wk_ = [v[:, k * P:(k + 1) * P] for v in w]
                                end = three(pe, PB[b][:, 0:CAP], wk_, (XH[:, k, :], XLow[:, k, :]), k == 0, k == KD - 1)
                        else:
                            kk = i - 2 * FE
                            pe.wait_ge(S["bl_ready"], p * FE + (kk + 1))
                            for j in range(2):
                                a = [v[:, kk, j * P:(j + 1) * P] for v in (BH, BL)]
                                for c in range(2):
                                    end = three(pe, PB[4 + 2 * j + c][:, :], a, [v[:, c * 512:(c + 1) * 512] for v in w], kk == 0, kk == FE - 1)
                        end.then_inc(S["w3_used"], 1)
                    pe.wait_ge(S["s_ready"], p + 2)
                    gather_pe(pe, p)
                    pe.wait_ge(S["st_ready"], p + 1)
                    pe.wait_ge(S["yh_ready"], p * 4 + 4)
                    pe.wait_ge(S["yl_ready"], p * 4 + 4)
                    for m in range(KD):
                        for part, c in (("sa", slice(0, HN)), ("sb", slice(HN, T))):
                            b, u = USE[part, m]
                            pe.wait_ge(fb[b], p * USES[b] + (FIRST[b] + u))
                            for j in range(2):
                                pe.matmul(PB[b][:, 0:HN], YH[:, j, m * P:(m + 1) * P], SLOT_TOK[:, j, c], start=(j == 0), stop=False)
                                end = pe.matmul(PB[b][:, 0:HN], YL[:, j, m * P:(m + 1) * P], SLOT_TOK[:, j, c], start=False, stop=(j == 1))
                        end.then_inc(S["sc_pe"], 1)

        @block.tensor
        def _(pe):
            mm = pe.matmul

            def norm_sums(q):
                if q == 0:
                    pe.wait_ge(S["ones_ready"], 2)
                for k in range(KD):
                    pe.wait_ge(S["sq_ready"], KD * q + k + 1)
                    mm(PB[5][:, 0:HN], ONES[:], SQ[:, k % 2, 0:HN], start=(k == 0), stop=(k == KD - 1))
                    mm(PB[6][:, 0:HN], ONES[:], SQ[:, k % 2, HN:T], start=(k == 0), stop=(k == KD - 1)).then_inc(S["sq_used"], 1)

            def tile_mms(slot, b):
                for k in range(KD):
                    w = ring[:, slot, k * P:(k + 1) * P]
                    mm(PM[b][:, 0:HN], w, hT[:, k, 0:HN], start=(k == 0), stop=(k == KD - 1))
                    end = mm(PS[b][:, 0:HN], w, hT[:, k, HN:T], start=(k == 0), stop=(k == KD - 1))
                end.then_inc(S["w_used"], 1)

            def wait_free(b, count):
                pe.wait_ge(free_m[b], count)
                pe.wait_ge(free_s[b], count)

            def gemm(l, stage, nt):
                f0, t0 = FILL[stage, l], TILE[stage, l]
                na = ADA_WITH[l] if stage == "in" else 0
                per = 1 + na
                def rnd(j, peeled):
                    for s in range(4):
                        for i in range(na):
                            wait_landed(pe, f0, per * s + i, j * per)
                            ada_mms(pe, slot_of(f0, per * s + i), (na * s + i) % 2)
                        wait_landed(pe, f0, per * s + na, j * per)
                        if not (peeled and t0 + s < 2):
                            wait_free(s % 2, j * 2 + (t0 + s) // 2)
                        tile_mms(slot_of(f0, per * s + na), s % 2)
                        for i in range(na):
                            n = na * s + i
                            ada_turn(pe, n % 2, j * (4 * na) + (ADA0[l] + n + 1), bass.ds(j * (4 * na * G9) + n * G9, G9))
                if t0 == 0:
                    rnd(0, True)
                with pe.Fori(1 if t0 == 0 else 0, nt // 4) as j:
                    rnd(j, False)

            for l in range(L):
                norm_sums(2 * l)
                if l == 0:
                    pe.wait_ge(S["c_act"], 1)
                    pe.wait_ge(S["rs_sqrt"], 2)
                    for i in range(ADA_FIRST):
                        wait_landed(pe, 0, i, 0)
                        ada_mms(pe, i % RING, i % 2)
                        if i > 0:
                            ada_turn(pe, (i - 1) % 2, i, slice((i - 1) * G9, i * G9))
                    ada_turn(pe, i % 2, i + 1, slice(i * G9, (i + 1) * G9))
                pe.wait_ge(S["h_main"], KD * (2 * l + 1))
                pe.wait_ge(S["h_small"], 2 * l + 1)
                gemm(l, "in", M_CONV)
                for n in range(NCH):
                    tok = slice(n * P, min((n + 1) * P, T))
                    m = tok.stop - tok.start
                    for k in range(KD):
                        end = mm(PB[7][0:m, n * 8:n * 8 + 8], hT[:, k, tok], WAB[:, l, k, :], start=(k == 0), stop=(k == KD - 1))
                end.then_inc(S["ab_pe"], 1)

                def z_tile(i):
                    wait_landed(pe, FILL["z", l], i, 0)
                    wait_free(i % 2, (TILE["z", l] + i) // 2)
                    tile_mms(slot_of(FILL["z", l], i), i % 2)
                mixer_pe(pe, l, z_tile)
                pe.wait_ge(S["ya_ready"], 2 * (l + 1))
                pe.wait_ge(S["yb_ready"], NORMS * (l + 1))
                pe.wait_ge(S["yc_ready"], 2 * (l + 1))
                gemm(l, "out", KD)
                norm_sums(2 * l + 1)
                if l % 2 == 0:
                    ffn_pe(pe, l)
                else:
                    router_pe(pe, l)
                    moe_pe(pe, l)
            norm_sums(2 * L)

        def mixer_act(act, l, z_out, row_out):
            fn = act.activation
            for fr in free_m + free_s:
                act.wait_ge(fr, TILE["z", l] // 2)
            for i in range(12):
                act.wait_ge(S["conv_q"], 12 * l + i + 1)
                fn(QC[:, i, :], QC[:, i, :], ACT.Silu).then_inc(S["q_silu"], 1)
            act.wait_ge(S["ab_gates"], l + 1)
            fn(SM[:, 1, :], SM[:, 0, :], ACT.Exp).then_inc(S["small_exp"], 1)
            fn(SM[:, 11, :].rearrange("p (n h) -> p n h", h=H), ABt[:, :, 0:H], ACT.Tanh, scale=0.5).then_inc(S["small_tanh"], 1)
            fn(SM[:, 12, 0:H], par("a_log", l, 0, H), ACT.Exp).then_inc(S["small_tanh"], 1)
            act.wait_ge(S["new_states"], l + 1)
            for c in range(2):
                for a in range(2):
                    act.wait_ge(S["lru_g_pe"], 4 * l + 2 * c + a + 1)
                    bias = LM[:, l, 6 + a, c:c + 1]
                    fn(lw(a)[:, c, 0:HN], PB[5][:, 0:HN], ACT.Tanh, scale=0.5, bias=bias)
                    fn(lw(a)[:, c, HN:T], PB[6][:, 0:HN], ACT.Tanh, scale=0.5, bias=bias).then_inc(S["lru_t"], 1)
                if c == 0:
                    z_out(0)
            act.wait_ge(S["lru_t"], 4 * (l + 1))
            for c in range(2):
                fn(lw(2)[:, c, :], lw(0)[:, c, :], ACT.Tanh, scale=LM[:, l, 5, c:c + 1], bias=LM[:, l, 5, c:c + 1]).then_inc(S["lru_tz"], 1)
            for c in range(2):
                act.wait_ge(S["ln_sub"], 2 * l + c + 1)
                fn(SQ[:, c, :], XA[:, c, :], ACT.Square).then_inc(S["ln_sq"], 1)
            act.wait_ge(S["lru_tz"], 2 * (l + 1))
            fn(lw(4)[:], lw(2)[:], ACT.Sqrt).then_inc(S["lru_sqrt"], 1)
            z_out(1)
            act.wait_ge(S["ln_sum"], 2 * l + 2)
            fn(RS[:, 0:HN], PB[5][:, 0:HN], ACT.Sqrt, scale=1.0 / 256, bias=EPSC[:, 0:1]).then_inc(S["ln_mean"], 1)
            fn(RS[:, HN:T], PB[6][:, 0:HN], ACT.Sqrt, scale=1.0 / 256, bias=EPSC[:, 0:1]).then_inc(S["ln_mean"], 1)
            for c in range(2):
                fn(pj[:, LRU_G + c, SO - TP:CW], pj[:, LRU_G + c, SO - TP:CW], ACT.Gelu_apprx_tanh).then_inc(S["gelu_ready"], 1)
            z_out(2)
            z_out(3)
            for c in range(2):
                act.wait_ge(S["lru_scan"], 2 * l + c + 1)
                fn(SQ[:, c, :], lw(3)[:, c, :], ACT.Square).then_inc(S["yc_sq"], 1)
            act.wait_ge(S["yc_pe"], l + 1)
            act.wait_ge(S["ln_used"], l + 1)
            fn(RS[:, 0:HN], PB[5][:, 0:HN], ACT.Sqrt, scale=1.0 / 256, bias=EPSC[:, 0:1]).then_inc(S["yc_sqrt"], 1)
            fn(RS[:, HN:T], PB[6][:, 0:HN], ACT.Sqrt, scale=1.0 / 256, bias=EPSC[:, 0:1]).then_inc(S["yc_sqrt"], 1)
            for hh in range(H):
                act.wait_ge(S["q_silu"], 12 * l + H + hh + 1)
                if hh >= 2:
                    act.wait_ge(S["l2_pe"], H * l + hh - 1)
                fn(SQ[:, hh % 2, :], QC[:, H + hh, :], ACT.Square).then_inc(S["l2_sq"], 1)
            act.wait_ge(S["l2_pe"], H * (l + 1))
            fn(SM[:, 13, 0:16], PB[1][:, 0:16], ACT.Sqrt, bias=EPSC[:, 0:1]).then_inc(S["l2_sqrt"], 1)
            fn(SM[0:TS, 13, 16:20], PB[1][0:TS, 16:20], ACT.Sqrt, bias=EPSC[0:TS, 0:1]).then_inc(S["l2_sqrt"], 1)
            act.wait_ge(S["small_ready"], 4 * l + 3)
            fn(SM[:, 6, :], SM[:, 4, :], ACT.Exp).then_inc(S["small_exp2"], 1)
            fn(SM[:, 8, :], SM[:, 7, :], ACT.Exp).then_inc(S["small_exp2"], 1)
            fn(SM[:, 9, :], SM[:, 5, :], ACT.Exp).then_inc(S["small_exp2"], 1)
            fn(ELS[:], ELS[:], ACT.Exp).then_inc(S["small_exp2"], 1)
            for i in range(ADA_MID[l]):
                row_out(i % 2, FILL["mid", l] + i + 1, MID_ROW)
            for c in range(2):
                act.wait_ge(S["ln_done"], 2 * l + c + 1)
                fn(hT[:, c, :], XA[:, c, :], ACT.Silu, scale=par("ln_a_g", l, c), bias=par("ln_a_b", l, c)).then_inc(S["ya_ready"], 1)
            for fr in free_m + free_s:
                act.wait_ge(fr, (TILE["z", l] + M_Z) // 2)
            fn(pj[:, ZT:ZT + H, SO - TP:CW], pj[:, ZT:ZT + H, SO - TP:CW], ACT.Silu).then_inc(S["silu_z"], 1)
            b4 = lambda i, rows=P, w=P: PB[i][0:rows, 0:H * w].rearrange("p (h c) -> p h c", h=H)

            def exp_decay(n):
                m, q = chunk(n)[1], NCH * l + n
                act.wait_ge(S["bc_pe"], q + 1)
                if q > 0:
                    act.wait_ge(S["qg_ready"], q)
                fn(w4(3)[:, :, 0:m], b4(6, P, m), ACT.Exp).then_inc(S["eg_ready"], 1)

            def exp_pairs(n):
                m, q = chunk(n)[1], NCH * l + n
                act.wait_ge(S["dd_min"], q + 1)
                fn(w4(4)[0:m, :, 0:m], w4(4)[0:m, :, 0:m], ACT.Exp).then_inc(S["dd_exp"], 1)

            def scaled(n, bank, dst, i, ready):
                m = chunk(n)[1]
                act.wait_ge(ready, NCH * l + n + 1)
                for hh in range(H):
                    e = fn(dst[0:m, hh, :], b4(bank, m)[:, hh, :], ACT.Copy, scale=SM[0:m, i, n * H + hh:n * H + hh + 1])
                e.then_inc(S["tr_evac"], 1)

            def norm_squares(u):
                act.wait_ge(S["o_copied"], NCH * l + (4 if u < H else NCH))
                if u >= 2:
                    act.wait_ge(S["on_pe"], NORMS * l + u - 1)
                sq = norm_part(u)[1]
                heads, tok = (slice(u, u + 1), slice(0, TP)) if u < H else (slice(0, H), slice(TP, T))
                view = lambda i: sq[:, i].rearrange("p (h t) -> p h t", h=heads.stop - heads.start)
                fn(view(0), QC[:, heads, tok], ACT.Square, scale=P * EPS ** 0.5)
                fn(view(1), hT[:, 2 + heads.start:2 + heads.stop, tok], ACT.Square).then_inc(S["on_sq"], 1)

            def norm_root(u):
                w, _, root, bank = norm_part(u)
                act.wait_ge(S["on_pe"], NORMS * l + u + 1)
                if u >= 2:
                    act.wait_ge(S["on_scaled"], NORMS * l + u - 1)
                else:
                    act.wait_ge(S["yc_ready"], 2 * (l + 1))
                fn(root, bank[:, 0:w], ACT.Sqrt, scale=1.0 / P, bias=EPSC[:, 1:2]).then_inc(S["on_sqrt"], 1)
            act.wait_ge(S["rk_ready"], l + 1)
            exp_decay(0)
            scaled(0, 1, w4(1), 2, S["vt_pe"])
            scaled(0, 0, w4(0), 8, S["kt_pe"])
            exp_pairs(0)
            for n in range(NCH):
                tok, m, levels = chunk(n)
                q = NCH * l + n
                for v in range(1, levels):
                    z = sum(chunk(i)[2] for i in range(n)) + v + len(LVL_ALL) * l
                    for g in range(2):
                        act.wait_ge(S["p_pe"], 2 * z + g + 1)
                        fn(w4(11)[0:m, 2 * g:2 * g + 2, 0:m], PB[BANK_P[g]][0:m, 0:2 * P].rearrange("p (h c) -> p h c", h=2)[:, :, 0:m],
                           ACT.Copy).then_inc(S["p_copied"], 1)
                if n == 4:
                    for u in range(2):
                        norm_squares(u)
                    for u in range(2):
                        norm_root(u)
                    act.wait_ge(S["ks_pe"], q + 1)
                    fn(w4(11)[:, :, 0:m], b4(1, P, m), ACT.Copy).then_inc(S["ks_copied"], 1)
                    for u in range(2, 4):
                        norm_squares(u)
                if n < 4:
                    exp_decay(n + 1)
                act.wait_ge(S["vn_pe"], q + 1)
                fn(w4(13)[0:m], b4(2, m), ACT.Copy).then_inc(S["vn_copied"], 1)
                if n < 4:
                    exp_pairs(n + 1)
                    scaled(n + 1, 1, w4(1), 2, S["vt_pe"])
                else:
                    for u in range(2, 4):
                        norm_root(u)
                act.wait_ge(S["o_pe"], q + 1)
                fn(hT[:, 2:2 + H, tok], b4(3, P, m), ACT.Copy).then_inc(S["o_copied"], 1)
                if n < 4:
                    act.wait_ge(S["st_pe"], 4 * l + n + 1)
                    scaled(n + 1, 0, w4(0), 8, S["kt_pe"])
            norm_squares(4)
            norm_root(4)

        X_DONE = {1: 2 * KD, 2: 6 * KD, 3: 8 * KD}

        def split_high(act, raw, high, s, g, last_use):
            act.wait_ge(landed3[s], g[1])
            if last_use is not None:
                act.wait_ge(S["w3_used"], last_use)
            act.activation(high, raw, ACT.Copy).then_inc(S["wh_ready"], 1)

        def ffn_act(act, l):
            fn, t0, q = act.activation, TILE["ffn", l], 2 * l + 1
            act.wait_ge(S["h_small"], q + 1)
            act.wait_ge(S["out_states"], 16 * 7 * (l + 1))
            act.wait_ge(S["x_ready"], X_DONE[q])

            def high(hv, i, first=False):
                s, w = i % RING3, WK if i % G3 < 2 * FE else SLOT
                split_high(act, raw3(s, w), VH[:, s, 0:w], s, (None, (hv * (G3 // RING3) + (i // RING3 + 1)) * 16),
                           None if first else hv * G3 + (i - 2))
            for i in range(AHEAD):
                high(0, i, first=True)
            for k in range(KD):
                act.wait_ge(S["h_main"], KD * q + k + 1)
                fn(HH[:, k, :], hT[:, k, :], ACT.Copy).then_inc(S["hh_ready"], 1)
            with act.Fori(0, 2) as hv:
                for i in range(G3):
                    if i > 0:
                        high(hv, i + AHEAD)
                    if i >= 2 * FE:
                        continue
                    pair, t = i // 2, t0 + i
                    if i % 2 == 0:
                        act.wait_ge(S["w3_used"], hv * G3 + (i + 1))
                        act.wait_ge(free_m[1], hv * (G3 // 2) + (t // 2 - 1))
                        act.wait_ge(free_s[1], hv * (G3 // 2) + (t // 2 - 1))
                        fn(SQ[:, pair % 2, 0:HN], PM[0][:, 0:HN], ACT.Silu).then_inc(free_m[0], 1)
                        fn(SQ[:, pair % 2, HN:T], PS[0][:, 0:HN], ACT.Silu).then_inc(free_s[0], 1)
                        if i == 0:
                            high(hv, AHEAD, first=True)
                    else:
                        act.wait_ge(S["af_ready"], hv * FE + (pair + 1))
                        fn(AH[:, pair, :], AF[:, pair % 2, :], ACT.Copy).then_inc(S["ah_ready"], 1)

        def moe_act(act, l):
            fn, q = act.activation, 2 * l + 1
            for h2 in range(2):
                act.wait_ge(S["lg_rows"], h2 + 1)
                fn(SQ[0:NE, 0, h2 * HN:(h2 + 1) * HN], PB[5 + h2][0:NE, 0:HN], ACT.Copy).then_inc(S["lg_copied"], 1)
            act.wait_ge(S["out_states"], 16 * 7 * (l + 1))
            for n in range(NCH):
                if n == NCH - 1:
                    act.wait_ge(S["lg_exp"], 1)
                    fn(G12[:, 1, :], G12[:, 0, :], ACT.Exp).then_inc(S["gate_exp"], 1)
                m = min((n + 1) * P, T) - n * P
                act.wait_ge(S["ht_pe"], n + 1)
                for c in range(2):
                    fn(HTH[0:m, n, c * 512:(c + 1) * 512], PB[2 * (n % 2) + c][0:m, :], ACT.Copy).then_inc(S["hth_ready"], 1)
            act.wait_ge(S["nr_ready"], 1)
            rounds = act.value_load(NR[0:1, 0:1], min_val=1, max_val=ROUNDS)

            def high(p, i):
                s = (B_MOE + i) % RING3
                split_high(act, raw3(s, WK), UH[:, s, :], s, (None, (p * (GX // RING3) + ((B_MOE + i) // RING3 + 1)) * 16), p * GX + (B_MOE + i - 2))

            def gather_high(p1):
                for k in range(KD):
                    act.wait_ge(S["gat_pe"], p1 * (2 * KD) + (2 * k + 1))
                    fn(XH[:, k, :], PB[k % 2][:, 0:CAP], ACT.Copy).then_inc(fb[k % 2], 1)
            for i in range(AHEAD):
                s = (B_MOE + i) % RING3
                split_high(act, raw3(s, WK), UH[:, s, :], s, (None, ((B_MOE + i) // RING3 + 1) * 16), B_MOE + i - 2)
            gather_high(0)
            with act.Fori(0, rounds) as rd:
                with act.Fori(0, NE) as e:
                    p = act.snap(rd * NE + e)
                    for i in range(GX):
                        high(p, i + AHEAD)
                        if i >= 2 * FE:
                            continue
                        pair = i // 2
                        if i % 2 == 0:
                            act.wait_ge(S["w3_used"], p * GX + (B_MOE + i + 1))
                            if pair >= 2:
                                act.wait_ge(S["bf_ready"], p * FE + (pair - 1))
                            fn(SQ[:, pair % 2, 0:CAP], PB[i % 4][:, 0:CAP], ACT.Silu).then_inc(fb[i % 4], 1)
                        else:
                            act.wait_ge(S["bf_ready"], p * FE + (pair + 1))
                            fn(BH[:, pair, :], AF[:, pair % 2, 0:CAP], ACT.Copy).then_inc(S["bh_ready"], 1)
                    act.wait_ge(S["w3_used"], p * GX + (B_MOE + GX))
                    act.wait_ge(S["st_ready"], p + 1)
                    for j in range(2):
                        for c in range(2):
                            fn(YH[:, j, c * 512:(c + 1) * 512], PB[4 + 2 * j + c][:, :], ACT.Copy, scale=GS[:, j:j + 1]).then_inc(S["yh_ready"], 1)
                    gather_high(p + 1)

        @block.scalar
        def _(act):
            fn = act.activation

            def squares(q):
                if q == 0:
                    act.wait_ge(S["consts"], 8 * 16)
                elif q == 2 * L:
                    act.wait_ge(S["moe_done"], 1)
                for k in range(KD):
                    if 0 < q < 2 * L:
                        act.wait_ge(S["x_ready"], X_DONE[q] - 2 * (KD - 1 - k))
                    if KD * q + k >= 2:
                        act.wait_ge(S["sq_used"], KD * q + k - 1)
                    fn(SQ[:, k % 2, :], xT[:, k, :], ACT.Square).then_inc(S["sq_ready"], 1)

            def root(q):
                act.wait_ge(S["sq_used"], KD * (q + 1))
                fn(RS[:, 0:HN], PB[5][:, 0:HN], ACT.Sqrt, scale=1.0 / D, bias=EPSC[:, 0:1]).then_inc(S["rs_sqrt"], 1)
                fn(RS[:, HN:T], PB[6][:, 0:HN], ACT.Sqrt, scale=1.0 / D, bias=EPSC[:, 0:1]).then_inc(S["rs_sqrt"], 1)

            def row_out(b, used, row=None):
                act.wait_ge(S["w_used"], used)
                fn(MROW[:, b, :], (row or ROW)[b], ACT.Copy).then_inc(S["row_out"], 1)

            def tile_out(row, b):
                fn(row[:, WQ - 1:WQ - 1 + HN], PM[b][:, 0:HN], ACT.Copy).then_inc(free_m[b], 1)
                fn(row[:, WQ - 1 + HN:SO], PS[b][:, 0:HP], ACT.Copy)
                smp = row[:, SO:CW].rearrange("p (b c) -> p b c", c=WQ - 1 + NS)[:, :, WQ - 1:]
                fn(smp, pv_s(PS[b][:, HP:HN]), ACT.Copy).then_inc(free_s[b], 1)

            def modulate(q):
                l, w = q // 2, q % 2
                act.wait_ge(S["mod_done"], MOD_BATCH[q])
                for k in range(KD):
                    act.wait_ge(S["h_mul"], KD * q + k + 1)
                    fn(hT[:, k, 0:TP], hT[:, k, 0:TP], ACT.Identity, scale=AM[:, q, k, 0:1], bias=MOD[:, l, 3 * KD * w + k, 0:1]).then_inc(S["h_main"], 1)

            act.wait_ge(S["consts"], 8 * 16)
            act.wait_ge(S["ones_ready"], 2)
            fn(CT[:], CT[:], ACT.Silu).then_inc(S["c_act"], 1)
            act.wait_ge(S["lam_abs"], 1)
            fn(LM[:, :, 1, :], LM[:, :, 0, :], ACT.Exp).then_inc(S["sp_exp"], 1)
            for l in range(L):
                squares(2 * l)
                root(2 * l)
                if l == 0:
                    for i in range(ADA_FIRST):
                        row_out(i % 2, i + 1)
                modulate(2 * l)
                f0 = FILL["in", l]
                act.wait_ge(S["pads_ready"], l + 1)
                na = ADA_WITH[l]
                per = na + 1
                for s in range(4):
                    for i in range(na):
                        row_out((na * s + i) % 2, f0 + per * s + i + 1)
                    act.wait_ge(S["w_used"], f0 + per * (s + 1))
                    func = ACT.Copy if s < 2 else ACT.Tanh
                    smp = pj[:, s, SO:CW].rearrange("p (b c) -> p b c", c=WQ - 1 + NS)[:, :, WQ - 1:]
                    fn(pj[:, s, WQ - 1:WQ - 1 + HN], PM[s % 2][:, 0:HN], func, scale=0.5).then_inc(free_m[s % 2], 1)
                    fn(pj[:, s, WQ - 1 + HN:SO], PS[s % 2][:, 0:HP], func, scale=0.5)
                    fn(smp, pv_s(PS[s % 2][:, HP:HN]), func, scale=0.5).then_inc(free_s[s % 2], 1)
                with act.Fori(1, M_CONV // RING) as j:
                    for s in range(RING):
                        for i in range(na):
                            row_out((na * s + i) % 2, j * (4 * per) + (f0 + per * s + i + 1))
                        act.wait_ge(S["w_used"], j * (4 * per) + (f0 + per * (s + 1)))
                        tile_out(PJ[:, bass.ds((j * RING + s) * CW, CW)], s % 2)

                def z_out(i):
                    act.wait_ge(S["w_used"], FILL["z", l] + i + 1)
                    tile_out(PJ[:, (ZT + i) * CW:(ZT + i + 1) * CW], i % 2)
                mixer_act(act, l, z_out, row_out)
                squares(2 * l + 1)
                root(2 * l + 1)
                modulate(2 * l + 1)
                if l % 2 == 0:
                    ffn_act(act, l)
                else:
                    moe_act(act, l)
            squares(2 * L)
            root(2 * L)

        def mixer_dve(dve, l, then, log1p_steps, modulation):
            t0 = TILE["in", l]
            for c in range(2):
                dve.wait_ge(free_s[c], t0 // 2 + 2)
                sv = lambda ap: ap.rearrange("p (b c) -> p b c", c=WQ - 1 + NS)[:, :, WQ - 1:]
                dve.scalar_tensor_tensor(UA[:, c, WA - 1:AO], pj[:, A_GATE + c, WQ - 1:SO], 1.0, pj[:, A_VAL + c, WQ - 1:SO], ALU.add, ALU.mult).then_inc(S["glu_ready"], 1)
                us = UA[:, c, AO:CA].rearrange("p (b c) -> p b c", c=WA - 1 + NS)[:, :, WA - 1:]
                dve.scalar_tensor_tensor(us, sv(pj[:, A_GATE + c, SO:CW]), 1.0, sv(pj[:, A_VAL + c, SO:CW]), ALU.add, ALU.mult).then_inc(S["glu_ready"], 1)
            dve.wait_ge(S["glu_ready"], 4 * (l + 1))
            dve.wait_ge(S["pads_ready"], l + 1)

            def conv(dst, src, so, width, w, bias, last_sem):
                step = width - 1 + NS
                for k in range(width):
                    smp = src[:, so:].rearrange("p (b c) -> p b c", c=step)[:, :, k:k + NS]
                    wk_ = w[:, k:k + 1]
                    if k == 0 and bias is not None:
                        a = dve.tensor_scalar(dst[:, 0:TP], src[:, 0:TP], wk_, bias, ALU.mult, ALU.add)
                        then(a)
                        a = dve.tensor_scalar(pv_s(dst[:, TP:T]), smp, wk_, bias, ALU.mult, ALU.add)
                    elif k == 0:
                        a = dve.tensor_scalar(dst[:, 0:TP], src[:, 0:TP], wk_, None, ALU.mult)
                        then(a)
                        a = dve.tensor_scalar(pv_s(dst[:, TP:T]), smp, wk_, None, ALU.mult)
                    else:
                        a = dve.scalar_tensor_tensor(dst[:, 0:TP], src[:, k:k + TP], wk_, dst[:, 0:TP], ALU.mult, ALU.add)
                        then(a)
                        a = dve.scalar_tensor_tensor(pv_s(dst[:, TP:T]), smp, wk_, pv_s(dst[:, TP:T]), ALU.mult, ALU.add)
                    if k < width - 1:
                        then(a)
                a.then_inc(last_sem, 1)

            for c in range(2):
                o = PC["conv_a_w"][0] + c * WA
                conv(XA[:, c, :], UA[:, c, :], AO, WA, PA[:, l, o:o + WA], par("conv_a_b", l, c), S["conv_a"])
            for c in range(2):
                dve.wait_ge(free_s[c], t0 // 2 + 3)
                o = PC["conv_lru_w"][0] + c * WQ
                conv(XL[:, c, :], pj[:, LRU_X + c, :], SO, WQ, PA[:, l, o:o + WQ], par("conv_lru_b", l, c), S["conv_l"])
            for i in range(12):
                dve.wait_ge(free_s[i % 2], (t0 + QKV + i) // 2 + 1)
                o = PC["conv_qkv_w"][0] + i * WQ
                conv(QC[:, i, :], pj[:, QKV + i, :], SO, WQ, PA[:, l, o:o + WQ], None, S["conv_q"])
            dve.wait_ge(S["conv_q"], 12 * (l + 1))
            modulation(IN_BATCH[l])
            dve.wait_ge(S["ab_pe"], l + 1)
            then(dve.tensor_copy(ABt[:, 0:4, :], PB[7][:, 0:32].rearrange("p (n c) -> p n c", c=8)))
            then(dve.tensor_copy(ABt[0:TS, 4, :], PB[7][0:TS, 32:40]))
            sm = lambda i: SM[:, i, :]
            v3 = lambda i: SM[:, i, :].rearrange("p (n h) -> p n h", h=H)
            b3 = lambda ap: ap.unsqueeze(1).broadcast_to([P, NCH, H])
            then(dve.tensor_tensor(v3(10), ABt[:, :, H:2 * H], b3(par("dt_bias", l, 0, H)), ALU.add))
            dve.scalar_tensor_tensor(sm(0), sm(10), -1.0, sm(10), ALU.mult, ALU.min).then_inc(S["ab_gates"], 1)
            then(dve.tensor_scalar(sm(10), sm(10), 0.0, None, ALU.max))
            dve.wait_ge(S["small_exp"], l + 1)
            dve.wait_ge(S["small_tanh"], 2 * (l + 1))
            log1p_steps(sm(3), sm(1), sm(13), sm(14), sm(10))
            then(dve.tensor_tensor(v3(3), v3(3), b3(SM[:, 12, 0:H]), ALU.mult))
            then(dve.tensor_scalar(sm(3), sm(3), -1.0, None, ALU.mult))
            dve.tensor_scalar(sm(2), sm(11), 0.5, 0.5, ALU.mult, ALU.add).then_inc(S["small_ready"], 1)
            dve.tensor_tensor(GSEL[:], SM[0:TS, 3, 16:20].unsqueeze(1).broadcast_to([TS, NB, H]),
                              bm.unsqueeze(2).broadcast_to([TS, NB, H]), ALU.mult).then_inc(S["small_ready"], 1)
            dve.wait_ge(S["ln_sum"], 2 * l + 1)
            for c in range(2):
                then(dve.scalar_tensor_tensor(XA[:, c, 0:HN], PB[5][:, 0:HN], -1.0 / 256, XA[:, c, 0:HN], ALU.mult, ALU.add))
                dve.scalar_tensor_tensor(XA[:, c, HN:T], PB[6][:, 0:HN], -1.0 / 256, XA[:, c, HN:T], ALU.mult, ALU.add).then_inc(S["ln_sub"], 1)
            dve.wait_ge(S["lru_sqrt"], l + 1)
            tr, ti, tz, hs, sq = lw(0), lw(1), lw(2), lw(3), lw(4)
            then(dve.tensor_scalar(tr, tz, 1.0, None, ALU.add))
            then(dve.reciprocal(tr, tr))
            then(dve.tensor_scalar(tz, tz, -1.0, 1.0, ALU.mult, ALU.add))
            then(dve.tensor_tensor(tz, tz, tr, ALU.mult))
            then(dve.tensor_tensor(sq, sq, tr, ALU.mult))
            then(dve.scalar_tensor_tensor(ti, ti, 1.0, XL[:], ALU.add, ALU.mult))
            then(dve.tensor_tensor(sq, sq, ti, ALU.mult))
            a0 = tz[:, :, TP:T].rearrange("p c (b s) -> p c b s", s=NS)[:, :, :, 0]
            b0 = sq[:, :, TP:T].rearrange("p c (b s) -> p c b s", s=NS)[:, :, :, 0]
            t0_ = SN[:, 0:2 * NB].rearrange("p (c b) -> p c b", c=2)
            dve.wait_ge(S["states_in"], 16 * 5 * (l + 1))
            then(dve.tensor_tensor(t0_, a0, ST[:].rearrange("p (c b) -> p c b", c=2), ALU.mult))
            then(dve.tensor_tensor(b0, b0, t0_, ALU.add))
            then(dve.memset(a0, 0.0))
            for c in range(2):
                then(dve.tensor_tensor_scan(hs[:, c, :], tz[:, c, :], sq[:, c, :], 0.0, ALU.mult, ALU.add))
            sn = SN[:].rearrange("p (c g) -> p c g", c=2)
            then(dve.tensor_copy(sn[:, :, 0:1], hs[:, :, TP - 1:TP]))
            dve.tensor_copy(sn[:, :, 1:G9], hs[:, :, TP:T].rearrange("p c (b s) -> p c b s", s=NS)[:, :, :, NS - 1]).then_inc(S["lru_new"], 1)
            dve.wait_ge(S["lru_new"], l + 1)
            dve.wait_ge(S["gelu_ready"], 2 * (l + 1))
            for c in range(2):
                then(dve.tensor_tensor(hs[:, c, 0:TP], hs[:, c, 0:TP], pj[:, LRU_G + c, SO - TP:SO], ALU.mult))
                gs = pj[:, LRU_G + c, SO:CW].rearrange("p (b c) -> p b c", c=WQ - 1 + NS)[:, :, WQ - 1:]
                dve.tensor_tensor(pv_s(hs[:, c, TP:T]), pv_s(hs[:, c, TP:T]), gs, ALU.mult).then_inc(S["lru_scan"], 1)
            dve.wait_ge(S["ln_mean"], 2 * (l + 1))
            then(dve.reciprocal(RS[:], RS[:]))
            for c in range(2):
                ins = dve.tensor_tensor(XA[:, c, :], XA[:, c, :], RS[:], ALU.mult)
                ins.then_inc(S["ln_done"], 1)
            dve.wait_ge(S["ln_done"], 2 * (l + 1))
            dve.sem_inc(S["ln_used"], 1)
            dve.wait_ge(S["gc_pe"], l + 1)
            then(dve.tensor_copy(SM[:, 4, 0:16], PB[7][:, 64:80]))
            then(dve.tensor_copy(SM[0:TS, 4, 16:20], PB[7][0:TS, 80:84]))
            then(dve.tensor_copy(SM[:, 5, 0:16], PB[7][:, 84:100]))
            then(dve.tensor_copy(SM[0:TS, 5, 16:20], PB[7][0:TS, 100:104]))
            then(dve.tensor_copy(ELS[:].rearrange("p b h -> p (b h)"), PB[7][:, 104:136]))
            dve.tensor_tensor(sm(7), sm(5), sm(4), ALU.subtract).then_inc(S["small_ready"], 1)
            dve.wait_ge(S["lru_scan"], 2 * (l + 1))
            dve.wait_ge(S["yc_sqrt"], 2 * (l + 1))
            then(dve.reciprocal(RS[:], RS[:]))
            for c in range(2):
                dve.scalar_tensor_tensor(hT[:, 6 + c, :], hs[:, c, :], par("lru_norm", l, c), RS[:], ALU.mult, ALU.mult).then_inc(S["yc_ready"], 1)
            dve.wait_ge(S["yc_ready"], 2 * (l + 1))
            dve.wait_ge(S["small_exp2"], 4 * (l + 1))
            dve.scalar_tensor_tensor(sm(15), sm(2), -1.0, sm(6), ALU.mult, ALU.mult).then_inc(S["small_ready"], 1)
            dve.wait_ge(S["l2_sqrt"], 2 * (l + 1))
            dve.wait_ge(S["small_exp2"], 4 * (l + 1))
            then(dve.reciprocal(sm(13), sm(13)))
            then(dve.tensor_tensor(sm(8), sm(8), sm(13), ALU.mult))
            then(dve.tensor_tensor(sm(14), sm(2), sm(13), ALU.mult))
            dve.tensor_tensor(sm(15), sm(15), sm(13), ALU.mult).then_inc(S["rk_ready"], 1)
            dve.wait_ge(S["rk_ready"], l + 1)
            dve.memset(SPR[:], 0.0).then_inc(S["sp_zero"], 1)
            if ADA_MID[l]:
                modulation(2)
            b4 = lambda i, rows=P, w=P: PB[i][0:rows, 0:H * w].rearrange("p (h c) -> p h c", h=H)

            def decay_pairs(n):
                m, q = chunk(n)[1], NCH * l + n
                dd = w4(4)[0:m, :, 0:m]
                dve.wait_ge(S["eg_ready"], q + 1)
                then(dve.tensor_tensor(dd, b4(6, m, m), SM[0:m, 4, n * H:(n + 1) * H].unsqueeze(2).broadcast_to([m, H, m]), ALU.subtract))
                dve.tensor_scalar(dd, dd, 0.0, None, ALU.min).then_inc(S["dd_min"], 1)

            def weights(n):
                m, q = chunk(n)[1], NCH * l + n
                mask = tri if n < 4 else btri
                dd, uu, qd = w4(4)[0:m, :, 0:m], w4(5)[0:m, :, 0:m], w4(6)[0:m, :, 0:m]
                dve.wait_ge(S["dd_exp"], q + 1)
                for hh in range(H):
                    ins = dve.scalar_tensor_tensor(dd[:, hh], dd[:, hh], SM[0:m, 13, n * H + hh:n * H + hh + 1], mask[0:m, :], ALU.mult, ALU.mult)
                then(ins)
                dve.wait_ge(S["mat_pe"], q + 1)
                then(dve.tensor_tensor(uu, b4(7, m, m), dd, ALU.mult))
                then(dve.tensor_tensor(uu, uu, b4(5, m, m), ALU.mult))
                dve.wait_ge(S["kq_pe"], q + 1)
                if q > 0:
                    dve.wait_ge(S["o_pe"], q)
                dve.tensor_tensor(qd, b4(2, m, m), dd, ALU.mult).then_inc(S["dd_ready"], 1)

            def norm_apply_part(u):
                root = norm_part(u)[2]
                dve.wait_ge(S["on_sqrt"], NORMS * l + u + 1)
                then(dve.reciprocal(root, root))
                dve.wait_ge(S["silu_z"], l + 1)
                if u < H:
                    o, z = hT[:, 2 + u, 0:TP], pj[:, ZT + u, SO - TP:SO]
                    dve.scalar_tensor_tensor(o, o, par("gdn_norm", l), root, ALU.mult, ALU.mult).then_inc(S["on_scaled"], 1)
                else:
                    o = hT[:, 2:2 + H, TP:T]
                    dve.scalar_tensor_tensor(o, o, par("gdn_norm", l), root.rearrange("p (h t) -> p h t", h=H), ALU.mult, ALU.mult).then_inc(S["on_scaled"], 1)
                    o = o.rearrange("p h (b s) -> p h b s", s=NS)
                    z = pj[:, ZT:ZT + H, SO:CW].rearrange("p h (b c) -> p h b c", c=WQ - 1 + NS)[:, :, :, WQ - 1:]
                dve.wait_ge(S["on_scaled"], NORMS * l + u + 1)
                dve.tensor_tensor(o, o, z, ALU.mult).then_inc(S["yb_ready"], 1)
            decay_pairs(0)
            weights(0)
            for n in range(NCH):
                tok, m, levels = chunk(n)
                q = NCH * l + n
                col = lambda i, hh, rows=m: SM[0:rows, i, n * H + hh:n * H + hh + 1]
                uu = w4(5)[0:m, :, 0:m]
                mb = lambda ap: ap.unsqueeze(1).broadcast_to([m, H, m])
                mb2 = lambda ap: ap.unsqueeze(1).broadcast_to([m, 2, m])

                def um_level(v):
                    dve.tensor_tensor(w4(7 + v % 2)[0:m, :, 0:m], uu, mb(lvl(v, m)), ALU.mult).then_inc(S["um_ready"], 1)
                um_level(0)
                for v in range(levels):
                    z = sum(chunk(i)[2] for i in range(n)) + v + len(LVL_ALL) * l
                    dve.wait_ge(S["um_ready"], z + 1)
                    if v + 1 < levels:
                        um_level(v + 1)
                    for g in range(2):
                        if v == 0:
                            then(dve.tensor_tensor(tg(g)[0:m, 1, :, 0:m], mb2(ident[0:m, 0:m]), w4(7)[0:m, 2 * g:2 * g + 2, 0:m], ALU.subtract))
                            dve.wait_ge(S["p_pe"], 2 * z + g + 1)
                            p = PB[BANK_P[g]][0:m, 0:2 * P].rearrange("p (h c) -> p h c", h=2)[:, :, 0:m]
                            dve.tensor_tensor(tg(g)[0:m, 0, :, 0:m], mb2(ident[0:m, 0:m]), p, ALU.subtract).then_inc(S["t_done"], 1)
                            continue
                        a = slice(0, 2) if v < levels - 1 else slice(1, 2)
                        dve.wait_ge(S["t_pe"], 2 * (z - q) + g - 1)
                        dve.wait_ge(S["t_done"], 2 * z + g - 1)
                        t = tg(g)[0:m, a, :, 0:m]
                        dve.tensor_tensor(t, t, pair(PB[BANK_T[g]])[0:m, a, :, 0:m], ALU.subtract).then_inc(S["t_done"], 1)
                dve.wait_ge(S["t_done"], 2 * (z + 1))
                src = b4(1, m)
                if n < 4:
                    dve.wait_ge(S["ks_pe"], q + 1)
                else:
                    norm_apply_part(0)
                    norm_apply_part(1)
                    dve.wait_ge(S["ks_tr"], l + 1)
                    src = b4(5, m)
                for hh in range(H):
                    ins = dve.scalar_tensor_tensor(w4(12)[0:m, hh, :], src[:, hh, :], col(15, hh), w4(1)[0:m, hh, :], ALU.mult, ALU.add)
                ins.then_inc(S["r_ready"], 1)
                if n < 4:
                    decay_pairs(n + 1)
                    dve.wait_ge(S["st_pe"], 4 * l + n + 1)
                    for hh in range(H):
                        dve.scalar_tensor_tensor(SPR[:, hh, :], SPR[:, hh, :], col(9, hh, P), b4(4)[:, hh, :], ALU.mult, ALU.add).then_inc(S["st_done"], 1)
                    dve.wait_ge(S["st_done"], H * (4 * l + n + 1))
                    weights(n + 1)
                else:
                    norm_apply_part(2)
                    norm_apply_part(3)
                    for b in range(NB):
                        if b == 6:
                            norm_apply_part(4)
                        if b >= 2:
                            dve.wait_ge(S["sm_pe"], NB * l + b - 1)
                        dve.tensor_scalar(w4(7 + b % 2)[0:TS], w4(0)[0:TS], bm[:, b:b + 1], None, ALU.mult).then_inc(S["sm_mask"], 1)
                        if b > 0:
                            sample_state(dve, l, b - 1, b4)
                    sample_state(dve, l, NB - 1, b4)

        def sample_state(dve, l, b, b4):
            dve.wait_ge(S["sm_pe"], NB * l + b + 1)
            for hh in range(H):
                dve.scalar_tensor_tensor(SS[:, b, hh, :], SS[:, b, hh, :], ELS[:, b, hh:hh + 1], b4(6 + b % 2)[:, hh, :], ALU.mult, ALU.add).then_inc(S["sm_upd"], 1)

        def ffn_dve(dve, l, residual_at):
            t0, q = TILE["ffn", l], 2 * l + 1
            def low(hv, i):
                s, w = i % RING3, WK if i % G3 < 2 * FE else SLOT
                dve.wait_ge(S["wh_ready"], hv * G3 + (i + 1))
                dve.tensor_tensor(VL[:, s, 0:w], raw3(s, w), f32(VH[:, s, 0:w]), ALU.subtract).then_inc(S["wl_ready"], 1)

            def act_low(hv, pair):
                dve.wait_ge(S["ah_ready"], hv * FE + (pair + 1))
                dve.tensor_tensor(AL[:, pair, :], AF[:, pair % 2, :], f32(AH[:, pair, :]), ALU.subtract).then_inc(S["al_ready"], 1)
            for i in range(AHEAD):
                low(0, i)
            for k in range(KD):
                dve.wait_ge(S["hh_ready"], k + 1)
                dve.tensor_tensor(HL[:, k, :], hT[:, k, :], f32(HH[:, k, :]), ALU.subtract).then_inc(S["hl_ready"], 1)
            with dve.Fori(0, 2) as hv:
                for i in range(G3):
                    low(hv, i + AHEAD)
                    pair, t = i // 2, t0 + i
                    if i < 2 * FE and i % 2 == 1:
                        dve.wait_ge(S["w3_used"], hv * G3 + (i + 1))
                        for fr in (free_m[0], free_s[0]):
                            dve.wait_ge(fr, hv * (G3 // 2) + (t // 2 + 1))
                        dve.tensor_tensor(AF[:, pair % 2, 0:HN], SQ[:, pair % 2, 0:HN], PM[1][:, 0:HN], ALU.mult).then_inc(free_m[1], 1)
                        dve.tensor_tensor(AF[:, pair % 2, HN:T], SQ[:, pair % 2, HN:T], PS[1][:, 0:HN], ALU.mult).then_inc(free_s[1], 1)
                        dve.wait_ge(free_m[1], hv * (G3 // 2) + (t // 2 + 1))
                        dve.wait_ge(free_s[1], hv * (G3 // 2) + (t // 2 + 1))
                        dve.sem_inc(S["af_ready"], 1)
                    elif 2 <= i <= 2 * FE:
                        act_low(hv, pair - 1)
                    if i >= 2 * FE:
                        m = i - 2 * FE
                        dve.wait_ge(S["w3_used"], hv * G3 + (i + 1))
                        dve.wait_ge(S["x_ready"], hv * (2 * KD) + X_DONE[q])
                        xm, tmp = residual_at(l, i % 2, m, 5 * KD)
                        dve.wait_ge(free_m[i % 2], hv * (G3 // 2) + (t // 2 + 1))
                        dve.wait_ge(free_s[i % 2], hv * (G3 // 2) + (t // 2 + 1))
                        dve.tensor_tensor(xm[:, TP:T], xm[:, TP:T], tmp, ALU.add).then_inc(S["x_ready"], 2)

        def moe_dve(dve, l, then):
            q = 2 * l + 1
            dve.wait_ge(S["cnt_pe"], 1)
            pf = PF[:].rearrange("p a n e -> p a (n e)")
            mk = MK[:].rearrange("p n e -> p (n e)")
            for a in range(2):
                then(dve.tensor_tensor(pf[:, a], PB[5][:, a * NCH * NE:(a + 1) * NCH * NE], mk, ALU.mult))
            then(dve.tensor_reduce(OV[:, 0:1], PB[5][:, 80:88], AX_X, ALU.max))
            then(dve.tensor_scalar(OV[:, 1:2], OV[:, 0:1], float(CAP), None, ALU.is_gt))
            then(dve.tensor_scalar(OV[:, 2:3], OV[:, 1:2], -1.0, 1.0, ALU.mult, ALU.add))
            dve.tensor_scalar(NR[:], OV[0:1, 1:2], float(ROUNDS - 1), 1.0, ALU.mult, ALU.add).then_inc(S["nr_ready"], 1)
            then(dve.memset(PG[:], 0.0))
            then(dve.tensor_scalar(pf[:, 1], pf[:, 1], OV[:, 1:2], None, ALU.mult))
            for rd in range(ROUNDS):
                n = slice(2 * rd, min(2 * rd + 2, NCH))
                then(dve.tensor_copy(PG[:, n, 0, rd * NE:(rd + 1) * NE], PF[:, 1, n]))
                then(dve.tensor_copy(PG[:, :, 1, rd * NE:(rd + 1) * NE], GG[:, 1]))
            dve.scalar_tensor_tensor(PG[:, :, 0, 0:NE], PF[:, 0], OV[:, 2:3], PG[:, :, 0, 0:NE], ALU.mult, ALU.add).then_inc(S["pg_ready"], 1)
            dve.wait_ge(S["pg_ready"], 1)
            dve.wait_ge(S["gt_pe"], 1)
            w = 2 * (NPASS + 1)
            then(dve.tensor_copy(ROWS[:, 0:TP], PB[6][0:w, :]))
            dve.tensor_copy(ROWS[:, TP:T], PB[7][0:w, 0:TS]).then_inc(S["gt_copied"], 1)
            rounds = dve.value_load(NR[0:1, 0:1], min_val=1, max_val=ROUNDS)

            def select(p):
                for n in range(NCH):
                    col = PG[:, n, 0, bass.ds(p, 1)]
                    ins = dve.tensor_scalar(TOK_SLOT[:, n, :], CO[:, C_SLOT:C_SLOT + CAP], col, None, ALU.is_equal)
                ins.then_inc(S["s_ready"], 1)

            def low(p, i):
                s = (B_MOE + i) % RING3
                dve.wait_ge(S["wh_ready"], p * GX + (B_MOE + i + 1))
                dve.tensor_tensor(UL[:, s, :], raw3(s, WK), f32(UH[:, s, :]), ALU.subtract).then_inc(S["wl_ready"], 1)

            def act_low(p, pair):
                dve.wait_ge(S["bh_ready"], p * FE + (pair + 1))
                dve.tensor_tensor(BL[:, pair, :], AF[:, pair % 2, 0:CAP], f32(BH[:, pair, :]), ALU.subtract).then_inc(S["bl_ready"], 1)

            def gather_low(p1):
                for k in range(KD):
                    dve.wait_ge(S["gat_pe"], p1 * (2 * KD) + (2 * k + 2))
                    dve.tensor_copy(XLow[:, k, :], PB[2 + k % 2][:, 0:CAP]).then_inc(fb[2 + k % 2], 1)
            select(0)
            for i in range(AHEAD):
                s = (B_MOE + i) % RING3
                dve.wait_ge(S["wh_ready"], B_MOE + i + 1)
                dve.tensor_tensor(UL[:, s, :], raw3(s, WK), f32(UH[:, s, :]), ALU.subtract).then_inc(S["wl_ready"], 1)
            gather_low(0)
            with dve.Fori(0, rounds) as rd:
                with dve.Fori(0, NE) as e:
                    p = dve.snap(rd * NE + e)
                    for i in range(GX):
                        low(p, i + AHEAD)
                        pair = i // 2
                        if i == 2:
                            dve.wait_ge(S["br_landed"], p * 16 + 16)
                            for j in range(2):
                                ins = dve.tensor_scalar(SLOT_TOK[:, j, :], BR[:, 0, :], CO[:, C_SLOT + CAP + j:C_SLOT + CAP + j + 1], None, ALU.is_equal)
                                ins.then_inc(S["st_own"], 1)
                            dve.wait_ge(S["st_own"], p * 2 + 2)
                        if i in (4, 6):
                            j = i // 2 - 2
                            ins = dve.tensor_tensor_reduce(JUNK, f32(SLOT_TOK[:, j, :]), BR[:, 1, :], 1.0, 0.0, ALU.mult, ALU.add, GS[:, j:j + 1])
                            if j == 1:
                                ins.then_inc(S["st_ready"], 1)
                        if i == 8:
                            select(p + 1)
                        if i < 2 * FE and i % 2 == 1:
                            dve.wait_ge(S["w3_used"], p * GX + (B_MOE + i + 1))
                            b, u = USE["gu", i - 1]
                            dve.wait_ge(fb[b], p * USES[b] + (FIRST[b] + u + 1))
                            dve.tensor_tensor(AF[:, pair % 2, 0:CAP], SQ[:, pair % 2, 0:CAP], PB[i % 4][:, 0:CAP], ALU.mult).then_inc(fb[i % 4], 1)
                            b, u = USE["gu", i]
                            dve.wait_ge(fb[b], p * USES[b] + (FIRST[b] + u + 1))
                            dve.sem_inc(S["bf_ready"], 1)
                        elif 2 <= i <= 2 * FE:
                            act_low(p, pair - 1)
                    for j in range(2):
                        for c in range(2):
                            dve.wait_ge(S["yh_ready"], p * 4 + (2 * j + c + 1))
                            cols = slice(c * 512, (c + 1) * 512)
                            dve.scalar_tensor_tensor(YL[:, j, cols], PB[4 + 2 * j + c][:, :], GS[:, j:j + 1], f32(YH[:, j, cols]), ALU.mult,
                                                     ALU.subtract).then_inc(S["yl_ready"], 1)
                    gather_low(p + 1)
                    for m in range(KD):
                        dve.wait_ge(S["sc_pe"], p * KD + (m + 1))
                        dve.wait_ge(S["x_ready"], p * (2 * KD) + X_DONE[q])
                        xm, gm = xT[:, m, :], MOD[:, l, 5 * KD + m, :]
                        (ba, ua), (bb, ub) = USE["sa", m], USE["sb", m]
                        dve.scalar_tensor_tensor(xm[:, 0:HN], PB[ba][:, 0:HN], gm[:, 0:1], xm[:, 0:HN], ALU.mult, ALU.add).then_inc(fb[ba], 1)
                        dve.scalar_tensor_tensor(xm[:, HN:TP], PB[bb][:, 0:HP], gm[:, 0:1], xm[:, HN:TP], ALU.mult, ALU.add)
                        tmp = TMP[:, m % 2, :]
                        dve.tensor_tensor(pv_s(tmp), pv_s(PB[bb][:, HP:HN]), gm[:, 1:G9].unsqueeze(2).broadcast_to([P, NB, NS]), ALU.mult).then_inc(fb[bb], 1)
                        dve.wait_ge(fb[ba], p * USES[ba] + (FIRST[ba] + ua + 1))
                        dve.wait_ge(fb[bb], p * USES[bb] + (FIRST[bb] + ub + 1))
                        dve.tensor_tensor(xm[:, TP:T], xm[:, TP:T], tmp, ALU.add).then_inc(S["x_ready"], 2)
            dve.wait_ge(S["x_ready"], rounds * (2 * KD * NE) + X_DONE[q])
            dve.wait_ge(S["br_landed"], rounds * (16 * NE) + 16)
            dve.sem_inc(S["moe_done"], 1)

        def router_dve(dve, l, then):
            dve.wait_ge(S["out_states"], 16 * 7 * (l + 1))
            for v in (HTH, HTL):
                then(dve.memset(f32(v[TS:P, NCH - 1, :]), 0.0))

            def input_low(n):
                m = min((n + 1) * P, T) - n * P
                for c in range(2):
                    dve.wait_ge(S["hth_ready"], 2 * n + c + 1)
                    dve.tensor_tensor(HTL[0:m, n, c * 512:(c + 1) * 512], PB[2 * (n % 2) + c][0:m, :], f32(HTH[0:m, n, c * 512:(c + 1) * 512]),
                                      ALU.subtract).then_inc(S["htl_ready"], 1)
            input_low(0)
            input_low(1)
            dve.wait_ge(S["lg_pe"], 1)
            then(dve.tensor_copy(LG[:, 0:4, :], PB[4][:, 0:4 * NE].rearrange("p (n e) -> p n e", e=NE)))
            then(dve.tensor_copy(LG[0:TS, 4, :], PB[4][0:TS, 4 * NE:5 * NE]))
            for n in range(NCH):
                ins = dve.max(MX[:, n, :], LG[:, n, :])
            then(ins)
            for n in range(NCH):
                ins = dve.max_index(IX[:, n, :], MX[:, n, :], LG[:, n, :])
            then(ins)
            then(dve.tensor_copy(IXF[:], IX[:, :, 0:2]))
            dve.tensor_tensor(G12[:, 0, :], MX[:, :, 1], MX[:, :, 0], ALU.subtract).then_inc(S["lg_exp"], 1)
            dve.wait_ge(S["gate_exp"], 1)
            then(dve.tensor_scalar(G12[:, 2, :], G12[:, 1, :], 1.0, None, ALU.add))
            then(dve.reciprocal(G12[:, 2, :], G12[:, 2, :]))
            then(dve.tensor_tensor(G12[:, 3, :], G12[:, 1, :], G12[:, 2, :], ALU.mult))
            for n in range(NCH):
                dve.tensor_scalar(GG[:, 0, n, :], iota, IXF[:, n, 0:1], G12[:, 2, n:n + 1], ALU.is_equal, ALU.mult)
                dve.tensor_scalar(GG[:, 1, n, :], iota, IXF[:, n, 1:2], G12[:, 3, n:n + 1], ALU.is_equal, ALU.mult)
            for n in range(NCH):
                ins = dve.tensor_scalar(MK[:, n, :], iota, IXF[:, n, 0:1], None, ALU.is_equal)
            then(ins)
            for n in range(NCH):
                ins = dve.scalar_tensor_tensor(MK[:, n, :], iota, IXF[:, n, 1:2], MK[:, n, :], ALU.is_equal, ALU.add)
            then(ins)
            then(dve.memset(MK[TS:P, 4, :], 0.0))
            dve.tensor_tensor(GG[:, 1], GG[:, 0], GG[:, 1], ALU.add).then_inc(S["mk_ready"], 1)
            for n in range(2, NCH):
                input_low(n)
            dve.wait_ge(S["mk_ready"], 1)

        @block.vector
        def _(dve):
            own = [0]

            def then(ins):
                own[0] += 1
                ins.then_inc(S["dve_own"], 1)
                dve.wait_ge(S["dve_own"], own[0])

            def log1p_steps(dst, y, s, s2, add):
                then(dve.tensor_scalar(s, y, 2.0, None, ALU.add))
                then(dve.reciprocal(s, s))
                then(dve.tensor_tensor(s, s, y, ALU.mult))
                then(dve.tensor_tensor(s2, s, s, ALU.mult))
                then(dve.tensor_scalar(dst, s2, LOG1P[0], None, ALU.mult))
                for c in LOG1P[1:]:
                    then(dve.scalar_tensor_tensor(dst, dst, c, s2, ALU.add, ALU.mult))
                then(dve.scalar_tensor_tensor(dst, dst, 1.0, s, ALU.add, ALU.mult))
                then(dve.scalar_tensor_tensor(dst, dst, 2.0, add, ALU.mult, ALU.add))

            def modulation(b):
                dve.wait_ge(S["mod_pe"], ADA_BATCH[b + 1])
                for l in range(L):
                    lo, hi = max(ADA_BATCH[b], l * M_ADA), min(ADA_BATCH[b + 1], (l + 1) * M_ADA)
                    if lo < hi:
                        w = hi - lo
                        tiles = PB[4][:, (lo - ADA_BATCH[b]) * G9:(hi - ADA_BATCH[b]) * G9].rearrange("p (m g) -> p m g", g=G9)
                        lo -= l * M_ADA
                        then(dve.tensor_tensor(MOD[:, l, lo:lo + w], tiles, par("b_ada", l, lo, w).unsqueeze(2).broadcast_to([P, w, G9]), ALU.add))
                for q in [q for q in range(2 * L) if MOD_BATCH[q] == b + 1]:
                    l, w = q // 2, q % 2
                    then(dve.scalar_tensor_tensor(AM[:, q], MOD[:, l, KD * (3 * w + 1):KD * (3 * w + 2), :], 1.0,
                                                  par(f"norm{w + 1}", l, 0, KD).unsqueeze(2).broadcast_to([P, KD, G9]), ALU.add, ALU.mult))
                dve.sem_inc(S["mod_done"], 1)

            def norm_apply(q):
                dve.wait_ge(S["rs_sqrt"], 2 * (q + 1))
                then(dve.reciprocal(RS[:], RS[:]))
                if q == 2 * L:
                    for k in range(KD):
                        dve.scalar_tensor_tensor(hT[:, k, :], xT[:, k, :], FN[:, k:k + 1], RS[:], ALU.mult, ALU.mult).then_inc(S["y_ready"], 1)
                    return
                l, w = q // 2, q % 2
                for k in range(KD):
                    dve.tensor_tensor(hT[:, k, :], xT[:, k, :], RS[:], ALU.mult).then_inc(S["h_mul"], 1)
                dve.wait_ge(S["h_mul"], KD * (q + 1))
                if q == 0:
                    modulation(0)
                hs = hT[:, :, TP:T].rearrange("p k (b s) -> p k b s", s=NS)
                bc = lambda ap: ap.unsqueeze(3).broadcast_to([P, KD, NB, NS])
                then(dve.tensor_tensor(hs, hs, bc(AM[:, q, :, 1:G9]), ALU.mult))
                dve.tensor_tensor(hs, hs, bc(MOD[:, l, 3 * KD * w:3 * KD * w + KD, 1:G9]), ALU.add).then_inc(S["h_small"], 1)

            def residual_at(l, b, m, g0):
                xm = xT[:, m, :] if isinstance(m, int) else xT[:, bass.ds(m, 1), :].rearrange("p a t -> p (a t)")
                gm = MOD[:, l, bass.ds(m + g0, 1), :].rearrange("p a t -> p (a t)")
                dve.scalar_tensor_tensor(xm[:, 0:HN], PM[b][:, 0:HN], gm[:, 0:1], xm[:, 0:HN], ALU.mult, ALU.add).then_inc(free_m[b], 1)
                dve.scalar_tensor_tensor(xm[:, HN:TP], PS[b][:, 0:HP], gm[:, 0:1], xm[:, HN:TP], ALU.mult, ALU.add)
                tmp = TMP[:, b, :]
                dve.tensor_tensor(pv_s(tmp), pv_s(PS[b][:, HP:HN]), gm[:, 1:G9].unsqueeze(2).broadcast_to([P, NB, NS]), ALU.mult).then_inc(free_s[b], 1)
                return xm, tmp

            dve.memset(ONES[:], 1.0).then_inc(S["ones_ready"], 1)
            dve.memset(SM[:], 0.0).then_inc(S["ones_ready"], 1)
            then(dve.memset(ABt[:], 0.0))
            then(dve.memset(EPSC[:, 0:1], EPS))
            then(dve.memset(EPSC[:, 1:2], EPS * EPS * P))
            then(dve.memset(LG[:], 0.0))
            dve.wait_ge(S["consts"], 8 * 16)
            o = PC["lru_lambda"][0]
            lam = PA[:, :, o:o + 2]
            dve.scalar_tensor_tensor(LM[:, :, 0, :], lam, -1.0, lam, ALU.mult, ALU.min).then_inc(S["lam_abs"], 1)
            then(dve.tensor_scalar(LM[:, :, 2, :], lam, -1.0, 0.0, ALU.mult, ALU.max))
            dve.wait_ge(S["sp_exp"], 1)
            log1p_steps(LM[:, :, 5, :], LM[:, :, 1, :], LM[:, :, 3, :], LM[:, :, 4, :], LM[:, :, 2, :])
            then(dve.tensor_scalar(LM[:, :, 5, :], LM[:, :, 5, :], 2.0, None, ALU.mult))
            for a, nm in enumerate(("lru_b_a", "lru_b_i")):
                o = PC[nm][0]
                then(dve.tensor_scalar(LM[:, :, 6 + a, :], PA[:, :, o:o + 2], 0.5, None, ALU.mult))
            for l in range(L):
                norm_apply(2 * l)
                mixer_dve(dve, l, then, log1p_steps, modulation)
                f0 = FILL["out", l]
                with dve.Fori(0, 2) as j:
                    for s in range(4):
                        m = j * 4 + s
                        dve.wait_ge(S["w_used"], j * 4 + (f0 + s + 1))
                        xm, tmp = residual_at(l, s % 2, m, 2 * KD)
                        dve.wait_ge(free_m[s % 2], j * 2 + (TILE["out", l] + s) // 2 + 1)
                        dve.wait_ge(free_s[s % 2], j * 2 + (TILE["out", l] + s) // 2 + 1)
                        dve.tensor_tensor(xm[:, TP:T], xm[:, TP:T], tmp, ALU.add).then_inc(S["x_ready"], 2)
                norm_apply(2 * l + 1)
                if l % 2 == 0:
                    ffn_dve(dve, l, residual_at)
                else:
                    router_dve(dve, l, then)
                    moe_dve(dve, l, then)
            norm_apply(2 * L)

        @block.gpsimd
        def _(pool):
            own = [0]

            def then(ins):
                own[0] += 1
                ins.then_inc(S["pool_own"], 1)
                pool.wait_ge(S["pool_own"], own[0])
            for l in range(L):
                if l > 0:
                    pool.wait_ge(S["out_states"], 16 * 7 * l)
                    pool.wait_ge(S["x_ready"], X_DONE[2 * l])
                for dst, nm in ((SC[:], "st_a"), (SCQ[:], "st_q"), (ST[:], "st_l")):
                    pool.dma_start(dst, io[nm][l]).then_inc(S["states_in"], 16)
                for h2 in range(2):
                    pool.dma_start(SS[:, 4 * h2:4 * h2 + 4], io["st_d"][l, :, 4 * h2:4 * h2 + 4]).then_inc(S["states_in"], 16)
                then(pool.memset(WL[:], 0.0))
                for a, nm in enumerate(("lru_w_a", "lru_w_i")):
                    for b in range(4):
                        o = 64 * (b % 2)
                        pool.dma_start(WL[o:o + 64, a, b // 2, o:o + 64], io[nm][l, b]).then_inc(S["in_small"], 16)
                pool.wait_ge(S["states_in"], 16 * 5 * (l + 1))
                pads = pj[:, :, SO:CW].rearrange("p m (b c) -> p m b c", c=WQ - 1 + NS)[:, :, :, 0:WQ - 1]
                then(pool.memset(pj[:, :, 0:WQ - 1], 0.0))
                then(pool.memset(pads, 0.0))
                then(pool.tensor_copy(pads[:, LRU_X:LRU_X + 2], SCQ[:, 0:2]))
                then(pool.tensor_copy(pads[:, QKV:ZT], SCQ[:, 2:14]))
                for c in range(2):
                    then(pool.memset(UA[:, c, 0:WA - 1], 0.0))
                    then(pool.tensor_copy(UA[:, c, AO:CA].rearrange("p (b c) -> p b c", c=WA - 1 + NS)[:, :, 0:WA - 1], SC[:, c]))
                pool.sem_inc(S["pads_ready"], 1)
                pool.wait_ge(S["glu_ready"], 4 * (l + 1))
                for c in range(2):
                    then(pool.tensor_copy(NA[:, c], UA[:, c, AO:CA].rearrange("p (b c) -> p b c", c=WA - 1 + NS)[:, :, NS:]))
                pool.dma_start(io["n_a"][l], NA[:]).then_inc(S["out_states"], 16)
                pool.dma_start(io["n_ap"][l], UA[:, :, TP:AO]).then_inc(S["out_states"], 16)
                for i in range(14):
                    m = LRU_X + i if i < 2 else QKV + i - 2
                    pool.wait_ge(free_m[m % 2], (TILE["in", l] + m) // 2 + 1)
                    pool.wait_ge(free_s[m % 2], (TILE["in", l] + m) // 2 + 1)
                    then(pool.tensor_copy(NQ[:, i, 0, :], pj[:, m, TP:SO]))
                    then(pool.tensor_copy(NQ[:, i, 1:G9, :], pj[:, m, SO:CW].rearrange("p (b c) -> p b c", c=WQ - 1 + NS)[:, :, NS:]))
                pool.sem_inc(S["new_states"], 1)
                pool.dma_start(io["n_q"][l], NQ[:]).then_inc(S["out_states"], 16)
                pool.wait_ge(S["lru_new"], l + 1)
                pool.dma_start(io["n_l"][l], SN[:]).then_inc(S["out_states"], 16)
                def diagonals(n):
                    m = chunk(n)[1]
                    col = lambda i: SM[0:m, i, n * H:(n + 1) * H].unsqueeze(2).broadcast_to([m, H, m])
                    rows = lambda ap: ap[0:m, :].unsqueeze(1).broadcast_to([m, H, m])
                    if n > 0:
                        pool.wait_ge(S["mat_pe"], NCH * l + n)
                    then(pool.tensor_tensor(diag_g[0:m, :, 0:m], rows(tri if n < 4 else btri), col(3), ALU.mult))
                    pool.tensor_tensor(diag_b[0:m, :, 0:m], rows(ident[:, 0:m]), col(14), ALU.mult).then_inc(S["diag_ready"], 1)
                pool.wait_ge(S["rk_ready"], l + 1)
                diagonals(0)
                for n in range(NCH):
                    tok, m, _ = chunk(n)
                    q = NCH * l + n
                    pool.wait_ge(S["eg_ready"], q + 1)
                    if q > 0:
                        pool.wait_ge(S["o_pe"], q)
                    pool.tensor_tensor(w4(2)[:, :, 0:m], QC[:, 0:H, tok], w4(3)[:, :, 0:m], ALU.mult).then_inc(S["qg_ready"], 1)
                    if n < 4:
                        diagonals(n + 1)
                pool.wait_ge(S["st_done"], H * 4 * (l + 1))
                pool.dma_start(io["n_dp"][l], SPR[:]).then_inc(S["out_states"], 16)
                pool.wait_ge(S["sm_upd"], H * NB * (l + 1))
                for h2 in range(2):
                    pool.dma_start(io["n_d"][l, :, 4 * h2:4 * h2 + 4], SS[:, 4 * h2:4 * h2 + 4]).then_inc(S["out_states"], 16)
            pool.wait_ge(S["gt_copied"], 1)
            pool.dma_start(scratch, ROWS).then_inc(S["rows_out"], 16)
            pool.wait_ge(S["rows_out"], 16)
            rows = scratch.rearrange("(a p) t -> p a t", a=2)
            pool.dma_start(BR[:, :, :], rows[0:1].broadcast_to([P, 2, T])).then_inc(S["br_landed"], 16)
            rounds = pool.value_load(NR[0:1, 0:1], min_val=1, max_val=ROUNDS)
            with pool.Fori(0, rounds) as rd:
                with pool.Fori(0, NE) as e:
                    p = pool.snap(rd * NE + e)
                    pool.wait_ge(S["st_ready"], p + 1)
                    pool.dma_start(BR[:, :, :], rows[bass.ds(p + 1, 1)].broadcast_to([P, 2, T])).then_inc(S["br_landed"], 16)
            pool.wait_ge(S["out_states"], 16 * 7 * L)
            pool.wait_ge(S["br_landed"], rounds * (16 * NE) + 16)


def _constants(np):
    c = np.zeros((P, C_END), np.float32)
    i = np.arange(P)
    c[:, C_ID:C_ID + P] = np.eye(P)
    c[:, C_TRI:C_TRI + P] = i[:, None] <= i[None, :]
    t = np.arange(TS)
    same = (t[:, None] // NS) == (t[None, :] // NS)
    c[:TS, C_BTRI:C_BTRI + TS] = same & (t[:, None] <= t[None, :])
    c[:TS, C_BONE:C_BONE + TS] = same
    c[:TS, C_BM:C_BM + NB] = (t[:, None] // NS) == np.arange(NB)[None, :]
    c[:, C_IOTA:C_IOTA + NE] = np.arange(NE)
    for v in range(LEVELS):
        blk = i // (1 << v)
        c[:, C_LVL + v * P:C_LVL + (v + 1) * P] = (blk[:, None] % 2 == 0) & (blk[None, :] == blk[:, None] + 1)
    c[:, C_SLOT:C_SLOT + CAP] = np.arange(1, CAP + 1)
    c[:, C_SLOT + CAP:] = np.stack([i + 1, i + 1 + P], 1)
    return c


def _tiles(np, w):
    *b, i, o = w.shape
    w = w.reshape(*b, i // P, P, o // P, P)
    n = len(b)
    return np.ascontiguousarray(np.moveaxis(w, (n + 2, n + 1, n), (n, n + 1, n + 2)))


def _layout(np, a):
    x = np.concatenate([a["x_prompt"][0], a["x_sample"].reshape(TS, D)], 0)
    feat = lambda v: np.moveaxis(v.reshape(*v.shape[:-1], -1, P), -1, 0)
    w_in = a["w_in"]
    parts = np.split(w_in, np.cumsum([256, 256, 1536, 512, H, H, 256]).tolist(), axis=-1)
    a_val, a_gate, qkv, z, b, aa, lx, lg = parts
    w24 = np.concatenate([a_val, a_gate, lx, lg, qkv, z], -1)
    wab = np.concatenate([b, aa], -1).reshape(L, KD, P, 2 * H).transpose(2, 0, 1, 3)
    params = np.zeros((P, L, PCOLS), np.float32)
    def put(name, v):
        o, w = PC[name]
        params[:, :, o:o + w] = v
    for name in ("b_ada", "norm1", "norm2", "conv_a_b", "ln_a_g", "ln_a_b", "conv_lru_b", "lru_b_a", "lru_b_i", "lru_lambda", "lru_norm", "gdn_norm"):
        put(name, feat(a[name]))
    for name in ("conv_a_w", "conv_qkv_w", "conv_lru_w"):
        put(name, feat(a[name]).transpose(0, 1, 3, 2).reshape(P, L, -1))
    put("a_log", np.broadcast_to(a["gdn_a_log"], (P, L, H)))
    put("dt_bias", np.broadcast_to(a["gdn_dt_bias"], (P, L, H)))
    gu = lambda g, u: np.stack([_tiles(np, g), _tiles(np, u)], -4)
    q = feat(np.concatenate([a["state_conv_lru"], a["state_conv_qkv"]], -1))
    dn = _tiles(np, a["ffn_wd"][0]).reshape(KD, P, 2, FE * P).transpose(2, 0, 1, 3)
    out = {
        "consts": _constants(np), "params": params,
        "cT": feat(np.concatenate([a["c_prompt"], a["c_sample"]], 0)).transpose(0, 2, 1),
        "x": feat(x).transpose(0, 2, 1), "wab": wab, "fnorm": feat(a["final_norm"]),
        "rw": a["router_w"][0].reshape(KD, P, NE).transpose(1, 0, 2), "rb": a["router_b"],
        "w_ada": _tiles(np, a["w_ada"]).reshape(L * M_ADA, P, KD * P), "w_in": _tiles(np, w24).reshape(L, M_IN, P, KD * P),
        "w_out": _tiles(np, a["w_out"]).reshape(L, KD, P, KD * P),
        "ffn_gu": gu(a["ffn_wg"][0], a["ffn_wu"][0]).reshape(2 * FF, P, KD * P), "ffn_dn": dn,
        "moe_gu": gu(a["moe_wg"][0], a["moe_wu"][0]).reshape(NE, 2 * FE, P, KD * P),
        "moe_dn": a["moe_wd"][0].reshape(NE, FE, P, D),
        "lru_w_a": a["lru_w_a"], "lru_w_i": a["lru_w_i"],
        "st_a": feat(a["state_conv_a"]).transpose(1, 0, 4, 2, 3), "st_q": q.transpose(1, 0, 4, 2, 3),
        "st_l": feat(a["state_lru"]).transpose(1, 0, 3, 2).reshape(L, P, 2 * NB),
        "st_d": a["state_delta"].transpose(0, 3, 1, 2, 4),
    }
    return {k: np.ascontiguousarray(v) for k, v in out.items()}


_OUT = {"y": (P, KD, T), "n_a": (L, P, 2, NB, WA - 1), "n_ap": (L, P, 2, WA - 1), "n_q": (L, P, 14, G9, WQ - 1),
        "n_l": (L, P, 2 * G9), "n_dp": (L, P, H, P), "n_d": (L, P, NB, H, P)}


def kernel(**inputs):
    import numpy as np
    from concourse import bacc
    from concourse.bass_utils import run_bass_kernel_spmd

    arrays = _layout(np, {k: np.asarray(v) for k, v in inputs.items()})
    nc = bacc.Bacc("TRN2", target_bir_lowering=False, num_devices=1)
    io = {k: nc.dram_tensor("in_" + k, v.shape, F32, kind="ExternalInput").ap() for k, v in arrays.items()}
    io.update({k: nc.dram_tensor("out_" + k, s, F32, kind="ExternalOutput").ap() for k, s in _OUT.items()})
    build(nc, io)
    r = run_bass_kernel_spmd(nc, [{"in_" + k: v for k, v in arrays.items()}], core_ids=[0]).results[0]
    o = {k: np.asarray(r["out_" + k]).reshape(s) for k, s in _OUT.items()}
    y = o["y"].transpose(2, 1, 0).reshape(T, D)
    unfeat = lambda v: v.reshape(*v.shape[:-2], -1)
    a_s = unfeat(o["n_a"].transpose(0, 3, 4, 2, 1))
    a_p = unfeat(o["n_ap"].transpose(0, 3, 2, 1))[:, None]
    q = unfeat(o["n_q"].transpose(0, 3, 4, 2, 1))
    lr = unfeat(o["n_l"].reshape(L, P, 2, G9).transpose(0, 3, 2, 1))
    c = np.ascontiguousarray
    return tuple(c(v) for v in (
        y[None, :TP], y[TP:].reshape(NB, NS, D), a_p, q[:, 0:1, :, 256:], o["n_dp"].transpose(0, 2, 1, 3)[:, None],
        q[:, 0:1, :, :256], lr[:, 0:1], a_s, q[:, 1:, :, 256:], o["n_d"].transpose(0, 2, 3, 1, 4), q[:, 1:, :, :256], lr[:, 1:]))
```
